# Optimizing a Trainium2 kernel written in Bass

```python
import math
import jax
import jax.numpy as jnp
from jax import lax
import numpy as np

D_MODEL = 1024
BATCH = 1
SEQ = 512
DEPTH = 2

N_META = 16
CHUNK = 128
EPS = 1e-6

SSD_HEADS = 16
SSD_HEAD_DIM = 64
SSD_INNER = SSD_HEADS * SSD_HEAD_DIM
SSD_GROUPS = 4
SSD_STATE = 128
SSD_CONV = 4
SSD_XBC = SSD_INNER + 2 * SSD_GROUPS * SSD_STATE

RET_HEADS = 4
RET_QK_DIM = 256
RET_V_DIM = 256
RET_QK_WIDTH = RET_HEADS * RET_QK_DIM
RET_WIDTH = RET_HEADS * RET_V_DIM

SB_HEADS = 16
SB_HEAD_DIM = 64
SB_WIDTH = SB_HEADS * SB_HEAD_DIM

LRU_WIDTH = 1024
LRU_BLOCKS = 8
LRU_BLOCK = LRU_WIDTH // LRU_BLOCKS
LRU_CONV = 4
LRU_C = 8.0

FFN_DIM = 2816
FFN_CONV = 3

MIX0_IN = SSD_INNER + SSD_XBC + SSD_HEADS + 2 * RET_QK_WIDTH + 2 * RET_WIDTH
MIX0_OUT = SSD_INNER + RET_WIDTH
MIX1_IN = 3 * SB_WIDTH + 2 * LRU_WIDTH
MIX1_OUT = SB_WIDTH + LRU_WIDTH

kernel_name = 'hybrid_ssd_retention_stickbreak_rglru_block'

def rmsnorm(x, g):
    xf = x.astype(jnp.float32)
    y = xf * lax.rsqrt(jnp.mean(xf * xf, -1, keepdims=True) + EPS)
    return (y * g).astype(x.dtype)

def causal_dwconv(x, w, b):
    K, C = w.shape
    y = lax.conv_general_dilated(x, w[:, None, :], window_strides=(1,), padding=[(K - 1, 0)],
                                 dimension_numbers=('NWC', 'WIO', 'NWC'), feature_group_count=C)
    return y + b

def split_cols(u, sizes):
    return jnp.split(u, np.cumsum(sizes)[:-1].tolist(), axis=-1)

def front_pad(t, pad):
    return jnp.pad(t, ((0, 0), (pad, 0)) + ((0, 0),) * (t.ndim - 2))

def segsum(a):
    L = a.shape[-1]
    cs = jnp.cumsum(a, -1)
    seg = cs[..., :, None] - cs[..., None, :]
    return jnp.where(jnp.tril(jnp.ones((L, L), bool)), seg, -jnp.inf)

def ssd_group(z, xbc, dt_raw, conv_w, conv_b, dt_bias, a_log, d_skip, norm_g):
    Bsz, T, _ = xbc.shape
    f32 = jnp.float32
    E = SSD_HEADS // SSD_GROUPS
    xbc = jax.nn.silu(causal_dwconv(xbc, conv_w, conv_b)).astype(f32)
    xs, bm, cm = jnp.split(xbc, [SSD_INNER, SSD_INNER + SSD_GROUPS * SSD_STATE], -1)
    dt = jax.nn.softplus(dt_raw.astype(f32) + dt_bias.astype(f32))
    a = -jnp.exp(a_log.astype(f32))
    pad = (-T) % CHUNK
    P = T + pad
    nc = P // CHUNK
    X = front_pad(xs * jnp.repeat(dt, SSD_HEAD_DIM, -1), pad).reshape(Bsz, nc, CHUNK, SSD_GROUPS, E, SSD_HEAD_DIM)
    Bm = front_pad(bm, pad).reshape(Bsz, nc, CHUNK, SSD_GROUPS, SSD_STATE)
    Cm = front_pad(cm, pad).reshape(Bsz, nc, CHUNK, SSD_GROUPS, SSD_STATE)
    a_dt = front_pad(dt * a, pad).reshape(Bsz, nc, CHUNK, SSD_GROUPS, E).transpose(0, 3, 4, 1, 2)
    a_cs = jnp.cumsum(a_dt, -1)
    cb = jnp.einsum('bclgn,bcsgn->bgcls', Cm, Bm)
    y_diag = jnp.einsum('bgecls,bcsgep->bclgep', cb[:, :, None] * jnp.exp(segsum(a_dt)), X)
    decay_states = jnp.exp(a_cs[..., -1:] - a_cs).transpose(0, 3, 4, 1, 2)
    states = jnp.einsum('bclgn,bclgep->bcgepn', Bm, X * decay_states[..., None])
    chunk_tot = jnp.pad(a_cs[..., -1], ((0, 0), (0, 0), (0, 0), (1, 0)))
    decay_chunk = jnp.exp(segsum(chunk_tot))
    states = jnp.concatenate([jnp.zeros_like(states[:, :1]), states], 1)
    prev = jnp.einsum('bgezc,bcgepn->bzgepn', decay_chunk, states)[:, :-1]
    y_off = jnp.einsum('bclgn,bcgepn->bclgep', Cm, prev) * jnp.exp(a_cs).transpose(0, 3, 4, 1, 2)[..., None]
    y = (y_diag + y_off).reshape(Bsz, P, SSD_INNER)[:, pad:]
    y = y + xs * jnp.repeat(d_skip.astype(f32), SSD_HEAD_DIM)
    y = (y * jax.nn.silu(z.astype(f32))).reshape(Bsz, T, SSD_GROUPS, SSD_INNER // SSD_GROUPS)
    y = y * lax.rsqrt(jnp.mean(y * y, -1, keepdims=True) + EPS)
    return (y.reshape(Bsz, T, SSD_INNER) * norm_g).astype(z.dtype)

def rotate_retnet(x, pos):
    half = x.shape[-1] // 2
    inv_freq = 1.0 / (10000.0 ** (jnp.arange(half, dtype=jnp.float32) / (half - 1)))
    ang = pos[:, None] * inv_freq[None, :]
    cos = jnp.cos(ang)[None, :, None, :]
    sin = jnp.sin(ang)[None, :, None, :]
    x1, x2 = x[..., :half], x[..., half:]
    return jnp.concatenate([x1 * cos - x2 * sin, x1 * sin + x2 * cos], -1)

def retention_group(q, k, v, g, norm_g):
    Bsz, T, _ = q.shape
    f32 = jnp.float32
    pos = jnp.arange(T, dtype=f32)
    q = rotate_retnet(q.astype(f32).reshape(Bsz, T, RET_HEADS, RET_QK_DIM), pos)
    k = rotate_retnet(k.astype(f32).reshape(Bsz, T, RET_HEADS, RET_QK_DIM), pos) * RET_QK_DIM ** -0.5
    v = v.astype(f32).reshape(Bsz, T, RET_HEADS, RET_V_DIM)
    pad = (-T) % CHUNK
    P = T + pad
    nc = P // CHUNK
    q = front_pad(q, pad).reshape(Bsz, nc, CHUNK, RET_HEADS, RET_QK_DIM)
    k = front_pad(k, pad).reshape(Bsz, nc, CHUNK, RET_HEADS, RET_QK_DIM)
    v = front_pad(v, pad).reshape(Bsz, nc, CHUNK, RET_HEADS, RET_V_DIM)
    log_gamma = jnp.log1p(-jnp.exp2(-5.0 - jnp.arange(RET_HEADS, dtype=f32)))
    idx = jnp.arange(CHUNK, dtype=f32)
    diff = idx[:, None] - idx[None, :]
    decay = jnp.where(diff >= 0, jnp.exp(log_gamma[:, None, None] * jnp.maximum(diff, 0.0)), 0.0)
    scores = jnp.einsum('bclhd,bcshd->bhcls', q, k) * decay[None, :, None]
    inner = jnp.einsum('bhcls,bcshe->bclhe', scores, v)
    zeta = jnp.exp(log_gamma[None, :] * (CHUNK - 1 - idx)[:, None])
    kv = jnp.einsum('bclhd,bclhe->bchde', k * zeta[..., None], v)
    chunk_decay = jnp.exp(CHUNK * log_gamma)[None, :, None, None]

    def step(R, kv_c):
        return chunk_decay * R + kv_c, R

    _, R_prev = lax.scan(step, jnp.zeros_like(kv[:, 0]), jnp.moveaxis(kv, 1, 0))
    R_prev = jnp.moveaxis(R_prev, 0, 1)
    xi = jnp.exp(log_gamma[None, :] * (idx + 1.0)[:, None])
    cross = jnp.einsum('bclhd,bchde->bclhe', q, R_prev) * xi[..., None]
    o = (inner + cross).reshape(Bsz, P, RET_HEADS, RET_V_DIM)[:, pad:]
    o = o - jnp.mean(o, -1, keepdims=True)
    o = o * lax.rsqrt(jnp.mean(o * o, -1, keepdims=True) + EPS)
    o = o.reshape(Bsz, T, RET_WIDTH) * norm_g
    return (jax.nn.silu(g.astype(f32)) * o).astype(g.dtype)

def stick_breaking_attention(q, k, v):
    Bsz, T, H, D = q.shape
    f32 = jnp.float32
    scale = D ** -0.5
    bounds = [(0, N_META)] + [(s, min(s + CHUNK, T)) for s in range(N_META, T, CHUNK)]
    outs = []
    for s0, s1 in bounds:
        z = jnp.einsum('bqhd,bkhd->bhqk', q[:, s0:s1].astype(f32), k[:, :s1].astype(f32)) * scale
        strict = jnp.arange(s1)[None, :] < jnp.arange(s0, s1)[:, None]
        log_1m = jnp.where(strict, jax.nn.log_sigmoid(-z), 0.0)
        after = lax.cumsum(log_1m, axis=3, reverse=True) - log_1m
        w = jnp.where(strict, jnp.exp(jax.nn.log_sigmoid(z) + after), 0.0)
        outs.append(jnp.einsum('bhqk,bkhd->bqhd', w, v[:, :s1].astype(f32)))
    return jnp.concatenate(outs, 1)

def rg_lru(x, w_a, b_a, w_x, b_x, lam):
    Bsz, T, W = x.shape
    f32 = jnp.float32
    x = x.astype(f32)
    xb = x.reshape(Bsz, T, LRU_BLOCKS, LRU_BLOCK)
    r = jax.nn.sigmoid(jnp.einsum('btni,nij->btnj', xb, w_a.astype(f32)).reshape(Bsz, T, W) + b_a)
    i = jax.nn.sigmoid(jnp.einsum('btni,nij->btnj', xb, w_x.astype(f32)).reshape(Bsz, T, W) + b_x)
    log_a = -LRU_C * r * jax.nn.softplus(-lam.astype(f32))
    a = jnp.exp(log_a)
    b = jnp.sqrt(jnp.maximum(-jnp.expm1(2.0 * log_a), 0.0)) * (i * x)

    def combine(left, right):
        a_l, b_l = left
        a_r, b_r = right
        return a_l * a_r, a_r * b_l + b_r

    _, hs = lax.associative_scan(combine, (a, b), axis=1)
    return hs

def ssd_retention_mixer(h, w_in, ssd_conv_w, ssd_conv_b, ssd_dt_bias, ssd_a_log, ssd_d, ssd_norm, ret_norm, w_out):
    u = h @ w_in
    z, xbc, dt_raw, q, k, v, g = split_cols(u, (SSD_INNER, SSD_XBC, SSD_HEADS, RET_QK_WIDTH, RET_QK_WIDTH, RET_WIDTH, RET_WIDTH))
    y_ssd = ssd_group(z, xbc, dt_raw, ssd_conv_w, ssd_conv_b, ssd_dt_bias, ssd_a_log, ssd_d, ssd_norm)
    y_ret = retention_group(q, k, v, g, ret_norm)
    return jnp.concatenate([y_ssd, y_ret], -1) @ w_out

def sb_lru_mixer(h, w_in, lru_conv_w, lru_conv_b, lru_wa, lru_ba, lru_wx, lru_bx, lru_lambda, w_out):
    Bsz, T, _ = h.shape
    u = h @ w_in
    q, k, v, gate, xr = split_cols(u, (SB_WIDTH, SB_WIDTH, SB_WIDTH, LRU_WIDTH, LRU_WIDTH))
    shp = (Bsz, T, SB_HEADS, SB_HEAD_DIM)
    y_sb = stick_breaking_attention(q.reshape(shp), k.reshape(shp), v.reshape(shp)).reshape(Bsz, T, SB_WIDTH)
    xr = causal_dwconv(xr, lru_conv_w, lru_conv_b)
    y_lru = rg_lru(xr, lru_wa, lru_ba, lru_wx, lru_bx, lru_lambda) * jax.nn.gelu(gate.astype(jnp.float32))
    return jnp.concatenate([y_sb.astype(h.dtype), y_lru.astype(h.dtype)], -1) @ w_out

def conv_ffn(h, w_in, conv_w, conv_b, w_out):
    u = causal_dwconv(h @ w_in, conv_w, conv_b)
    g, up = jnp.split(u, 2, -1)
    return (jax.nn.silu(g) * up) @ w_out

def setup_inputs(seed: int = 0) -> dict:
    key = jax.random.key(seed)
    ks = iter(jax.random.split(key, 64))
    f32 = jnp.float32

    def nrm(shape, scale):
        return jax.random.normal(next(ks), shape, f32) * scale

    def gain(n):
        return 1.0 + nrm((n,), 0.02)

    dt0 = jnp.exp(jax.random.uniform(next(ks), (SSD_HEADS,), f32, math.log(1e-3), math.log(1e-1)))
    dt_bias = dt0 + jnp.log(-jnp.expm1(-dt0))
    a_log = jnp.log(jax.random.uniform(next(ks), (SSD_HEADS,), f32, 1.0, 16.0))
    a_lru = jax.random.uniform(next(ks), (LRU_WIDTH,), f32, 0.9, 0.999) ** (1.0 / LRU_C)
    lam = jnp.log(a_lru) - jnp.log1p(-a_lru)
    return {
        'x': nrm((BATCH, SEQ, D_MODEL), 1.0),
        'meta_tokens': nrm((N_META, D_MODEL), 1.0),
        'l0_mix_norm': gain(D_MODEL),
        'l0_w_in': nrm((D_MODEL, MIX0_IN), D_MODEL ** -0.5),
        'l0_ssd_conv_w': nrm((SSD_CONV, SSD_XBC), SSD_CONV ** -0.5),
        'l0_ssd_conv_b': nrm((SSD_XBC,), 0.01),
        'l0_ssd_dt_bias': dt_bias,
        'l0_ssd_a_log': a_log,
        'l0_ssd_d': gain(SSD_HEADS),
        'l0_ssd_norm': gain(SSD_INNER),
        'l0_ret_norm': gain(RET_WIDTH),
        'l0_w_out': nrm((MIX0_OUT, D_MODEL), MIX0_OUT ** -0.5),
        'l0_ffn_norm': gain(D_MODEL),
        'l0_ffn_w_in': nrm((D_MODEL, 2 * FFN_DIM), D_MODEL ** -0.5),
        'l0_ffn_conv_w': nrm((FFN_CONV, 2 * FFN_DIM), FFN_CONV ** -0.5),
        'l0_ffn_conv_b': nrm((2 * FFN_DIM,), 0.01),
        'l0_ffn_w_out': nrm((FFN_DIM, D_MODEL), FFN_DIM ** -0.5),
        'l1_mix_norm': gain(D_MODEL),
        'l1_w_in': nrm((D_MODEL, MIX1_IN), D_MODEL ** -0.5),
        'l1_lru_conv_w': nrm((LRU_CONV, LRU_WIDTH), LRU_CONV ** -0.5),
        'l1_lru_conv_b': nrm((LRU_WIDTH,), 0.01),
        'l1_lru_wa': nrm((LRU_BLOCKS, LRU_BLOCK, LRU_BLOCK), LRU_BLOCK ** -0.5),
        'l1_lru_ba': nrm((LRU_WIDTH,), 0.01),
        'l1_lru_wx': nrm((LRU_BLOCKS, LRU_BLOCK, LRU_BLOCK), LRU_BLOCK ** -0.5),
        'l1_lru_bx': nrm((LRU_WIDTH,), 0.01),
        'l1_lru_lambda': lam,
        'l1_w_out': nrm((MIX1_OUT, D_MODEL), MIX1_OUT ** -0.5),
        'l1_ffn_norm': gain(D_MODEL),
        'l1_ffn_w_in': nrm((D_MODEL, 2 * FFN_DIM), D_MODEL ** -0.5),
        'l1_ffn_conv_w': nrm((FFN_CONV, 2 * FFN_DIM), FFN_CONV ** -0.5),
        'l1_ffn_conv_b': nrm((2 * FFN_DIM,), 0.01),
        'l1_ffn_w_out': nrm((FFN_DIM, D_MODEL), FFN_DIM ** -0.5),
        'final_norm': gain(D_MODEL),
    }

def reference(x, meta_tokens, l0_mix_norm, l0_w_in, l0_ssd_conv_w, l0_ssd_conv_b, l0_ssd_dt_bias, l0_ssd_a_log,
              l0_ssd_d, l0_ssd_norm, l0_ret_norm, l0_w_out, l0_ffn_norm, l0_ffn_w_in, l0_ffn_conv_w, l0_ffn_conv_b,
              l0_ffn_w_out, l1_mix_norm, l1_w_in, l1_lru_conv_w, l1_lru_conv_b, l1_lru_wa, l1_lru_ba, l1_lru_wx,
              l1_lru_bx, l1_lru_lambda, l1_w_out, l1_ffn_norm, l1_ffn_w_in, l1_ffn_conv_w, l1_ffn_conv_b,
              l1_ffn_w_out, final_norm):
    Bsz = x.shape[0]
    meta = jnp.broadcast_to(meta_tokens[None].astype(x.dtype), (Bsz, N_META, D_MODEL))
    h = jnp.concatenate([meta, x], 1)
    even_layers = [(l0_mix_norm,
                    (l0_w_in, l0_ssd_conv_w, l0_ssd_conv_b, l0_ssd_dt_bias, l0_ssd_a_log, l0_ssd_d, l0_ssd_norm, l0_ret_norm, l0_w_out),
                    l0_ffn_norm, (l0_ffn_w_in, l0_ffn_conv_w, l0_ffn_conv_b, l0_ffn_w_out))]
    odd_layers = [(l1_mix_norm,
                   (l1_w_in, l1_lru_conv_w, l1_lru_conv_b, l1_lru_wa, l1_lru_ba, l1_lru_wx, l1_lru_bx, l1_lru_lambda, l1_w_out),
                   l1_ffn_norm, (l1_ffn_w_in, l1_ffn_conv_w, l1_ffn_conv_b, l1_ffn_w_out))]
    for layer in range(DEPTH):
        if layer % 2 == 0:
            mix_norm, mix_params, ffn_norm, ffn_params = even_layers[layer // 2]
            h = h + ssd_retention_mixer(rmsnorm(h, mix_norm), *mix_params)
        else:
            mix_norm, mix_params, ffn_norm, ffn_params = odd_layers[layer // 2]
            h = h + sb_lru_mixer(rmsnorm(h, mix_norm), *mix_params)
        h = h + conv_ffn(rmsnorm(h, ffn_norm), *ffn_params)
    return rmsnorm(h, final_norm)[:, N_META:]


_drawn_inputs = setup_inputs


def setup_inputs(seed=0):
    import zlib

    import numpy as np

    out = dict(_drawn_inputs(seed))
    spreads = {}
    factors = {'l0_ssd_conv_b': 5.266,
     'l0_ssd_d': 6.212,
     'l0_ssd_norm': 4.296,
     'l0_ret_norm': 7.064,
     'l0_ffn_norm': 3.965,
     'l0_ffn_conv_b': 7.751,
     'l1_mix_norm': 5.696,
     'l1_lru_conv_b': 3.74,
     'l1_lru_ba': 55.895,
     'l1_lru_bx': 44.771,
     'l1_ffn_norm': 15.766,
     'l1_ffn_conv_b': 28.344,
     'final_norm': 7.538}
    for name, (base, spread) in spreads.items():
        noise = np.random.default_rng([zlib.crc32(name.encode()), seed]).standard_normal(out[name].shape)
        drawn = base * np.exp(spread * noise) if base else spread * noise
        out[name] = jnp.asarray(drawn.astype(out[name].dtype))
    for name, factor in factors.items():
        out[name] = (out[name] * factor).astype(out[name].dtype)
    return out
```

```python
import concourse.bass as bass
from concourse import mybir
from contextlib import ExitStack

P = 128
D_MODEL, SEQ, N_META = 1024, 512, 16
T = SEQ + N_META
H2 = T // 2
KD = D_MODEL // P
EPS = 1e-6
SSD_HEADS, SSD_GROUPS, HEAD = 16, 4, 64
HPG = SSD_HEADS // SSD_GROUPS
RET_HEADS = 4
SB_SCALE = HEAD ** -0.5
LRU_C = 8.0
GELU_C = (2.0 / 3.141592653589793) ** 0.5
FFN = 2816
KF = FFN // P
KH = KF // 2
NT = 5
SZ = [P, P, P, P, T - 4 * P]
WJ = [T - P * j for j in range(NT)]
OFF = [sum(WJ[:j]) for j in range(NT)]
CAUSAL = sum(WJ)
FULL = OFF[4]
PIECES = [(0, 0, 512, 0, 0, 0), (0, 512, 16, 1, 0, 512), (1, 128, 400, 1, 16, 528),
          (2, 256, 272, 2, 0, 928), (3, 384, 144, 2, 272, 1200), (4, 512, 16, 2, 416, 1344)]
BANKS = [(0, 512, 0), (1, 416, 512), (2, 416, 928)]

COLS = {}
_n = 0
for _name, _k in [("mix0", KD), ("ffn0", KD), ("mix1", KD), ("ffn1", KD), ("final", KD),
                  ("ssd_cw", 64), ("ssd_cb", 16), ("ssd_norm", 8), ("ret_norm", 8),
                  ("f0_cw", 3 * 2 * KF), ("f0_cb", 2 * KF), ("f1_cw", 3 * 2 * KF), ("f1_cb", 2 * KF),
                  ("lru_cw", 32), ("lru_cb", 8), ("lru_ba", 8), ("lru_bx", 8), ("lru_lam", 8),
                  ("ssd_d", 16), ("ssd_dtb", 1), ("ssd_alog", 1)]:
    COLS[_name] = _n
    _n += _k
NCOL = _n

W_DT, W_SSD, W_RET, W_OUT0, W_FI0, W_FO0 = 0, 1, 25, 57, 73, 117
W_L1, W_OUT1, W_FI1, W_FO1, W_END = 133, 173, 189, 233, 249
T_DT, T_SSD, T_RET, T_OUT0, T_FI0, T_FO0 = 0, 1, 25, 57, 65, 109
T_L1, T_OUT1, T_FI1, T_FO1 = 117, 157, 165, 209


class At:

    def __init__(self, a, i, c):
        self.a, self.i, self.c = a, i, c
        self.v = a * i + c
        self.par = c % 2
        self.half = (a // 2) * i + c // 2

    def plus(self, d):
        return At(self.a, self.i, self.c + d)


def wait_count(eng, sem, n):
    if isinstance(n, int) and n <= 0:
        return
    eng.wait_ge(sem, n)


class Chain:

    def __init__(self, eng, sem):
        self.eng, self.sem, self.base, self.n = eng, sem, 0, 0

    def link(self, ins):
        ins.then_inc(self.sem, 1)
        self.n += 1
        self.eng.wait_ge(self.sem, self.base + self.n)

    def enter(self, i, lo, per):
        self.saved, self.per = self.base + self.n, per
        self.base, self.n = self.saved + per * (i - lo), 0

    def leave(self, lo, hi):
        assert self.n == self.per, f"{self.n} links in the loop's body, not {self.per}"
        self.base, self.n = self.saved + self.per * (hi - lo), 0


def build(nc, x_h, vec_h, cst_h, dec_h, w_dt, w_ssd, w_ret, w_out0, w_fi0, w_fo0, w_l1, w_out1, w_fi1, w_fo1,
          w_gate, out):
    f32, f32r = mybir.dt.float32, mybir.dt.float32r
    ALU, ACT = mybir.AluOpType, mybir.ActivationFunctionType
    ctx = ExitStack()
    with ctx:
        def sb(name, shape, dt=f32, where=ctx):
            return where.enter_context(nc.sbuf_tensor(name, shape, dt))

        def sem(name):
            return ctx.enter_context(nc.semaphore(name))

        hT = sb("hT", [P, KD, T])
        hn_hi = sb("hn_hi", [P, KD, T], f32r)
        hn_lo = sb("hn_lo", [P, KD, T], f32r)
        raw = [sb(f"raw{s}", [P, KH * P]) for s in range(2)]
        whi = [sb(f"whi{s}", [P, KH * P], f32r) for s in range(2)]
        wlo = [sb(f"wlo{s}", [P, KH * P], f32r) for s in range(2)]
        vec = sb("vec", [P, NCOL])
        cst = sb("cst", [P, 5 * P])
        ident_b = sb("ident_b", [P, P], mybir.dt.bfloat16)
        never = sb("never", [P, P], mybir.dt.bfloat16)
        ident, ones, neg_u, neg_1 = (cst[:, n * P:(n + 1) * P] for n in range(4))
        sq = [sb(f"sq{s}", [P, T]) for s in range(2)]
        rstd = sb("rstd", [P, T])
        eps_col = sb("eps_col", [P, 1])
        idle_g, idle_v = sb("idle_g", [P, 6]), sb("idle_v", [P, 1])
        nt = [sb(f"nt{s}", [P, T]) for s in range(2)]

        def scope():
            return ExitStack()

        with scope() as mix:
            yT = sb("yT", [P, 16, T], f32, mix)
            with scope() as s1:
                ub = [sb(f"ub{s}", [P, 3 + T], f32, s1) for s in range(2)]
                xcv = sb("xcv", [P, 4, T], f32, s1)
                zc = sb("zc", [P, 2, T], f32, s1)
                xs_tok = sb("xs_tok", [P, NT, 256], f32, s1)
                x_dt = sb("x_dt", [P, NT, 256], f32, s1)
                z_tok = sb("z_tok", [P, NT, 256], f32, s1)
                y_tok = sb("y_tok", [P, NT, 256], f32, s1)
                cbs = sb("cbs", [P, CAUSAL], f32, s1)
                dec = [sb(f"dec{s}", [P, CAUSAL], f32, s1) for s in range(2)]
                cs_bc = sb("cs_bc", [P, HPG, T], f32, s1)
                dt_tok = sb("dt_tok", [P, NT, SSD_HEADS], f32, s1)
                ncs_tok = sb("ncs_tok", [P, NT, SSD_HEADS], f32, s1)
                dtx = sb("dtx", [SSD_HEADS, T], f32, s1)
                dtl = sb("dtl", [SSD_HEADS, T], f32, s1)
                csr = sb("csr", [SSD_HEADS, T], f32, s1)
                one_row = sb("one_row", [SSD_HEADS, T], f32, s1)
                aexp = sb("aexp", [SSD_HEADS, 1], f32, s1)
                ssq_tok = sb("ssq_tok", [P, NT], f32, s1)
                rs_tok = sb("rs_tok", [P, NT], f32, s1)
                neg_half = sb("neg_half", [P, NT], f32, s1)
            with scope() as s2:
                rope = sb("rope", [P, 2, T], f32, s2)
                rdec = sb("rdec", [P, RET_HEADS, T], f32, s2)
                qr = sb("qr", [P, 2, T], f32, s2)
                kr = sb("kr", [P, 2, T], f32, s2)
                rq = sb("rq", [P, 2, T], f32, s2)
                rk = sb("rk", [P, 2, T], f32, s2)
                vr = sb("vr", [P, 2, T], f32, s2)
                gr = sb("gr", [P, 2, T], f32, s2)
                rt = sb("rt", [P, T], f32, s2)
                v_tok = sb("v_tok", [P, NT, 256], f32, s2)
                sdec = sb("sdec", [P, CAUSAL], f32, s2)
                o_tok = sb("o_tok", [P, NT, 256], f32, s2)
                stats = sb("stats", [P, NT, 6], f32, s2)
                mv = sb("mv", [P, NT, 2], f32, s2)
                ret_rs = sb("ret_rs", [P, NT], f32, s2)
                ret_nh = sb("ret_nh", [P, NT], f32, s2)
            with scope() as s3:
                qs = [sb(f"qs{s}", [P, T], f32, s3) for s in range(2)]
                ks = [sb(f"ks{s}", [P, T], f32, s3) for s in range(2)]
                vs = sb("vs", [P, T], f32, s3)
                gt = sb("gt", [P, T], f32, s3)
                ubx = sb("ubx", [P, 3 + T], f32, s3)
                xc = sb("xc", [P, T], f32, s3)
                gw = [sb(f"gw{s}", [P, 2 * P], f32, s3) for s in range(2)]
                sv_tok = sb("sv_tok", [P, NT, P], f32, s3)
                so_tok = sb("so_tok", [P, NT, P], f32, s3)
                lbuf = sb("lbuf", [P, CAUSAL], f32, s3)
                spb = sb("spb", [P, CAUSAL], f32, s3)
                wts = [sb(f"wts{s}", [P, CAUSAL], f32, s3) for s in range(2)]
                tr, ti, la, lt, lb, ge = (sb(n, [P, T], f32, s3) for n in ("tr", "ti", "la", "lt", "lb", "ge"))
                hb = sb("hb", [P, 2, 8], f32, s3)
                nsp = sb("nsp", [P, 8], f32, s3)
                nspt = sb("nspt", [P, 8], f32, s3)
            with scope() as s4:
                y_hi = sb("y_hi", [P, 16, T], f32r, s4)
                y_lo = sb("y_lo", [P, 16, T], f32r, s4)
        with scope() as ffn:
            hid_hi = sb("hid_hi", [P, KF, T], f32r, ffn)
            hid_lo = sb("hid_lo", [P, KF, T], f32r, ffn)
            ubf = [sb(f"ubf{s}", [P, 2 + T], f32, ffn) for s in range(2)]
            cg = sb("cg", [P, T], f32, ffn)
            cu = sb("cu", [P, T], f32, ffn)
            hidf = sb("hidf", [P, T], f32, ffn)

        gp = [ctx.enter_context(nc.psum_tensor(f"gp{s}", [P, 2, 512], f32)) for s in range(2)]
        sp_ = ctx.enter_context(nc.psum_tensor("small", [P, 4, 512], f32))

        def halves(ap):
            return ap.rearrange("p (h t) -> p h t", h=2)

        def gout(s):
            return gp[s][:, :, 0:H2]

        def pcol(name, c=0, n=1, rows=P):
            return vec[0:rows, bass.ds(COLS[name] + c, n)]

        cs_d = nc.dram_tensor("cs_scratch", [SSD_HEADS, T], f32, kind="Internal").ap()

        raw_in = [sem(f"raw_in{s}") for s in range(2)]
        hi_done, lo_done, unit_done = sem("hi_done"), sem("lo_done"), sem("unit_done")
        pair_free = [sem(f"pair_free{s}") for s in range(2)]
        const_in, h_in = sem("const_in"), sem("h_in")
        sq_done, ssq_done, root_done = sem("sq_done"), sem("ssq_done"), sem("root_done")
        nt_done, nhi_done, nlo_done = sem("nt_done"), sem("nhi_done"), sem("nlo_done")
        v_seq, a_seq, g_seq = sem("v_seq"), sem("a_seq"), sem("g_seq")
        yhi_done, ylo_done = sem("yhi_done"), sem("ylo_done")
        ev_f, cg_done, cu_done, sg_done = sem("ev_f"), sem("cg_done"), sem("cu_done"), sem("sg_done")
        hidf_done, hhi_done, hlo_done = sem("hidf_done"), sem("hhi_done"), sem("hlo_done")
        out_done = sem("out_done")
        dtl_done, aexp_done, cs_done, cs_out = (sem(n) for n in ("dtl_done", "aexp_done", "cs_done", "cs_out"))
        dtT_done, dtok_done, bc_in = sem("dtT_done"), sem("dtok_done"), sem("bc_in")
        conv_done, silu_done, txs_done, xstok_done, xdt_done = (
            sem(n) for n in ("conv_done", "silu_done", "txs_done", "xstok_done", "xdt_done"))
        tz_done, ztok_done, cb_done, cbs_done = (sem(n) for n in ("tz_done", "ztok_done", "cb_done", "cbs_done"))
        arg_done, e_done, es_done, m_done, y_done, ytok_done = (
            sem(n) for n in ("arg_done", "e_done", "es_done", "m_done", "y_done", "ytok_done"))
        yz_done, ysq_done, yrs_done, yn_done, tout_done, yout_done = (
            sem(n) for n in ("yz_done", "ysq_done", "yrs_done", "yn_done", "tout_done", "yout_done"))
        tab_in, rot_done, tv_done, vtok_done, sc_done, sdec_done = (
            sem(n) for n in ("tab_in", "rot_done", "tv_done", "vtok_done", "sc_done", "sdec_done"))
        o_done, mv_done, rrs_done, on_done, tro_done, yret_done = (
            sem(n) for n in ("o_done", "mv_done", "rrs_done", "on_done", "tro_done", "yret_done"))
        gw_in = [sem(f"gw_in{s}") for s in range(2)]
        xc_done, gates_done, tri_done, la_done, lb_done, root1_done = (
            sem(n) for n in ("xc_done", "gates_done", "tri_done", "la_done", "lb_done", "root1_done"))
        z_done, l_done, spf_done, suf_done, w_done, pv_done, so_done = (
            sem(n) for n in ("z_done", "l_done", "spf_done", "suf_done", "w_done", "pv_done", "so_done"))
        tvs_done, svtok_done, tso_done, ysb_done, gu_done, gth_done, ylru_done = (
            sem(n) for n in ("tvs_done", "svtok_done", "tso_done", "ysb_done", "gu_done", "gth_done", "ylru_done"))
        prep_done, spl_done, spl_ln = sem("prep_done"), sem("spl_done"), sem("spl_ln")

        block = ctx.enter_context(nc.Block())

        @block.sync
        def _(sp):
            def unit(w, src, kt=KD):
                wait_count(sp, lo_done, w.v - 1)
                sp.dma_start(raw[w.par][:, 0:kt * P], src).then_inc(raw_in[w.par], 16)

            sp.dma_start(hT[:], x_h).then_inc(h_in, 16)
            sp.dma_start(vec[:], vec_h).then_inc(const_in, 16)
            sp.dma_start(cst[:], cst_h[:, 0:5 * P]).then_inc(const_in, 16)
            unit(At(0, 0, 0), w_dt[0])
            unit(At(0, 0, 1), w_ssd[0])
            for c in range(1, 6):
                unit(At(6, 0, W_SSD + c), w_ssd[c])
            with sp.Fori(1, SSD_GROUPS) as g:
                for c in range(6):
                    unit(At(6, g, W_SSD + c), w_ssd[6 * g + c])
            for c in range(2):
                unit(At(8, 0, W_RET + c), w_ret[c])
            sp.wait_ge(yout_done, SSD_GROUPS)
            sp.dma_start(rope[:], cst_h[:, 5 * P:5 * P + 2 * T].rearrange("p (a t) -> p a t", a=2)).then_inc(tab_in, 16)
            sp.dma_start(rdec[:], dec_h).then_inc(tab_in, 16)
            for c in range(2, 8):
                unit(At(8, 0, W_RET + c), w_ret[c])
            with sp.Fori(1, RET_HEADS) as r:
                for c in range(8):
                    unit(At(8, r, W_RET + c), w_ret[8 * r + c])

            def stream(base, n, src, kt=KD):
                with sp.Fori(0, n // 2) as i:
                    for s in range(2):
                        unit(At(2, i, base + s), src[2 * i + s], kt)

            stream(W_OUT0, 16, w_out0)
            stream(W_FI0, 2 * KF, w_fi0)
            stream(W_FO0, 16, w_fo0, KH)

            def l1_pair(i):
                for b in range(2):
                    for c in range(5):
                        if c == 4:
                            if isinstance(i, int):
                                sp.wait_ge(unit_done, W_L1)
                            else:
                                sp.wait_ge(gates_done, 2 * i + b - 1)
                            sp.dma_start(gw[b][:], w_gate[2 * i + b]).then_inc(gw_in[b], 16)
                        unit(At(10, i, W_L1 + 5 * b + c), w_l1[10 * i + 5 * b + c])

            l1_pair(0)
            with sp.Fori(1, 4) as i:
                l1_pair(i)
            stream(W_OUT1, 16, w_out1)
            stream(W_FI1, 2 * KF, w_fi1)
            stream(W_FO1, 16, w_fo1, KH)
            sp.wait_ge(nt_done, 5 * KD)
            sp.dma_start(out, yT[:, 0:KD, N_META:T]).then_inc(out_done, 16)
            sp.wait_ge(out_done, 16)

        @block.tensor
        def _(pe):
            def gemm(w, t, rhs_hi, rhs_lo, k0=0, kt=KD, first=True, last=True, ready=None):
                pe.wait_ge(lo_done, w.v + 1)
                if first:
                    wait_count(pe, pair_free[t.par], t.half)
                for k in range(kt):
                    if ready is not None:
                        pe.wait_ge(ready[0], ready[1] + k0 + k + 1)
                    cols = slice(k * P, (k + 1) * P)
                    for n, (wp, rp) in enumerate(((whi, rhs_hi), (whi, rhs_lo), (wlo, rhs_hi))):
                        for h in range(2):
                            ins = pe.matmul(gp[t.par][:, h, 0:H2], wp[w.par][:, cols],
                                            rp[:, k0 + k, h * H2:(h + 1) * H2],
                                            start=first and k == 0 and n == 0,
                                            stop=last and k == kt - 1 and n == 2)
                ins.then_inc(unit_done, 1)

            def hgemm(w, t, ready=None):
                gemm(w, t, hn_hi, hn_lo, ready=ready)

            def sum_squares(n, m):
                pe.wait_ge(sq_done, KD * n + m + 1)
                for h in range(2):
                    ins = pe.matmul(sp_[:, h, 0:H2], ones, sq[m % 2][:, h * H2:(h + 1) * H2],
                                    start=m == 0, stop=m == KD - 1)
                ins.then_inc(ssq_done, 1)

            def to_tokens(src, bank0, done):
                for i in range(NT):
                    for c in range(2):
                        ins = pe.transpose(sp_[0:SZ[i], bank0 + i // 2, (i % 2) * 256 + c * P:(i % 2) * 256 + (c + 1) * P],
                                           src[:, c, P * i:P * i + SZ[i]], ident)
                ins.then_inc(done, 1)

            def to_channels(src, done):
                for i in range(NT):
                    for c in range(2):
                        dst = sp_[:, 2 * c, P * i:P * i + P] if i < 4 else sp_[:, 2 * c + 1, 0:SZ[4]]
                        ins = pe.transpose(dst, src[0:SZ[i], i, c * P:(c + 1) * P], ident[0:SZ[i], 0:SZ[i]])
                ins.then_inc(done, 1)

            def causal(keys, queries, done, once=False):
                for j, q0, n, b, c0, _ in PIECES:
                    for d, (kk, qq) in enumerate(zip(keys, queries)):
                        ins = pe.matmul(sp_[0:SZ[j], b, c0:c0 + n], kk[:, P * j:P * j + SZ[j]], qq[:, q0:q0 + n],
                                        start=(d == 0) if not once else c0 == 0, stop=d == len(keys) - 1,
                                        skip_group_check=once)
                if done is not None:
                    ins.then_inc(done, 1)

            def mix_values(wt, val, width, dst, done):
                for i in range(NT):
                    for j in range(i + 1):
                        at = OFF[j] + P * (i - j)
                        ins = pe.matmul(dst(i), wt[0:SZ[j], at:at + SZ[i]], val(j), start=j == 0, stop=j == i)
                ins.then_inc(done, 1)

            pe.wait_ge(const_in, 32)
            for m in range(KD):
                sum_squares(0, m)

            hgemm(At(0, 0, W_DT), At(0, 0, T_DT), ready=(nlo_done, 0))
            for c in range(6):
                hgemm(At(6, 0, W_SSD + c), At(6, 0, T_SSD + c))
                if c == 0:
                    pe.wait_ge(cs_done, 1)
                    for n, src in enumerate((dtx, csr)):
                        for i in range(NT):
                            ins = pe.transpose(sp_[0:SZ[i], 2, 80 * n + 16 * i:80 * n + 16 * i + 16],
                                               src[:, P * i:P * i + SZ[i]], ident[0:16, 0:16])
                    ins.then_inc(dtT_done, 1)
            pe.wait_ge(dtok_done, 1)

            def ssd_small(g, step):
                if step == 0:
                    pe.wait_ge(silu_done, g + 1)
                    wait_count(pe, yout_done, g)
                    to_tokens(xcv[:, 0:2, :], 0, txs_done)
                if step == 1:
                    pe.wait_ge(xstok_done, g + 1)
                    to_tokens(zc, 0, tz_done)
                if step == 2:
                    pe.wait_ge(ztok_done, g + 1)
                    causal([xcv[:, 2, :]], [xcv[:, 3, :]], cb_done)
                if step in (3, 4):
                    for h in ((0, 1) if step == 3 else (2, 3)):
                        pe.wait_ge(m_done, HPG * g + h + 1)
                        if h == 0:
                            pe.wait_ge(cbs_done, g + 1)
                        mix_values(dec[h % 2], lambda j: x_dt[0:SZ[j], j, HEAD * h:HEAD * (h + 1)], HEAD,
                                   lambda i: sp_[0:SZ[i], h, HEAD * i:HEAD * (i + 1)], y_done)
                if step == 5:
                    pe.wait_ge(yn_done, g + 1)
                    to_channels(y_tok, tout_done)

            def ssd_stage(g):
                for c in range(6):
                    hgemm(At(6, g, W_SSD + c), At(6, g, T_SSD + c))
                    ssd_small(g - 1, c)

            ssd_stage(1)
            with pe.Fori(2, SSD_GROUPS) as g:
                ssd_stage(g)
            for c in range(6):
                ssd_small(SSD_GROUPS - 1, c)

            def ret_small(r, step):
                if step == 0:
                    wait_count(pe, yret_done, r)
                    pe.wait_ge(pair_free[(T_RET + 5) % 2], (T_RET + 5) // 2 + 1 + 4 * r)
                    to_tokens(vr, 0, tv_done)
                if step == 1:
                    pe.wait_ge(vtok_done, r + 1)
                    pe.wait_ge(rot_done, 2 * (r + 1))
                    causal([rk[:, 0, :], rk[:, 1, :]], [rq[:, 0, :], rq[:, 1, :]], sc_done)
                if step == 3:
                    pe.wait_ge(sdec_done, r + 1)
                    mix_values(sdec, lambda j: v_tok[0:SZ[j], j, :], 256,
                               lambda i: sp_[0:SZ[i], i // 2, (i % 2) * 256:(i % 2) * 256 + 256], o_done)
                if step == 5:
                    pe.wait_ge(on_done, r + 1)
                    to_channels(o_tok, tro_done)

            for c in range(8):
                hgemm(At(8, 0, W_RET + c), At(8, 0, T_RET + c))
            def ret_stage(r):
                for c in range(8):
                    hgemm(At(8, r, W_RET + c), At(8, r, T_RET + c))
                    ret_small(r - 1, c)

            ret_stage(1)
            with pe.Fori(2, RET_HEADS) as r:
                ret_stage(r)
            for c in range(8):
                ret_small(RET_HEADS - 1, c)

            def project(wb, tb, rhs_hi, rhs_lo, kt, n, ready):
                def tile(i, s, m, first_pair):
                    for kh in range(2):
                        gemm(At(4, i, wb + 2 * s + kh), At(2, i, tb + s), rhs_hi, rhs_lo, k0=kh * kt, kt=kt,
                             first=kh == 0, last=kh == 1, ready=ready if first_pair and s == 0 else None)
                        if kh == 0 and not (first_pair and s == 0):
                            squares(n, m, s, first_pair)

                def squares(n, m, s, first_pair):
                    pe.wait_ge(sq_done, KD * n + m)
                    for h in range(2):
                        ins = pe.matmul(sp_[:, h, 0:H2], ones, sq[(s - 1) % 2][:, h * H2:(h + 1) * H2],
                                        start=first_pair and s == 1, stop=False, skip_group_check=True)
                    ins.then_inc(ssq_done, 1)

                for s in range(2):
                    tile(0, s, s, True)
                with pe.Fori(1, KD // 2) as i:
                    for s in range(2):
                        tile(i, s, 2 * i + s, False)
                pe.wait_ge(sq_done, KD * (n + 1))
                for h in range(2):
                    ins = pe.matmul(sp_[:, h, 0:H2], ones, sq[1][:, h * H2:(h + 1) * H2],
                                    start=False, stop=True, skip_group_check=True)
                ins.then_inc(ssq_done, 1)

            def ffn_in(wb, tb, n):
                for s in range(2):
                    hgemm(At(2, 0, wb + s), At(2, 0, tb + s), ready=(nlo_done, KD * n) if s == 0 else None)
                with pe.Fori(1, KF) as i:
                    for s in range(2):
                        hgemm(At(2, i, wb + s), At(2, i, tb + s))

            project(W_OUT0, T_OUT0, y_hi, y_lo, KD, 1, (ylo_done, 0))
            ffn_in(W_FI0, T_FI0, 1)
            project(W_FO0, T_FO0, hid_hi, hid_lo, KH, 2, (hlo_done, 0))

            def sb_small(i, b, step):
                n = 2 * i + b

                def scores(e):
                    rows = slice(HEAD * e, HEAD * (e + 1))
                    causal([ks[b][rows, :]], [qs[b][rows, :]], None, once=True)
                    for j, _, _, bk, c0, _ in (PIECES[0], *PIECES[2:]):
                        ins = pe.matmul(sp_[0:SZ[j], bk, c0:c0 + SZ[j]], ident_b[0:SZ[j], 0:SZ[j]],
                                        never[0:SZ[j], 0:SZ[j]], start=False, stop=True, skip_group_check=True)
                    ins.then_inc(z_done, 1)

                def suffix(e):
                    pe.wait_ge(spf_done, 2 * n + e + 1)
                    for j, q0, w, bk, c0, _ in PIECES:
                        for jj in range(j, NT):
                            lo = max(q0, P * jj)
                            if lo >= q0 + w:
                                continue
                            lhs = neg_u[0:SZ[j], 0:SZ[j]] if jj == j else neg_1[0:SZ[jj], 0:SZ[j]]
                            at = OFF[jj] + lo - P * jj
                            ins = pe.matmul(sp_[0:SZ[j], bk, c0 + lo - q0:c0 + w], lhs,
                                            spb[0:SZ[jj], at:at + q0 + w - lo], start=False, stop=True,
                                            skip_group_check=True)
                    ins.then_inc(suf_done, 1)

                def values(e):
                    pe.wait_ge(w_done, 2 * n + e + 1)
                    wait_count(pe, so_done, 2 * n + e)
                    mix_values(wts[e], lambda j: sv_tok[0:SZ[j], j, HEAD * e:HEAD * (e + 1)], HEAD,
                               lambda i: sp_[0:SZ[i], 3, HEAD * i:HEAD * (i + 1)], pv_done)

                if step == 0:
                    pe.wait_ge(xc_done, n + 1)
                    pe.wait_ge(gw_in[b], 16 * (i + 1))
                    wait_count(pe, ysb_done, n)
                    for gate, (b0, b1, c1) in enumerate(((0, 1, 0), (2, 1, 16))):
                        pe.matmul(sp_[:, b0, 0:512], gw[b][:, gate * P:(gate + 1) * P], xc[:, 0:512],
                                  start=True, stop=True)
                        ins = pe.matmul(sp_[:, b1, c1:c1 + 16], gw[b][:, gate * P:(gate + 1) * P], xc[:, 512:T],
                                        start=True, stop=True)
                    ins.then_inc(gates_done, 1)
                    for i in range(NT):
                        dst = sp_[:, 3, P * i:P * (i + 1)] if i < 4 else sp_[0:SZ[4], 1, 32:32 + P]
                        ins = pe.transpose(dst, vs[:, P * i:P * i + SZ[i]], ident)
                    ins.then_inc(tvs_done, 1)
                if step == 1:
                    pe.wait_ge(tri_done, n + 1)
                    pe.wait_ge(svtok_done, n + 1)
                    scores(0)
                if step == 2:
                    suffix(0)
                if step == 3:
                    pe.wait_ge(w_done, 2 * n + 1)
                    values(0)
                    scores(1)
                if step == 4:
                    suffix(1)
                    pe.wait_ge(w_done, 2 * n + 2)
                    values(1)
                    pe.wait_ge(so_done, 2 * n + 2)
                    for i in range(NT):
                        dst = sp_[:, 0, P * i:P * (i + 1)] if i < 4 else sp_[:, 1, 0:SZ[4]]
                        ins = pe.transpose(dst, so_tok[0:SZ[i], i, :], ident[0:SZ[i], 0:SZ[i]])
                    ins.then_inc(tso_done, 1)

            def l1_pair(i):
                for b in range(2):
                    for c in range(5):
                        hgemm(At(10, i, W_L1 + 5 * (b + 1) + c), At(10, i, T_L1 + 5 * (b + 1) + c))
                        sb_small(i, b, c)

            for c in range(5):
                hgemm(At(10, 0, W_L1 + c), At(10, 0, T_L1 + c), ready=(nlo_done, 2 * KD) if c == 0 else None)
            l1_pair(0)
            with pe.Fori(1, 3) as i:
                l1_pair(i)
            for c in range(5):
                hgemm(At(10, 3, W_L1 + 5 + c), At(10, 3, T_L1 + 5 + c))
                sb_small(3, 0, c)
            for c in range(5):
                sb_small(3, 1, c)

            project(W_OUT1, T_OUT1, y_hi, y_lo, KD, 3, (ylo_done, 16))
            ffn_in(W_FI1, T_FI1, 3)
            project(W_FO1, T_FO1, hid_hi, hid_lo, KH, 4, (hlo_done, KF))

        @block.scalar
        def _(act):
            ch = Chain(act, a_seq)

            def split_hi(w, kt=KD):
                act.wait_ge(raw_in[w.par], 16 * (w.half + 1))
                wait_count(act, unit_done, w.v - 1)
                act.activation(whi[w.par][:, 0:kt * P], raw[w.par][:, 0:kt * P], ACT.Copy).then_inc(hi_done, 1)
                act.wait_ge(hi_done, w.v + 1)

            def evacuate(w, t, dst, func=ACT.Copy, scale=1.0):
                act.wait_ge(unit_done, w.v + 1)
                act.activation(dst, gout(t.par), func, scale=scale).then_inc(pair_free[t.par], 1)

            def square(n, m, s):
                wait_count(act, ssq_done, KD * n + m - 1)
                act.activation(sq[s][:], hT[:, m, :], ACT.Square).then_inc(sq_done, 1)

            def root(n):
                act.wait_ge(ssq_done, KD * (n + 1))
                act.activation(halves(rstd[:]), sp_[:, 0:2, 0:H2], ACT.Sqrt, scale=1.0 / D_MODEL,
                               bias=eps_col[:, 0:1]).then_inc(root_done, 1)

            def norm_hi(n):
                root(n)
                for k in range(KD):
                    act.wait_ge(nt_done, KD * n + k + 1)
                    act.activation(hn_hi[:, k, :], nt[k % 2][:], ACT.Copy).then_inc(nhi_done, 1)

            split_hi(At(0, 0, 0))
            act.wait_ge(h_in, 16)
            for m in range(KD):
                square(0, m, m % 2)
            act.wait_ge(prep_done, 1)
            norm_hi(0)

            split_hi(At(0, 0, 1))
            act.wait_ge(const_in, 32)
            act.activation(aexp[:], pcol("ssd_alog", rows=16), ACT.Exp).then_inc(aexp_done, 1)
            act.wait_ge(pair_free[0], 1)
            ch.link(act.activation(dtl[:], dtx[:], ACT.Abs))
            ch.link(act.activation(dtl[:], dtl[:], ACT.Exp, scale=-1.0))
            act.activation(dtl[:], dtl[:], ACT.Ln, bias=1.0).then_inc(dtl_done, 1)

            def load_bc(g):
                src = cs_d[bass.ds(HPG * g, HPG), :].unsqueeze(0).to_broadcast([P, HPG, T])
                act.dma_start(cs_bc[:], src).then_inc(bc_in, 16)

            def ssd_gemm(g, c):
                w, t = At(6, g, W_SSD + c), At(6, g, T_SSD + c)
                if c < 4:
                    wait_count(act, conv_done, 4 * g + c - 1)
                    evacuate(w, t, halves(ub[c % 2][:, 3:3 + T]))
                else:
                    wait_count(act, tz_done, g)
                    evacuate(w, t, halves(zc[:, c - 4, :]))

            def ssd_silu(g):
                act.wait_ge(conv_done, 4 * (g + 1))
                act.activation(xcv[:], xcv[:], ACT.Silu)
                act.wait_ge(pair_free[(T_SSD + 5) % 2], (T_SSD + 5) // 2 + 1 + 3 * g)
                act.activation(zc[:], zc[:], ACT.Silu).then_inc(silu_done, 1)

            def ssd_small(g, step):
                if step == 0:
                    ssd_silu(g)
                if step == 1:
                    act.wait_ge(txs_done, g + 1)
                    wait_count(act, ytok_done, HPG * g)
                    act.activation(xs_tok[:, 0:4, :].rearrange("p (b i) c -> p b (i c)", b=2), sp_[:, 0:2, :], ACT.Copy)
                    act.activation(xs_tok[0:SZ[4], 4, :], sp_[0:SZ[4], 2, 0:256], ACT.Copy).then_inc(xstok_done, 1)
                    for h in range(2):
                        decay(g, h)
                if step == 2:
                    act.wait_ge(tz_done, g + 1)
                    wait_count(act, yz_done, g)
                    act.activation(z_tok[:, 0:4, :].rearrange("p (b i) c -> p b (i c)", b=2), sp_[:, 0:2, :], ACT.Copy)
                    act.activation(z_tok[0:SZ[4], 4, :], sp_[0:SZ[4], 2, 0:256], ACT.Copy).then_inc(ztok_done, 1)
                if step == 3:
                    act.wait_ge(cb_done, g + 1)
                    for b, n, at in BANKS:
                        act.activation(cbs[:, at:at + n], sp_[:, b, 0:n], ACT.Copy)
                    act.activation(cbs[0:SZ[4], FULL:CAUSAL], sp_[0:SZ[4], 2, 416:432], ACT.Copy).then_inc(cbs_done, 1)
                if step == 4:
                    for h in range(2, 4):
                        decay(g, h)
                if step == 5:
                    act.wait_ge(yz_done, g + 1)
                    wait_count(act, yrs_done, g)
                    for i in range(NT):
                        ins = act.activation(x_dt[0:SZ[i], i, :], y_tok[0:SZ[i], i, :], ACT.Square,
                                             accum_out=ssq_tok[0:SZ[i], i:i + 1])
                    ins.then_inc(ysq_done, 1)
                if step == 6:
                    act.wait_ge(tout_done, g + 1)
                    for c in range(2):
                        act.activation(yT[:, 2 * g + c, 0:512], sp_[:, 2 * c, :], ACT.Copy, scale=pcol("ssd_norm", 2 * g + c))
                        ins = act.activation(yT[:, 2 * g + c, 512:T], sp_[:, 2 * c + 1, 0:16], ACT.Copy,
                                             scale=pcol("ssd_norm", 2 * g + c))
                    ins.then_inc(yout_done, 1)

            def decay(g, h):
                act.wait_ge(arg_done, HPG * g + h + 1)
                e = dec[h % 2]
                act.activation(e[:, 0:FULL], e[:, 0:FULL], ACT.Exp)
                act.activation(e[0:SZ[4], FULL:CAUSAL], e[0:SZ[4], FULL:CAUSAL], ACT.Exp).then_inc(e_done, 1)

            split_hi(At(6, 0, W_SSD + 1))
            for c in range(5):
                split_hi(At(6, 0, W_SSD + c + 2))
                ssd_gemm(0, c)
                if c == 0:
                    act.wait_ge(cs_done, 1)
                    act.dma_start(cs_d, csr[:]).then_inc(cs_out, 16)
                    act.wait_ge(cs_out, 16)
                    load_bc(0)

            def ssd_stage(g):
                for c in range(6):
                    split_hi(At(6, g, W_SSD + c + 1))
                    if c == 0:
                        ssd_gemm(g - 1, 5)
                    else:
                        ssd_gemm(g, c - 1)
                    ssd_small(g - 1, c)
                    if c == 4:
                        act.wait_ge(arg_done, HPG * g)
                        load_bc(g)
                ssd_small(g - 1, 6)

            ssd_stage(1)
            with act.Fori(2, SSD_GROUPS) as g:
                ssd_stage(g)
            ssd_gemm(SSD_GROUPS - 1, 5)
            for c in range(7):
                ssd_small(SSD_GROUPS - 1, c)

            def ret_gemm(r, c):
                w, t = At(8, r, W_RET + c), At(8, r, T_RET + c)
                if c < 2:
                    wait_count(act, rot_done, 2 * r - 1)
                    evacuate(w, t, halves(qr[:, c, :]))
                elif c < 4:
                    wait_count(act, rot_done, 2 * r)
                    evacuate(w, t, halves(kr[:, c - 2, :]))
                elif c < 6:
                    wait_count(act, tv_done, r)
                    evacuate(w, t, halves(vr[:, c - 4, :]))
                else:
                    wait_count(act, yret_done, r)
                    evacuate(w, t, halves(gr[:, c - 6, :]), ACT.Silu)

            def ret_small(r, step):
                if step == 1:
                    act.wait_ge(tv_done, r + 1)
                    wait_count(act, o_done, r)
                    act.activation(v_tok[:, 0:4, :].rearrange("p (b i) c -> p b (i c)", b=2), sp_[:, 0:2, :], ACT.Copy)
                    act.activation(v_tok[0:SZ[4], 4, :], sp_[0:SZ[4], 2, 0:256], ACT.Copy).then_inc(vtok_done, 1)

            for c in range(8):
                if c > 0:
                    split_hi(At(8, 0, W_RET + c + 1))
                    ret_gemm(0, c - 1)
                else:
                    split_hi(At(8, 0, W_RET + 1))

            def ret_stage(r):
                for c in range(8):
                    split_hi(At(8, r, W_RET + c + 1))
                    if c == 0:
                        ret_gemm(r - 1, 7)
                    else:
                        ret_gemm(r, c - 1)
                    ret_small(r - 1, c)

            ret_stage(1)
            with act.Fori(2, RET_HEADS) as r:
                ret_stage(r)
            ret_gemm(RET_HEADS - 1, 7)
            ret_small(RET_HEADS - 1, 1)

            def project(wb, tb, kt, n, src=False, following=True):
                if src:
                    for k in range(16):
                        act.activation(y_hi[:, k, :], yT[:, k, :], ACT.Copy).then_inc(yhi_done, 1)
                        if k == 7:
                            split_hi(At(0, 0, wb + 1), kt)
                else:
                    split_hi(At(0, 0, wb + 1), kt)

                def tile(i, s, m, last=False):
                    if following or not last:
                        split_hi(At(4, i, wb + 2 * s + 2), KD if last else kt)
                    if not last:
                        split_hi(At(4, i, wb + 2 * s + 3), kt)
                    t = At(2, i, tb + s)
                    act.wait_ge(pair_free[t.par], t.half + 1)
                    square(n, m, s)

                for s in range(2):
                    tile(0, s, s)
                with act.Fori(1, KD // 2 - 1) as i:
                    for s in range(2):
                        tile(i, s, 2 * i + s)
                tile(KD // 2 - 1, 0, KD - 2)
                tile(KD // 2 - 1, 1, KD - 1, last=True)

            def ffn_in(wb, tb, L):
                def slot_a(i):
                    wait_count(act, cu_done, KF * L + i - 1)
                    evacuate(At(2, i, wb - 1), At(2, i, tb - 1), halves(ubf[1][:, 2:2 + T]))
                    act.wait_ge(cg_done, KF * L + i)
                    act.activation(cg[:], cg[:], ACT.Silu).then_inc(sg_done, 1)

                def slot_b(i):
                    wait_count(act, cg_done, KF * L + i)
                    evacuate(At(2, i, wb), At(2, i, tb), halves(ubf[0][:, 2:2 + T]))

                def hid(i):
                    act.wait_ge(hidf_done, KF * L + i)
                    act.activation(hid_hi[:, i - 1, :], hidf[:], ACT.Copy).then_inc(hhi_done, 1)

                split_hi(At(2, 0, wb + 1))
                split_hi(At(2, 0, wb + 2))
                slot_b(0)

                def pair(i):
                    split_hi(At(2, i, wb + 1))
                    slot_a(i)
                    split_hi(At(2, i, wb + 2))
                    slot_b(i)
                    hid(i)

                pair(1)
                with act.Fori(2, KF - 1) as i:
                    pair(i)
                i = KF - 1
                split_hi(At(2, i, wb + 1))
                slot_a(i)
                split_hi(At(2, i, wb + 2), KH)
                slot_b(i)
                hid(i)
                slot_a(KF)
                hid(KF)

            act.wait_ge(yret_done, RET_HEADS)
            project(W_OUT0, T_OUT0, KD, 1, src=True)
            norm_hi(1)
            ffn_in(W_FI0, T_FI0, 0)
            project(W_FO0, T_FO0, KH, 2)
            norm_hi(2)

            act.wait_ge(spl_done, 1)
            ch.link(act.activation(nspt[:], pcol("lru_lam", 0, 8), ACT.Abs))
            ch.link(act.activation(nspt[:], nspt[:], ACT.Exp, scale=-1.0))
            act.activation(nspt[:], nspt[:], ACT.Ln, bias=1.0).then_inc(spl_ln, 1)
            act.wait_ge(spl_done, 2)

            def l1_gemm(i, b, c):
                n = 2 * i + b
                w, t = At(10, i, W_L1 + 5 * b + c), At(10, i, T_L1 + 5 * b + c)
                if c == 0:
                    wait_count(act, z_done, 2 * n - 2)
                    evacuate(w, t, halves(qs[b % 2][:]), scale=SB_SCALE)
                if c == 1:
                    wait_count(act, z_done, 2 * n - 2)
                    evacuate(w, t, halves(ks[b % 2][:]))
                if c == 2:
                    wait_count(act, tvs_done, n)
                    evacuate(w, t, halves(vs[:]))
                if c == 3:
                    wait_count(act, ylru_done, n)
                    evacuate(w, t, halves(gt[:]))
                if c == 4:
                    wait_count(act, xc_done, n)
                    evacuate(w, t, halves(ubx[:, 3:3 + T]))

            def soft(n, e):
                act.wait_ge(z_done, 2 * n + e + 1)
                for b, w, at in BANKS:
                    act.activation(lbuf[:, at:at + w], sp_[:, b, 0:w], ACT.Abs)
                ch.link(act.activation(lbuf[0:SZ[4], FULL:CAUSAL], sp_[0:SZ[4], 2, 416:432], ACT.Abs))
                act.activation(lbuf[:, 0:FULL], lbuf[:, 0:FULL], ACT.Exp, scale=-1.0)
                ch.link(act.activation(lbuf[0:SZ[4], FULL:CAUSAL], lbuf[0:SZ[4], FULL:CAUSAL], ACT.Exp, scale=-1.0))
                act.activation(lbuf[:, 0:FULL], lbuf[:, 0:FULL], ACT.Ln, bias=1.0)
                act.activation(lbuf[0:SZ[4], FULL:CAUSAL], lbuf[0:SZ[4], FULL:CAUSAL], ACT.Ln, bias=1.0).then_inc(l_done, 1)

            def weigh(n, e):
                act.wait_ge(suf_done, 2 * n + e + 1)
                wait_count(act, pv_done, 2 * n + e - 1)
                for b, w, at in BANKS:
                    act.activation(wts[e][:, at:at + w], sp_[:, b, 0:w], ACT.Exp)
                act.activation(wts[e][0:SZ[4], FULL:CAUSAL], sp_[0:SZ[4], 2, 416:432], ACT.Exp).then_inc(w_done, 1)

            def l1_small(n, step):
                if step == 1:
                    act.wait_ge(tvs_done, n + 1)
                    for dst, gate, (b0, b1, c1) in ((tr, 0, (0, 1, 0)), (ti, 1, (2, 1, 16))):
                        wait_count(act, ylru_done, n)
                        act.activation(dst[:, 0:512], sp_[:, b0, 0:512], ACT.Tanh, scale=0.5, bias=hb_col(gate, n))
                        ins = act.activation(dst[:, 512:T], sp_[:, b1, c1:c1 + 16], ACT.Tanh, scale=0.5,
                                             bias=hb_col(gate, n))
                    ins.then_inc(tri_done, 1)
                    act.wait_ge(tri_done, n + 1)
                    wait_count(act, pv_done, 2 * n)
                    act.activation(sv_tok[:, 0:4, :], sp_[:, 3, :].rearrange("p (i c) -> p i c", c=P), ACT.Copy)
                    act.activation(sv_tok[0:SZ[4], 4, :], sp_[0:SZ[4], 1, 32:32 + P], ACT.Copy).then_inc(svtok_done, 1)
                    act.activation(lt[:], tr[:], ACT.Tanh, scale=nsp_col(n), bias=nsp_col(n))
                    act.activation(la[:], tr[:], ACT.Exp, scale=nsp_col(n), bias=nsp_col(n)).then_inc(la_done, 1)
                    act.wait_ge(gu_done, n + 1)
                    act.activation(ge[:], ge[:], ACT.Tanh, scale=GELU_C).then_inc(gth_done, 1)
                    act.wait_ge(lb_done, n + 1)
                    act.activation(lb[:], lb[:], ACT.Sqrt, scale=0.25).then_inc(root1_done, 1)
                if step == 2:
                    soft(n, 0)
                if step == 3:
                    weigh(n, 0)
                if step == 4:
                    soft(n, 1)
                if step == 5:
                    weigh(n, 1)
                    act.wait_ge(tso_done, n + 1)
                    act.activation(yT[:, n, 0:512], sp_[:, 0, :], ACT.Copy)
                    act.activation(yT[:, n, 512:T], sp_[:, 1, 0:16], ACT.Copy).then_inc(ysb_done, 1)

            def hb_col(gate, n):
                return hb[:, gate, bass.ds(n, 1)]

            def nsp_col(n):
                return nsp[:, bass.ds(n, 1)]

            split_hi(At(10, 0, W_L1 + 1))
            for c in range(1, 5):
                split_hi(At(10, 0, W_L1 + c + 1))
                l1_gemm(0, 0, c - 1)

            def l1_pair(i):
                for b in range(2):
                    for c in range(5):
                        split_hi(At(10, i, W_L1 + 5 * (b + 1) + c + 1))
                        if c == 0:
                            l1_gemm(i, b, 4)
                        else:
                            l1_gemm(i, b + 1, c - 1)
                        l1_small(2 * i + b, c)
                    l1_small(2 * i + b, 5)

            l1_pair(0)
            with act.Fori(1, 3) as i:
                ch.enter(i, 1, 8)
                l1_pair(i)
            ch.leave(1, 3)
            for c in range(5):
                split_hi(At(10, 3, W_L1 + 5 + c + 1))
                if c == 0:
                    l1_gemm(3, 0, 4)
                else:
                    l1_gemm(3, 1, c - 1)
                l1_small(6, c)
            l1_small(6, 5)
            l1_gemm(3, 1, 4)
            for c in range(6):
                l1_small(7, c)
            act.wait_ge(ysb_done, 8)
            act.wait_ge(ylru_done, 8)
            project(W_OUT1, T_OUT1, KD, 3, src=True)
            norm_hi(3)
            ffn_in(W_FI1, T_FI1, 1)
            project(W_FO1, T_FO1, KH, 4, following=False)
            root(4)

        @block.vector
        def _(ve):
            ch = Chain(ve, v_seq)

            def split_lo(w, kt=KD):
                ve.wait_ge(hi_done, w.v + 1)
                n = slice(0, kt * P)
                ve.tensor_tensor(wlo[w.par][:, n], raw[w.par][:, n], whi[w.par][:, n].bitcast(f32),
                                 ALU.subtract).then_inc(lo_done, 1)
                ve.wait_ge(lo_done, w.v + 1)

            def apply_norm(n, gain, parts=True):
                ve.wait_ge(root_done, n + 1)
                ch.link(ve.reciprocal(rstd[:], rstd[:]))

                def lo(k):
                    ve.wait_ge(nhi_done, KD * n + k + 1)
                    ve.tensor_tensor(hn_lo[:, k, :], nt[k % 2][:], hn_hi[:, k, :].bitcast(f32),
                                     ALU.subtract).then_inc(nlo_done, 1)

                for k in range(KD):
                    dst = nt[k % 2][:] if parts else yT[:, k, :]
                    if parts and k > 1:
                        ve.wait_ge(nlo_done, KD * n + k - 1)
                    ve.scalar_tensor_tensor(dst, hT[:, k, :], pcol(gain, k), rstd[:], ALU.mult,
                                            ALU.mult).then_inc(nt_done, 1)
                    if parts and k > 0:
                        lo(k - 1)
                if parts:
                    lo(KD - 1)

            def conv(dst, src, taps, w0, b0, link, done):
                link(ve.tensor_scalar(dst, src[:, taps - 1:taps - 1 + T], w0(taps - 1), b0, ALU.mult, ALU.add))
                for k in range(taps - 2, -1, -1):
                    ins = ve.scalar_tensor_tensor(dst, src[:, k:k + T], w0(k), dst, ALU.mult, ALU.add)
                    if k:
                        link(ins)
                ins.then_inc(done, 1)

            for s in range(2):
                ve.memset(ub[s][:, 0:3], 0.0)
            ve.memset(neg_half[:], -0.5)
            ve.memset(one_row[:], 1.0)
            ve.memset(eps_col[:], EPS).then_inc(prep_done, 1)
            ve.wait_ge(h_in, 16)
            ve.wait_ge(const_in, 32)
            ve.tensor_copy(ident_b[:], ident)
            ve.tensor_copy(never[:], cst[:, 4 * P:5 * P])
            split_lo(At(0, 0, 0))
            apply_norm(0, "mix0")
            split_lo(At(0, 0, 1))

            ve.wait_ge(unit_done, 1)
            ve.tensor_scalar(halves(dtx[:]), gp[0][0:16, :, 0:H2], pcol("ssd_dtb", rows=16), None,
                             ALU.add).then_inc(pair_free[0], 1)
            ve.wait_ge(dtl_done, 1)
            ch.link(ve.scalar_tensor_tensor(dtx[:], dtx[:], 0.0, dtl[:], ALU.max, ALU.add))
            ve.wait_ge(aexp_done, 1)
            ch.link(ve.tensor_scalar(dtl[:], dtx[:], aexp[:, 0:1], -1.0, ALU.mult, ALU.mult))
            ve.tensor_tensor_scan(csr[:], one_row[:], dtl[:], 0.0, ALU.mult, ALU.add).then_inc(cs_done, 1)

            def ssd_conv(g, c):
                t = At(6, g, T_SSD + c)
                ve.wait_ge(pair_free[t.par], t.half + 1)
                ct = 2 * g + c if c < 2 else (8 + g if c == 2 else 12 + g)
                wait_count(ve, txs_done if c < 2 else cb_done, g)
                conv(xcv[:, c, :], ub[c % 2], 4, lambda k: pcol("ssd_cw", 4 * ct + k), pcol("ssd_cb", ct),
                     ch.link, conv_done)

            def bc4(ap, n):
                return ap.unsqueeze(3).to_broadcast([n, ap.shape[1], HPG, HEAD])

            def heads(ap):
                return ap.rearrange("p i (h d) -> p i h d", h=HPG)

            def ssd_small(g, step):
                if step == 1:
                    for h in range(2):
                        args(g, h)
                    ve.wait_ge(xstok_done, g + 1)
                    wait_count(ve, y_done, HPG * g)
                    dts = dt_tok[:, :, bass.ds(HPG * g, HPG)]
                    ve.tensor_tensor(heads(x_dt[:, 0:4, :]), heads(xs_tok[:, 0:4, :]), bc4(dts[:, 0:4, :], P), ALU.mult)
                    ch.link(ve.tensor_tensor(heads(x_dt[0:SZ[4], 4:5, :]), heads(xs_tok[0:SZ[4], 4:5, :]),
                                             bc4(dts[0:SZ[4], 4:5, :], SZ[4]), ALU.mult))
                    skip = pcol("ssd_d", HPG * g, HPG).unsqueeze(1).to_broadcast([P, 4, HPG])
                    ve.tensor_tensor(heads(xs_tok[:, 0:4, :]), heads(xs_tok[:, 0:4, :]), bc4(skip, P), ALU.mult)
                    ch.link(ve.tensor_tensor(heads(xs_tok[0:SZ[4], 4:5, :]), heads(xs_tok[0:SZ[4], 4:5, :]),
                                             bc4(skip[0:SZ[4], 0:1, :], SZ[4]), ALU.mult))
                if step in (3, 4):
                    if step == 4:
                        for h in range(2):
                            take(g, h)
                            args(g, h + 2)
                    for h in ((0, 1) if step == 3 else (2, 3)):
                        ve.wait_ge(es_done, HPG * g + h + 1)
                        ve.wait_ge(cbs_done, g + 1)
                        e = dec[h % 2]
                        ve.tensor_tensor(e[:, 0:FULL], e[:, 0:FULL], cbs[:, 0:FULL], ALU.mult)
                        ve.tensor_tensor(e[0:SZ[4], FULL:CAUSAL], e[0:SZ[4], FULL:CAUSAL], cbs[0:SZ[4], FULL:CAUSAL],
                                         ALU.mult).then_inc(m_done, 1)
                if step == 5:
                    take(g, 2)
                    take(g, 3)
                    ve.wait_ge(ytok_done, HPG * (g + 1))
                    ve.wait_ge(ztok_done, g + 1)
                    ve.tensor_tensor(y_tok[:, 0:4, :], y_tok[:, 0:4, :], z_tok[:, 0:4, :], ALU.mult)
                    ve.tensor_tensor(y_tok[0:SZ[4], 4, :], y_tok[0:SZ[4], 4, :], z_tok[0:SZ[4], 4, :],
                                     ALU.mult).then_inc(yz_done, 1)
                    ve.wait_ge(yrs_done, g + 1)
                    for i in range(NT):
                        ins = ve.tensor_scalar(y_tok[0:SZ[i], i, :], y_tok[0:SZ[i], i, :], rs_tok[0:SZ[i], i:i + 1],
                                               None, ALU.mult)
                    ins.then_inc(yn_done, 1)

            def args(g, h):
                if h == 0:
                    ve.wait_ge(bc_in, 16 * (g + 1))
                wait_count(ve, y_done, HPG * g + h - 1)
                for j in range(NT):
                    ins = ve.tensor_scalar(dec[h % 2][0:SZ[j], OFF[j]:OFF[j] + WJ[j]], cs_bc[0:SZ[j], h, P * j:T],
                                           ncs_tok[0:SZ[j], j, bass.ds(HPG * g + h, 1)], 0.0, ALU.add, ALU.min)
                ins.then_inc(arg_done, 1)

            def take(g, h):
                ve.wait_ge(y_done, HPG * g + h + 1)
                if h == 0:
                    wait_count(ve, tout_done, g)
                c = slice(HEAD * h, HEAD * (h + 1))
                ve.tensor_tensor(y_tok[:, 0:4, c], sp_[:, h, 0:256].rearrange("p (i d) -> p i d", d=HEAD),
                                 xs_tok[:, 0:4, c], ALU.add)
                ve.tensor_tensor(y_tok[0:SZ[4], 4, c], sp_[0:SZ[4], h, 256:320], xs_tok[0:SZ[4], 4, c],
                                 ALU.add).then_inc(ytok_done, 1)

            split_lo(At(6, 0, W_SSD + 1))
            ve.wait_ge(dtT_done, 1)
            for n, (dst, sign) in enumerate(((dt_tok, 1.0), (ncs_tok, -1.0))):
                ve.tensor_scalar(dst[:, 0:4, :], sp_[:, 2, 80 * n:80 * n + 64].rearrange("p (i h) -> p i h", h=16),
                                 sign, None, ALU.mult)
                ins = ve.tensor_scalar(dst[0:SZ[4], 4, :], sp_[0:SZ[4], 2, 80 * n + 64:80 * n + 80], sign, None,
                                       ALU.mult)
            ins.then_inc(dtok_done, 1)
            for c in range(5):
                split_lo(At(6, 0, W_SSD + c + 2))
                if c < 4:
                    ssd_conv(0, c)

            def ssd_stage(g):
                for c in range(6):
                    split_lo(At(6, g, W_SSD + c + 1))
                    if 1 <= c <= 4:
                        ssd_conv(g, c - 1)
                    ssd_small(g - 1, c)

            ve.wait_ge(dtok_done, 1)
            ssd_stage(1)
            with ve.Fori(2, SSD_GROUPS) as g:
                ch.enter(g, 2, 14)
                ssd_stage(g)
            ch.leave(2, SSD_GROUPS)
            for c in range(6):
                ssd_small(SSD_GROUPS - 1, c)

            ve.wait_ge(yout_done, SSD_GROUPS)
            ve.memset(ret_nh[:], -0.5).then_inc(prep_done, 1)

            def rotate(r, dst, src, last_tile, link):
                t = At(8, r, T_RET + last_tile)
                ve.wait_ge(pair_free[t.par], t.half + 1)
                wait_count(ve, sc_done, r)
                cos, sin = rope[:, 0, :], rope[:, 1, :]
                ve.tensor_tensor(rt[:], src[:, 1, :], sin, ALU.mult)
                link(ve.tensor_tensor(dst[:, 0, :], src[:, 0, :], cos, ALU.mult))
                link(ve.tensor_tensor(dst[:, 0, :], dst[:, 0, :], rt[:], ALU.subtract))
                ve.tensor_tensor(rt[:], src[:, 1, :], cos, ALU.mult)
                link(ve.tensor_tensor(dst[:, 1, :], src[:, 0, :], sin, ALU.mult))
                ve.tensor_tensor(dst[:, 1, :], dst[:, 1, :], rt[:], ALU.add).then_inc(rot_done, 1)

            def ret_small(r, step):
                if step == 2:
                    ve.wait_ge(sc_done, r + 1)
                    wait_count(ve, o_done, r)
                    for j, q0, n, b, c0, at in PIECES:
                        d0 = q0 - P * j
                        ins = ve.tensor_tensor(sdec[0:SZ[j], at:at + n], sp_[0:SZ[j], b, c0:c0 + n],
                                               rdec[0:SZ[j], r, d0:d0 + n], ALU.mult)
                    ins.then_inc(sdec_done, 1)
                if step == 4:
                    ve.wait_ge(o_done, r + 1)
                    wait_count(ve, tro_done, r)
                    for i in range(NT):
                        ins = ve.bn_stats(stats[0:SZ[i], i, :], sp_[0:SZ[i], i // 2, (i % 2) * 256:(i % 2) * 256 + 256])
                    ch.link(ins)
                    ve.tensor_copy(idle_v[:], eps_col[:])
                    for i in range(NT):
                        ins = ve.bn_aggr(mv[0:SZ[i], i, :], stats[0:SZ[i], i, :])
                    ins.then_inc(mv_done, 1)
                    ve.wait_ge(rrs_done, r + 1)
                    for i in range(NT):
                        ins = ve.tensor_scalar(o_tok[0:SZ[i], i, :], sp_[0:SZ[i], i // 2, (i % 2) * 256:(i % 2) * 256 + 256],
                                               mv[0:SZ[i], i, 0:1], ret_rs[0:SZ[i], i:i + 1], ALU.subtract, ALU.mult)
                    ins.then_inc(on_done, 1)
                if step == 6:
                    t = At(8, r, T_RET + 7)
                    ve.wait_ge(pair_free[t.par], t.half + 1)
                    ve.wait_ge(tro_done, r + 1)
                    for c in range(2):
                        gain = pcol("ret_norm", 2 * r + c)
                        ve.scalar_tensor_tensor(yT[:, 8 + 2 * r + c, 0:512], sp_[:, 2 * c, :], gain, gr[:, c, 0:512],
                                                ALU.mult, ALU.mult)
                        ins = ve.scalar_tensor_tensor(yT[:, 8 + 2 * r + c, 512:T], sp_[:, 2 * c + 1, 0:16], gain,
                                                      gr[:, c, 512:T], ALU.mult, ALU.mult)
                    ins.then_inc(yret_done, 1)

            def ret_stage(r):
                for c in range(8):
                    split_lo(At(8, r, W_RET + c + 1))
                    if c == 2:
                        rotate(r, rq, qr, 1, ch.link)
                    if c == 4:
                        rotate(r, rk, kr, 3, ch.link)
                    ret_small(r - 1, c)

            ve.wait_ge(tab_in, 32)
            for c in range(8):
                split_lo(At(8, 0, W_RET + c + 1))
                if c == 2:
                    rotate(0, rq, qr, 1, ch.link)
                if c == 4:
                    rotate(0, rk, kr, 3, ch.link)
            ret_stage(1)
            with ve.Fori(2, RET_HEADS) as r:
                ch.enter(r, 2, 7)
                ret_stage(r)
            ch.leave(2, RET_HEADS)
            for c in (2, 4, 6):
                ret_small(RET_HEADS - 1, c)

            def project(wb, tb, kt, yb=None, following=True):
                if yb is not None:
                    for k in range(16):
                        ve.wait_ge(yhi_done, yb + k + 1)
                        ve.tensor_tensor(y_lo[:, k, :], yT[:, k, :], y_hi[:, k, :].bitcast(f32),
                                         ALU.subtract).then_inc(ylo_done, 1)
                        if k == 7:
                            split_lo(At(0, 0, wb + 1), kt)
                else:
                    split_lo(At(0, 0, wb + 1), kt)

                def tile(i, s, m, last=False):
                    if following or not last:
                        split_lo(At(4, i, wb + 2 * s + 2), KD if last else kt)
                    if not last:
                        split_lo(At(4, i, wb + 2 * s + 3), kt)
                    ve.wait_ge(unit_done, At(4, i, wb + 2 * s + 2).v)
                    t = At(2, i, tb + s)
                    ve.tensor_tensor(halves(hT[:, m, :]), gout(t.par), halves(hT[:, m, :]), ALU.add)\
                      .then_inc(pair_free[t.par], 1)

                for s in range(2):
                    tile(0, s, s)
                with ve.Fori(1, KD // 2 - 1) as i:
                    for s in range(2):
                        tile(i, s, 2 * i + s)
                tile(KD // 2 - 1, 0, KD - 2)
                tile(KD // 2 - 1, 1, KD - 1, last=True)

            def ffn_in(wb, tb, L):
                def f_conv(i, half, dst, done):
                    t = At(2, i, tb + half)
                    ve.wait_ge(pair_free[t.par], t.half + 1)
                    ct = i + KF * half
                    conv(dst[:], ubf[half], 3, lambda k: pcol(f"f{L}_cw", 3 * ct + k), pcol(f"f{L}_cb", ct),
                         ch.link, done)

                def slot_a(i):
                    f_conv(i - 1, 1, cu, cu_done)
                    ve.wait_ge(cu_done, KF * L + i)
                    ve.wait_ge(sg_done, KF * L + i)
                    ve.tensor_tensor(hidf[:], cg[:], cu[:], ALU.mult).then_inc(hidf_done, 1)

                def lo(i):
                    ve.wait_ge(hhi_done, KF * L + i)
                    ve.tensor_tensor(hid_lo[:, i - 1, :], hidf[:], hid_hi[:, i - 1, :].bitcast(f32),
                                     ALU.subtract).then_inc(hlo_done, 1)

                ve.wait_ge(unit_done, wb)
                for s in range(2):
                    ins = ve.memset(ubf[s][:, 0:2], 0.0)
                ch.link(ins)
                split_lo(At(2, 0, wb + 1))
                split_lo(At(2, 0, wb + 2))
                f_conv(0, 0, cg, cg_done)

                def pair(i, kt=KD):
                    split_lo(At(2, i, wb + 1))
                    slot_a(i)
                    split_lo(At(2, i, wb + 2), kt)
                    f_conv(i, 0, cg, cg_done)
                    lo(i)

                pair(1)
                with ve.Fori(2, KF - 1) as i:
                    ch.enter(i, 2, 4)
                    pair(i)
                ch.leave(2, KF - 1)
                pair(KF - 1, KH)
                slot_a(KF)
                lo(KF)

            project(W_OUT0, T_OUT0, KD, yb=0)
            apply_norm(1, "ffn0")
            ffn_in(W_FI0, T_FI0, 0)
            project(W_FO0, T_FO0, KH)
            apply_norm(2, "mix1")

            ch.link(ve.memset(ubx[:, 0:3], 0.0))
            ve.tensor_scalar(hb[:, 0, :], pcol("lru_ba", 0, 8), 0.5, None, ALU.mult)
            ve.tensor_scalar(hb[:, 1, :], pcol("lru_bx", 0, 8), 0.5, None, ALU.mult)
            ve.tensor_scalar(nsp[:], pcol("lru_lam", 0, 8), -1.0, 0.0, ALU.mult, ALU.max).then_inc(spl_done, 1)
            ve.wait_ge(spl_ln, 1)
            ve.wait_ge(spl_done, 1)
            ch.link(ve.tensor_tensor(nsp[:], nsp[:], nspt[:], ALU.add))
            ve.tensor_scalar(nsp[:], nsp[:], -0.5 * LRU_C, None, ALU.mult).then_inc(spl_done, 1)

            def soft(n, e):
                ve.wait_ge(l_done, 2 * n + e + 1)
                wait_count(ve, suf_done, 2 * n + e)
                for b, w, at in BANKS:
                    ve.scalar_tensor_tensor(spb[:, at:at + w], sp_[:, b, 0:w], 0.0, lbuf[:, at:at + w], ALU.max, ALU.add)
                ve.scalar_tensor_tensor(spb[0:SZ[4], FULL:CAUSAL], sp_[0:SZ[4], 2, 416:432], 0.0,
                                        lbuf[0:SZ[4], FULL:CAUSAL], ALU.max, ALU.add).then_inc(spf_done, 1)

            def take_head(n, e):
                ve.wait_ge(pv_done, 2 * n + e + 1)
                if e == 0:
                    wait_count(ve, tso_done, n)
                c = slice(HEAD * e, HEAD * (e + 1))
                ve.tensor_copy(so_tok[:, 0:4, c], sp_[:, 3, 0:256].rearrange("p (i d) -> p i d", d=HEAD))
                ve.tensor_copy(so_tok[0:SZ[4], 4, c], sp_[0:SZ[4], 3, 256:320]).then_inc(so_done, 1)

            def l1_small(i, b, step):
                n = 2 * i + b
                if step == 0:
                    t = At(10, i, T_L1 + 5 * b + 4)
                    ve.wait_ge(pair_free[t.par], t.half + 1)
                    wait_count(ve, gates_done, n)
                    conv(xc[:], ubx, 4, lambda k: pcol("lru_cw", 4 * n + k), pcol("lru_cb", n), ch.link, xc_done)
                    t = At(10, i, T_L1 + 5 * b + 3)
                    ve.wait_ge(pair_free[t.par], t.half + 1)
                    ch.link(ve.tensor_tensor(ge[:], gt[:], gt[:], ALU.mult))
                    ch.link(ve.tensor_scalar(ge[:], ge[:], 0.044715, 1.0, ALU.mult, ALU.add))
                    ve.tensor_tensor(ge[:], ge[:], gt[:], ALU.mult).then_inc(gu_done, 1)
                if step == 1:
                    ve.wait_ge(la_done, n + 1)
                    ve.scalar_tensor_tensor(ti[:], ti[:], 1.0, xc[:], ALU.add, ALU.mult)
                    ch.link(ve.tensor_scalar(lb[:], lt[:], -1.0, 1.0, ALU.mult, ALU.add))
                    ch.link(ve.reciprocal(lb[:], lb[:]))
                    ch.link(ve.scalar_tensor_tensor(lb[:], lt[:], -2.0, lb[:], ALU.mult, ALU.mult))
                    ve.tensor_scalar(lb[:], lb[:], 0.0, None, ALU.max).then_inc(lb_done, 1)
                if step == 2:
                    ve.wait_ge(root1_done, n + 1)
                    ch.link(ve.tensor_tensor(lb[:], lb[:], ti[:], ALU.mult))
                    ch.link(ve.tensor_tensor_scan(tr[:], la[:], lb[:], 0.0, ALU.mult, ALU.add))
                    ve.wait_ge(gth_done, n + 1)
                    ch.link(ve.scalar_tensor_tensor(ge[:], ge[:], 1.0, gt[:], ALU.add, ALU.mult))
                    ve.scalar_tensor_tensor(yT[:, 8 + n, :], ge[:], 0.5, tr[:], ALU.mult, ALU.mult).then_inc(ylru_done, 1)
                    soft(n, 0)
                if step == 4:
                    take_head(n, 0)
                    soft(n, 1)
                if step == 5:
                    take_head(n, 1)

            split_lo(At(10, 0, W_L1 + 1))
            for c in range(1, 5):
                split_lo(At(10, 0, W_L1 + c + 1))

            def l1_pair(i):
                for b in range(2):
                    for c in range(5):
                        split_lo(At(10, i, W_L1 + 5 * (b + 1) + c + 1))
                        l1_small(i, b, c)
                    l1_small(i, b, 5)

            l1_pair(0)
            with ve.Fori(1, 3) as i:
                ch.enter(i, 1, 22)
                l1_pair(i)
            ch.leave(1, 3)
            for c in range(5):
                split_lo(At(10, 3, W_L1 + 5 + c + 1))
                l1_small(3, 0, c)
            l1_small(3, 0, 5)
            for c in range(6):
                l1_small(3, 1, c)
            project(W_OUT1, T_OUT1, KD, yb=16)
            apply_norm(3, "ffn1")
            ffn_in(W_FI1, T_FI1, 1)
            project(W_FO1, T_FO1, KH, following=False)
            apply_norm(4, "final", parts=False)

        @block.gpsimd
        def _(po):
            ch = Chain(po, g_seq)

            def await_count(sem_, n, k=0):
                po.wait_ge(sem_, n)
                po.tensor_tensor(idle_g[:, k:k + 1], eps_col[:], eps_col[:], ALU.mult)

            def mask(buf, done):
                for j in range(NT):
                    blk = buf[0:SZ[j], OFF[j]:OFF[j] + SZ[j]]
                    ins = po.affine_select(out=blk, in_=blk, compare_op=ALU.is_ge, fill=0.0, base=0,
                                           pattern=[[1, SZ[j]]], channel_multiplier=-1)
                ins.then_inc(done, 1)

            po.wait_ge(prep_done, 1)
            with po.Fori(0, SSD_GROUPS) as g:
                ch.enter(g, 0, 1)
                for h in range(HPG):
                    await_count(e_done, HPG * g + h + 1, h)
                    mask(dec[h % 2], es_done)
                await_count(ysq_done, g + 1, 4)
                po.tensor_scalar(rs_tok[:, 0:4], ssq_tok[:, 0:4], 1.0 / 256, EPS, ALU.mult, ALU.add)
                ch.link(po.tensor_scalar(rs_tok[0:SZ[4], 4:5], ssq_tok[0:SZ[4], 4:5], 1.0 / 256, EPS, ALU.mult, ALU.add))
                po.tensor_tensor(rs_tok[:, 0:4], rs_tok[:, 0:4], neg_half[:, 0:4], ALU.pow)
                po.tensor_tensor(rs_tok[0:SZ[4], 4:5], rs_tok[0:SZ[4], 4:5], neg_half[0:SZ[4], 4:5],
                                 ALU.pow).then_inc(yrs_done, 1)
            ch.leave(0, SSD_GROUPS)
            po.wait_ge(prep_done, 2)
            with po.Fori(0, RET_HEADS) as r:
                ch.enter(r, 0, 1)
                await_count(mv_done, r + 1, 5)
                po.tensor_scalar(ret_rs[:, 0:4], mv[:, 0:4, 1], 1.0, EPS, ALU.mult, ALU.add)
                ch.link(po.tensor_scalar(ret_rs[0:SZ[4], 4:5], mv[0:SZ[4], 4:5, 1], 1.0, EPS, ALU.mult, ALU.add))
                po.tensor_tensor(ret_rs[:, 0:4], ret_rs[:, 0:4], ret_nh[:, 0:4], ALU.pow)
                po.tensor_tensor(ret_rs[0:SZ[4], 4:5], ret_rs[0:SZ[4], 4:5], ret_nh[0:SZ[4], 4:5],
                                 ALU.pow).then_inc(rrs_done, 1)
            ch.leave(0, RET_HEADS)


def kernel(**inputs):
    import numpy as np
    import concourse.bacc as bacc
    from concourse.bass_utils import run_bass_kernel_spmd as run

    a = {k: np.asarray(v) for k, v in inputs.items()}

    def units(w, cols, kts):
        res = []
        for c in cols:
            k0 = 0
            for kt in kts:
                blk = w[k0 * P:(k0 + kt) * P, c:c + P]
                res.append(blk.reshape(kt, P, P).transpose(1, 0, 2).reshape(P, kt * P))
                k0 += kt
        return np.ascontiguousarray(np.stack(res))

    def per_channel(v):
        v = v.reshape(-1, v.shape[-1])
        return v.reshape(v.shape[0], -1, P).transpose(2, 1, 0).reshape(P, -1)

    def rows(v):
        res = np.zeros((P, 1), np.float32)
        res[:v.size, 0] = v
        return res

    h = np.concatenate([a["meta_tokens"], a["x"][0]], 0)
    x_h = np.ascontiguousarray(h.reshape(T, KD, P).transpose(2, 1, 0))
    parts = {"mix0": per_channel(a["l0_mix_norm"]), "ffn0": per_channel(a["l0_ffn_norm"]),
             "mix1": per_channel(a["l1_mix_norm"]), "ffn1": per_channel(a["l1_ffn_norm"]),
             "final": per_channel(a["final_norm"]), "ssd_cw": per_channel(a["l0_ssd_conv_w"]),
             "ssd_cb": per_channel(a["l0_ssd_conv_b"]), "ssd_norm": per_channel(a["l0_ssd_norm"]),
             "ret_norm": per_channel(a["l0_ret_norm"]),
             "f0_cw": per_channel(a["l0_ffn_conv_w"]), "f0_cb": per_channel(a["l0_ffn_conv_b"]),
             "f1_cw": per_channel(a["l1_ffn_conv_w"]), "f1_cb": per_channel(a["l1_ffn_conv_b"]),
             "lru_cw": per_channel(a["l1_lru_conv_w"]), "lru_cb": per_channel(a["l1_lru_conv_b"]),
             "lru_ba": per_channel(a["l1_lru_ba"]), "lru_bx": per_channel(a["l1_lru_bx"]),
             "lru_lam": per_channel(a["l1_lru_lambda"]), "ssd_d": np.tile(a["l0_ssd_d"][None], (P, 1)),
             "ssd_dtb": rows(a["l0_ssd_dt_bias"]), "ssd_alog": rows(a["l0_ssd_a_log"])}
    vec_h = np.ascontiguousarray(np.concatenate([parts[n] for n in COLS], 1))

    f = np.float32
    half = P
    inv = (1.0 / (f(10000.0) ** (np.arange(half, dtype=f) / f(half - 1)))).astype(f)
    ang = (np.arange(T, dtype=f)[None, :] * inv[:, None]).astype(f)
    tri = (np.arange(P)[:, None] >= np.arange(P)[None, :]).astype(f)
    cst_h = np.concatenate([np.eye(P, dtype=f), np.ones((P, P), f), -tri, -np.ones((P, P), f), -1e30 * tri, np.cos(ang),
                            np.sin(ang)],
                           1).astype(f)
    log_gamma = np.log1p(-np.exp2(-5.0 - np.arange(RET_HEADS)))
    diff = np.arange(T)[None, :] - np.arange(P)[:, None]
    dec_h = np.where(diff[:, None, :] >= 0, np.exp(log_gamma[None, :, None] * np.maximum(diff, 0)[:, None, :]), 0.0)
    dec_h = (dec_h / 16.0).astype(f)

    w = a["l0_w_in"]
    z0, x0, b0, c0 = 0, 1024, 2048, 2560
    dt0, q0 = 3072, 3088
    ssd_cols = [c for g in range(SSD_GROUPS) for c in (x0 + 256 * g, x0 + 256 * g + P, b0 + P * g, c0 + P * g,
                                                       z0 + 256 * g, z0 + 256 * g + P)]
    ret_cols = [q0 + 1024 * n + 256 * r + P * d for r in range(RET_HEADS) for n in range(4) for d in range(2)]
    l1_cols = [1024 * n + P * i for i in range(8) for n in range(5)]
    fi_cols = [FFN * n + P * i for i in range(KF) for n in range(2)]
    oc = [P * m for m in range(KD)]
    gate = np.ascontiguousarray(np.concatenate([a["l1_lru_wa"], a["l1_lru_wx"]], 2))
    arrays = [x_h, vec_h, cst_h, dec_h, units(w, [dt0], [KD]), units(w, ssd_cols, [KD]), units(w, ret_cols, [KD]),
              units(a["l0_w_out"], oc, [KD, KD]), units(a["l0_ffn_w_in"], fi_cols, [KD]),
              units(a["l0_ffn_w_out"], oc, [KH, KH]), units(a["l1_w_in"], l1_cols, [KD]),
              units(a["l1_w_out"], oc, [KD, KD]), units(a["l1_ffn_w_in"], fi_cols, [KD]),
              units(a["l1_ffn_w_out"], oc, [KH, KH]), gate]
    nc = bacc.Bacc("TRN2", target_bir_lowering=False, num_devices=1)
    named = {f"in_{n}": v for n, v in enumerate(arrays)}
    aps = [nc.dram_tensor(k, v.shape, mybir.dt.from_np(v.dtype), kind="ExternalInput").ap() for k, v in named.items()]
    out = nc.dram_tensor("out", (P, KD, SEQ), mybir.dt.float32, kind="ExternalOutput").ap()
    build(nc, *aps, out)
    r = run(nc, [named], core_ids=[0])
    got = r.results[0]["out"]
    return np.ascontiguousarray(got.transpose(2, 1, 0).reshape(1, SEQ, D_MODEL))
```

```python
import concourse.bass as bass
from concourse import mybir
from contextlib import ExitStack

P = 128
D_MODEL, SEQ, N_META = 1024, 512, 16
T = SEQ + N_META
H2 = T // 2
KD = D_MODEL // P
EPS = 1e-6
SSD_HEADS, SSD_GROUPS, HEAD = 16, 4, 64
HPG = SSD_HEADS // SSD_GROUPS
RET_HEADS = 4
SB_SCALE = HEAD ** -0.5
LRU_C = 8.0
GELU_C = (2.0 / 3.141592653589793) ** 0.5
FFN = 2816
KF = FFN // P
KH = KF // 2
NT = 5
SZ = [P, P, P, P, T - 4 * P]
WJ = [T - P * j for j in range(NT)]
OFF = [sum(WJ[:j]) for j in range(NT)]
CAUSAL = sum(WJ)
FULL = OFF[4]
PIECES = [(0, 0, 512, 0, 0, 0), (0, 512, 16, 1, 0, 512), (1, 128, 400, 1, 16, 528),
          (2, 256, 272, 2, 0, 928), (3, 384, 144, 2, 272, 1200), (4, 512, 16, 2, 416, 1344)]
BANKS = [(0, 512, 0), (1, 416, 512), (2, 416, 928)]

V_LAST = ((1, 416), (2, 432))

COLS = {}
_n = 0
for _name, _k in [("mix0", KD), ("ffn0", KD), ("mix1", KD), ("ffn1", KD), ("final", KD),
                  ("ssd_cw", 64), ("ssd_cb", 16), ("ssd_norm", 8), ("ret_norm", 8),
                  ("f0_cw", 3 * 2 * KF), ("f0_cb", 2 * KF), ("f1_cw", 3 * 2 * KF), ("f1_cb", 2 * KF),
                  ("lru_cw", 32), ("lru_cb", 8), ("lru_ba", 8), ("lru_bx", 8), ("lru_lam", 8),
                  ("ssd_d", 16), ("ssd_dtb", 1), ("ssd_alog", 1)]:
    COLS[_name] = _n
    _n += _k
NCOL = _n
NORMS = ("mix0", "ffn0", "mix1", "ffn1", "final")

W_DT, W_SSD, W_RET, W_OUT0, W_FI0, W_FO0 = 0, 1, 25, 57, 73, 117
W_L1, W_OUT1, W_FI1, W_FO1, W_END = 133, 173, 189, 233, 249
T_DT, T_SSD, T_RET, T_OUT0, T_FI0, T_FO0 = 0, 1, 25, 57, 65, 109
T_L1, T_OUT1, T_FI1, T_FO1 = 117, 157, 165, 209


class At:

    def __init__(self, a, i, c):
        self.a, self.i, self.c = a, i, c
        self.v = a * i + c
        self.par = c % 2
        self.half = (a // 2) * i + c // 2

    def plus(self, d):
        return At(self.a, self.i, self.c + d)


def wait_count(eng, sem, n):
    if isinstance(n, int) and n <= 0:
        return
    eng.wait_ge(sem, n)


class Chain:

    def __init__(self, eng, sem):
        self.eng, self.sem, self.base, self.n = eng, sem, 0, 0

    def link(self, ins):
        ins.then_inc(self.sem, 1)
        self.n += 1
        self.eng.wait_ge(self.sem, self.base + self.n)

    def enter(self, i, lo, per):
        self.saved, self.per = self.base + self.n, per
        self.base, self.n = self.saved + per * (i - lo), 0

    def leave(self, lo, hi):
        assert self.n == self.per, f"{self.n} links in the loop's body, not {self.per}"
        self.base, self.n = self.saved + self.per * (hi - lo), 0


def build(nc, x_h, vec_h, cst_h, dec_h, w_dt, w_ssd, w_ret, w_out0, w_fi0, w_fo0, w_l1, w_out1, w_fi1, w_fo1,
          w_gate, out):
    f32, f32r = mybir.dt.float32, mybir.dt.float32r
    ALU, ACT = mybir.AluOpType, mybir.ActivationFunctionType
    ctx = ExitStack()
    with ctx:
        def sb(name, shape, dt=f32, where=ctx):
            return where.enter_context(nc.sbuf_tensor(name, shape, dt))

        def sem(name):
            return ctx.enter_context(nc.semaphore(name))

        hT = sb("hT", [P, KD, T])
        hn_hi = sb("hn_hi", [P, KD, T], f32r)
        hn_lo = sb("hn_lo", [P, KD, T], f32r)
        raw = [sb(f"raw{s}", [P, KH * P]) for s in range(2)]
        whi = [sb(f"whi{s}", [P, KH * P], f32r) for s in range(2)]
        wlo = [sb(f"wlo{s}", [P, KH * P], f32r) for s in range(2)]
        vec = sb("vec", [P, NCOL])
        cst = sb("cst", [P, 5 * P])
        ident_b = sb("ident_b", [P, P], mybir.dt.bfloat16)
        never = sb("never", [P, P], mybir.dt.bfloat16)
        neg_r = sb("neg_r", [P, 2, P], f32r)
        ident, ones = cst[:, 0:P], cst[:, P:2 * P]
        sq = [sb(f"sq{s}", [P, T]) for s in range(2)]
        acc = sb("acc", [P, T])
        rstd = sb("rstd", [P, T])
        eps_col = sb("eps_col", [P, 1])
        idle_g, idle_v, idle_a = (sb(n, [P, 6]) for n in ("idle_g", "idle_v", "idle_a"))

        def scope():
            return ExitStack()

        with scope() as mix:
            yT = sb("yT", [P, 16, T], f32, mix)
            with scope() as s1:
                ub = [sb(f"ub{s}", [P, 3 + T], f32, s1) for s in range(2)]
                xcv = sb("xcv", [P, 4, T], f32, s1)
                zc = sb("zc", [P, 2, T], f32, s1)
                xs_tok = sb("xs_tok", [P, NT, 256], f32, s1)
                x_dt = sb("x_dt", [P, NT, 256], f32, s1)
                z_tok = sb("z_tok", [P, NT, 256], f32, s1)
                y_tok = sb("y_tok", [P, NT, 256], f32, s1)
                cbs = sb("cbs", [P, CAUSAL], f32, s1)
                dec = [sb(f"dec{s}", [P, CAUSAL], f32, s1) for s in range(2)]
                cs_bc = sb("cs_bc", [P, HPG, T], f32, s1)
                dt_tok = sb("dt_tok", [P, NT, SSD_HEADS], f32, s1)
                ncs_tok = sb("ncs_tok", [P, NT, SSD_HEADS], f32, s1)
                dtx = sb("dtx", [SSD_HEADS, T], f32, s1)
                dtl = sb("dtl", [SSD_HEADS, T], f32, s1)
                csr = sb("csr", [SSD_HEADS, T], f32, s1)
                one_row = sb("one_row", [SSD_HEADS, T], f32, s1)
                aexp = sb("aexp", [SSD_HEADS, 1], f32, s1)
                ssq_tok = sb("ssq_tok", [P, NT], f32, s1)
                rs_tok = sb("rs_tok", [P, NT], f32, s1)
                neg_half = sb("neg_half", [P, NT], f32, s1)
            with scope() as s2:
                rope = sb("rope", [P, 2, T], f32, s2)
                rdec = sb("rdec", [P, RET_HEADS, T], f32, s2)
                qr = sb("qr", [P, 2, T], f32, s2)
                kr = sb("kr", [P, 2, T], f32, s2)
                rq = sb("rq", [P, 2, T], f32, s2)
                rk = sb("rk", [P, 2, T], f32, s2)
                vr = sb("vr", [P, 2, T], f32, s2)
                gr = sb("gr", [P, 2, T], f32, s2)
                rt = sb("rt", [P, T], f32, s2)
                v_tok = sb("v_tok", [P, NT, 256], f32, s2)
                sdec = sb("sdec", [P, CAUSAL], f32, s2)
                o_tok = sb("o_tok", [P, NT, 256], f32, s2)
                stats = sb("stats", [P, NT, 6], f32, s2)
                mv = sb("mv", [P, NT, 2], f32, s2)
                ret_rs = sb("ret_rs", [P, NT], f32, s2)
                ret_nh = sb("ret_nh", [P, NT], f32, s2)
            with scope() as s3:
                qs = [sb(f"qs{s}", [P, T], f32, s3) for s in range(2)]
                ks = [sb(f"ks{s}", [P, T], f32, s3) for s in range(2)]
                vs = sb("vs", [P, T], f32, s3)
                gt = sb("gt", [P, T], f32, s3)
                ubx = sb("ubx", [P, 3 + T], f32, s3)
                xc = sb("xc", [P, T], f32, s3)
                gw = [sb(f"gw{s}", [P, 2 * P], f32, s3) for s in range(2)]
                sv_tok = sb("sv_tok", [P, NT, P], f32, s3)
                so_tok = sb("so_tok", [P, NT, P], f32, s3)
                lbuf = sb("lbuf", [P, CAUSAL], f32, s3)
                spb = sb("spb", [P, CAUSAL], f32, s3)
                sp_hi = sb("sp_hi", [P, CAUSAL], f32r, s3)
                sp_lo = sb("sp_lo", [P, CAUSAL], f32r, s3)
                wts = [sb(f"wts{s}", [P, CAUSAL], f32, s3) for s in range(2)]
                tr, ti, la, lt, lb, ge = (sb(n, [P, T], f32, s3) for n in ("tr", "ti", "la", "lt", "lb", "ge"))
                hb = sb("hb", [P, 2, 8], f32, s3)
                nsp = sb("nsp", [P, 8], f32, s3)
                nspt = sb("nspt", [P, 8], f32, s3)
            with scope() as s4:
                y_hi = sb("y_hi", [P, 16, T], f32r, s4)
                y_lo = sb("y_lo", [P, 16, T], f32r, s4)
        with scope() as ffn:
            hid_hi = sb("hid_hi", [P, KF, T], f32r, ffn)
            hid_lo = sb("hid_lo", [P, KF, T], f32r, ffn)
            ubf = [sb(f"ubf{s}", [P, 2 + T], f32, ffn) for s in range(2)]
            cg = sb("cg", [P, T], f32, ffn)
            cu = sb("cu", [P, T], f32, ffn)
            hidf = sb("hidf", [P, T], f32, ffn)

        gp = [ctx.enter_context(nc.psum_tensor(f"gp{s}", [P, 2, 512], f32)) for s in range(2)]
        sp_ = ctx.enter_context(nc.psum_tensor("small", [P, 4, 512], f32))

        def halves(ap):
            return ap.rearrange("p (h t) -> p h t", h=2)

        def gout(s):
            return gp[s][:, :, 0:H2]

        def pcol(name, c=0, n=1, rows=P):
            return vec[0:rows, bass.ds(COLS[name] + c, n)]

        cs_d = nc.dram_tensor("cs_scratch", [SSD_HEADS, T], f32, kind="Internal").ap()

        raw_in = [sem(f"raw_in{s}") for s in range(2)]
        hi_done, lo_done, unit_done = sem("hi_done"), sem("lo_done"), sem("unit_done")
        pair_free = [sem(f"pair_free{s}") for s in range(2)]
        vec_in, const_in = sem("vec_in"), sem("const_in")
        h_in = [sem(f"h_in{c}") for c in range(KD // 2)]
        sq_done, acc_done, ssq_done, root_done = (sem(n) for n in ("sq_done", "acc_done", "ssq_done", "root_done"))
        rstd_done, nhi_done, nlo_done = sem("rstd_done"), sem("nhi_done"), sem("nlo_done")
        v_seq, a_seq, g_seq = sem("v_seq"), sem("a_seq"), sem("g_seq")
        yhi_done, ylo_done = sem("yhi_done"), sem("ylo_done")
        cg_done, cu_done, sg_done = sem("cg_done"), sem("cu_done"), sem("sg_done")
        hidf_done, hhi_done, hlo_done = sem("hidf_done"), sem("hhi_done"), sem("hlo_done")
        final_done, out_done = sem("final_done"), sem("out_done")
        dtl_done, aexp_done, cs_done, cs_out = (sem(n) for n in ("dtl_done", "aexp_done", "cs_done", "cs_out"))
        dtx_done, dtT_done, dtok_done, bc_in = sem("dtx_done"), sem("dtT_done"), sem("dtok_done"), sem("bc_in")
        conv_done, silu_done, txs_done, xstok_done, xdt_done = (
            sem(n) for n in ("conv_done", "silu_done", "txs_done", "xstok_done", "xdt_done"))
        tz_done, ztok_done, cb_done, cbs_done = (sem(n) for n in ("tz_done", "ztok_done", "cb_done", "cbs_done"))
        arg_done, e_done, es_done, m_done, y_done, ytok_done = (
            sem(n) for n in ("arg_done", "e_done", "es_done", "m_done", "y_done", "ytok_done"))
        yz_done, ysq_done, yrs_done, yn_done, tout_done, yout_done = (
            sem(n) for n in ("yz_done", "ysq_done", "yrs_done", "yn_done", "tout_done", "yout_done"))
        tab_in, rot_done, tv_done, vtok_done, sc_done, sdec_done = (
            sem(n) for n in ("tab_in", "rot_done", "tv_done", "vtok_done", "sc_done", "sdec_done"))
        o_done, mv_done, rrs_done, on_done, tro_done, yret_done, gs_done = (
            sem(n) for n in ("o_done", "mv_done", "rrs_done", "on_done", "tro_done", "yret_done", "gs_done"))
        gw_in = [sem(f"gw_in{s}") for s in range(2)]
        xc_done, gates_done, tri_done, la_done, lb_done, root1_done = (
            sem(n) for n in ("xc_done", "gates_done", "tri_done", "la_done", "lb_done", "root1_done"))
        z_done, l_done, spf_done, suf_done, w_done, pv_done, so_done = (
            sem(n) for n in ("z_done", "l_done", "spf_done", "suf_done", "w_done", "pv_done", "so_done"))
        tvs_done, svtok_done, tso_done, ysb_done, gu_done, gth_done, ylru_done = (
            sem(n) for n in ("tvs_done", "svtok_done", "tso_done", "ysb_done", "gu_done", "gth_done", "ylru_done"))
        prep_done, spl_done, spl_ln = sem("prep_done"), sem("spl_done"), sem("spl_ln")

        block = ctx.enter_context(nc.Block())

        @block.sync
        def _(sp):
            def unit(w, src, kt=KD):
                wait_count(sp, lo_done, w.v - 1)
                sp.dma_start(raw[w.par][:, 0:kt * P], src).then_inc(raw_in[w.par], 16)

            sp.dma_start(vec[:], vec_h).then_inc(vec_in, 16)
            for c in range(KD // 2):
                sp.dma_start(hT[:, 2 * c:2 * c + 2, :], x_h[:, 2 * c:2 * c + 2, :]).then_inc(h_in[c], 16)
                if c == 0:
                    unit(At(0, 0, 0), w_dt[0])
            unit(At(0, 0, 1), w_ssd[0])
            for c in range(1, 6):
                unit(At(6, 0, W_SSD + c), w_ssd[c])
            with sp.Fori(1, SSD_GROUPS) as g:
                for c in range(6):
                    unit(At(6, g, W_SSD + c), w_ssd[6 * g + c])
            for c in range(2):
                unit(At(8, 0, W_RET + c), w_ret[c])
            sp.wait_ge(yout_done, SSD_GROUPS)
            sp.dma_start(rope[:], cst_h[:, 5 * P:5 * P + 2 * T].rearrange("p (a t) -> p a t", a=2)).then_inc(tab_in, 16)
            sp.dma_start(rdec[:], dec_h).then_inc(tab_in, 16)
            for c in range(2, 8):
                unit(At(8, 0, W_RET + c), w_ret[c])
            with sp.Fori(1, RET_HEADS) as r:
                for c in range(8):
                    unit(At(8, r, W_RET + c), w_ret[8 * r + c])

            def stream(base, n, src, kt=KD):
                with sp.Fori(0, n // 2) as i:
                    for s in range(2):
                        unit(At(2, i, base + s), src[2 * i + s], kt)

            stream(W_OUT0, 16, w_out0)
            stream(W_FI0, 2 * KF, w_fi0)
            stream(W_FO0, 16, w_fo0, KH)

            def l1_pair(i):
                for b in range(2):
                    for c in range(5):
                        if c == 4:
                            if isinstance(i, int):
                                sp.wait_ge(unit_done, W_L1)
                            else:
                                sp.wait_ge(gates_done, 2 * i + b - 1)
                            sp.dma_start(gw[b][:], w_gate[2 * i + b]).then_inc(gw_in[b], 16)
                        unit(At(10, i, W_L1 + 5 * b + c), w_l1[10 * i + 5 * b + c])

            l1_pair(0)
            with sp.Fori(1, 4) as i:
                l1_pair(i)
            stream(W_OUT1, 16, w_out1)
            stream(W_FI1, 2 * KF, w_fi1)
            stream(W_FO1, 16, w_fo1, KH)
            sp.wait_ge(final_done, KD)
            sp.dma_start(out, yT[:, 0:KD, N_META:T]).then_inc(out_done, 16)
            sp.wait_ge(out_done, 16)

        @block.tensor
        def _(pe):
            def gemm(w, t, rhs_hi, rhs_lo, k0=0, kt=KD, first=True, last=True, ready=None, after=None):
                pe.wait_ge(lo_done, w.v + 1)
                if first:
                    wait_count(pe, pair_free[t.par], t.half)
                for k in range(kt):
                    if ready is not None:
                        pe.wait_ge(ready[0], ready[1] + k0 + k + 1)
                    cols = slice(k * P, (k + 1) * P)
                    for n, (wp, rp) in enumerate(((whi, rhs_hi), (whi, rhs_lo), (wlo, rhs_hi))):
                        for h in range(2):
                            ins = pe.matmul(gp[t.par][:, h, 0:H2], wp[w.par][:, cols],
                                            rp[:, k0 + k, h * H2:(h + 1) * H2],
                                            start=first and k == 0 and n == 0,
                                            stop=last and k == kt - 1 and n == 2)
                    if k == kt - 1:
                        ins.then_inc(unit_done, 1)
                    if after is not None:
                        after(k)

            def hgemm(w, t, ready=None, after=None):
                gemm(w, t, hn_hi, hn_lo, ready=ready, after=after)

            def sum_squares(n):
                pe.wait_ge(acc_done, KD * (n + 1))
                for h in range(2):
                    ins = pe.matmul(sp_[:, h, 0:H2], ones, acc[:, h * H2:(h + 1) * H2], start=True, stop=True)
                ins.then_inc(ssq_done, 1)

            def norm_behind(n):
                return lambda k: sum_squares(n) if k == 1 else None

            def to_tokens(src, bank0, done):
                for i in range(NT):
                    for c in range(2):
                        ins = pe.transpose(sp_[0:SZ[i], bank0 + i // 2, (i % 2) * 256 + c * P:(i % 2) * 256 + (c + 1) * P],
                                           src[:, c, P * i:P * i + SZ[i]], ident)
                ins.then_inc(done, 1)

            def to_channels(src, done):
                for i in range(NT):
                    for c in range(2):
                        dst = sp_[:, 2 * c, P * i:P * i + P] if i < 4 else sp_[:, 2 * c + 1, 0:SZ[4]]
                        ins = pe.transpose(dst, src[0:SZ[i], i, c * P:(c + 1) * P], ident[0:SZ[i], 0:SZ[i]])
                ins.then_inc(done, 1)

            def causal(keys, queries, done, once=False):
                for j, q0, n, b, c0, _ in PIECES:
                    for d, (kk, qq) in enumerate(zip(keys, queries)):
                        ins = pe.matmul(sp_[0:SZ[j], b, c0:c0 + n], kk[:, P * j:P * j + SZ[j]], qq[:, q0:q0 + n],
                                        start=(d == 0) if not once else c0 == 0, stop=d == len(keys) - 1,
                                        skip_group_check=once)
                if done is not None:
                    ins.then_inc(done, 1)

            def mix_values(wt, val, width, dst, done):
                for i in range(NT):
                    for j in range(i + 1):
                        at = OFF[j] + P * (i - j)
                        ins = pe.matmul(dst(i), wt[0:SZ[j], at:at + SZ[i]], val(j), start=j == 0, stop=j == i)
                ins.then_inc(done, 1)

            hgemm(At(0, 0, W_DT), At(0, 0, T_DT), ready=(nlo_done, 0))
            pe.wait_ge(const_in, 16)
            sum_squares(0)
            for c in range(6):
                hgemm(At(6, 0, W_SSD + c), At(6, 0, T_SSD + c))
                if c == 0:
                    pe.wait_ge(cs_done, 1)
                    for n, src in enumerate((dtx, csr)):
                        for i in range(NT):
                            ins = pe.transpose(sp_[0:SZ[i], 2, 80 * n + 16 * i:80 * n + 16 * i + 16],
                                               src[:, P * i:P * i + SZ[i]], ident[0:16, 0:16])
                    ins.then_inc(dtT_done, 1)
            pe.wait_ge(dtok_done, 1)

            def ssd_small(g, step):
                if step == 0:
                    pe.wait_ge(silu_done, g + 1)
                    wait_count(pe, yout_done, g)
                    to_tokens(xcv[:, 0:2, :], 0, txs_done)
                if step == 1:
                    pe.wait_ge(xstok_done, g + 1)
                    to_tokens(zc, 0, tz_done)
                if step == 2:
                    pe.wait_ge(ztok_done, g + 1)
                    causal([xcv[:, 2, :]], [xcv[:, 3, :]], cb_done)
                if step in (3, 4):
                    for h in ((0, 1) if step == 3 else (2, 3)):
                        pe.wait_ge(m_done, HPG * g + h + 1)
                        if h == 0:
                            pe.wait_ge(cbs_done, g + 1)
                        mix_values(dec[h % 2], lambda j: x_dt[0:SZ[j], j, HEAD * h:HEAD * (h + 1)], HEAD,
                                   lambda i: sp_[0:SZ[i], h, HEAD * i:HEAD * (i + 1)], y_done)
                if step == 5:
                    pe.wait_ge(yn_done, g + 1)
                    to_channels(y_tok, tout_done)

            def ssd_stage(g):
                for c in range(6):
                    hgemm(At(6, g, W_SSD + c), At(6, g, T_SSD + c))
                    ssd_small(g - 1, c)

            ssd_stage(1)
            with pe.Fori(2, SSD_GROUPS) as g:
                ssd_stage(g)
            for c in range(6):
                ssd_small(SSD_GROUPS - 1, c)

            def ret_small(r, step):
                if step == 0:
                    wait_count(pe, yret_done, r)
                    pe.wait_ge(pair_free[(T_RET + 5) % 2], (T_RET + 5) // 2 + 1 + 4 * r)
                    to_tokens(vr, 0, tv_done)
                if step == 1:
                    pe.wait_ge(vtok_done, r + 1)
                    pe.wait_ge(rot_done, 2 * (r + 1))
                    causal([rk[:, 0, :], rk[:, 1, :]], [rq[:, 0, :], rq[:, 1, :]], sc_done)
                if step == 3:
                    pe.wait_ge(sdec_done, r + 1)
                    mix_values(sdec, lambda j: v_tok[0:SZ[j], j, :], 256,
                               lambda i: sp_[0:SZ[i], i // 2, (i % 2) * 256:(i % 2) * 256 + 256], o_done)
                if step == 5:
                    pe.wait_ge(on_done, r + 1)
                    to_channels(o_tok, tro_done)

            for c in range(8):
                hgemm(At(8, 0, W_RET + c), At(8, 0, T_RET + c))
            def ret_stage(r):
                for c in range(8):
                    hgemm(At(8, r, W_RET + c), At(8, r, T_RET + c))
                    ret_small(r - 1, c)

            ret_stage(1)
            with pe.Fori(2, RET_HEADS) as r:
                ret_stage(r)
            for c in range(8):
                ret_small(RET_HEADS - 1, c)

            def project(wb, tb, rhs_hi, rhs_lo, kt, ready):
                def tile(i, s, first_pair):
                    for kh in range(2):
                        gemm(At(4, i, wb + 2 * s + kh), At(2, i, tb + s), rhs_hi, rhs_lo, k0=kh * kt, kt=kt,
                             first=kh == 0, last=kh == 1, ready=ready if first_pair and s == 0 else None)

                for s in range(2):
                    tile(0, s, True)
                with pe.Fori(1, KD // 2) as i:
                    for s in range(2):
                        tile(i, s, False)

            def ffn_in(wb, tb, n):
                for s in range(2):
                    hgemm(At(2, 0, wb + s), At(2, 0, tb + s), ready=(nlo_done, KD * n) if s == 0 else None,
                          after=norm_behind(n) if s == 0 else None)
                with pe.Fori(1, KF) as i:
                    for s in range(2):
                        hgemm(At(2, i, wb + s), At(2, i, tb + s))

            project(W_OUT0, T_OUT0, y_hi, y_lo, KD, (ylo_done, 0))
            ffn_in(W_FI0, T_FI0, 1)
            project(W_FO0, T_FO0, hid_hi, hid_lo, KH, (hlo_done, 0))

            def scores(n, b, e):
                rows = slice(HEAD * e, HEAD * (e + 1))
                causal([ks[b][rows, :]], [qs[b][rows, :]], None, once=True)
                for j, _, _, bk, c0, _ in (PIECES[0], *PIECES[2:]):
                    ins = pe.matmul(sp_[0:SZ[j], bk, c0:c0 + SZ[j]], ident_b[0:SZ[j], 0:SZ[j]],
                                    never[0:SZ[j], 0:SZ[j]], start=False, stop=True, skip_group_check=True)
                ins.then_inc(z_done, 1)

            def suffix(n, e):
                pe.wait_ge(spf_done, 2 * n + e + 1)
                for j, q0, w, bk, c0, _ in PIECES:
                    for jj in range(j, NT):
                        lo = max(q0, P * jj)
                        if lo >= q0 + w:
                            continue
                        lhs = neg_r[0:SZ[j], 0, 0:SZ[j]] if jj == j else neg_r[0:SZ[jj], 1, 0:SZ[j]]
                        at = OFF[jj] + lo - P * jj
                        for part in (sp_hi, sp_lo):
                            ins = pe.matmul(sp_[0:SZ[j], bk, c0 + lo - q0:c0 + w], lhs,
                                            part[0:SZ[jj], at:at + q0 + w - lo], start=False, stop=True,
                                            skip_group_check=True)
                ins.then_inc(suf_done, 1)

            def values(n, e):
                pe.wait_ge(w_done, 2 * n + e + 1)
                wait_count(pe, so_done, 2 * n + e)
                if e == 0:
                    pe.wait_ge(svtok_done, n + 1)
                mix_values(wts[e], lambda j: sv_tok[0:SZ[j], j, HEAD * e:HEAD * (e + 1)], HEAD,
                           lambda i: sp_[0:SZ[i], 3, HEAD * i:HEAD * (i + 1)], pv_done)

            def heads_out(n):
                pe.wait_ge(so_done, 2 * n + 2)
                for i in range(NT):
                    dst = sp_[:, 3, P * i:P * (i + 1)] if i < 4 else sp_[:, 1, 32:32 + SZ[4]]
                    ins = pe.transpose(dst, so_tok[0:SZ[i], i, :], ident[0:SZ[i], 0:SZ[i]])
                ins.then_inc(tso_done, 1)

            def gates(n, b, half_n):
                pe.wait_ge(xc_done, n + 1)
                pe.wait_ge(gw_in[b], 16 * (half_n + 1))
                for gate, (b0, b1, c1) in enumerate(((0, 1, 0), (2, 1, 16))):
                    pe.matmul(sp_[:, b0, 0:512], gw[b][:, gate * P:(gate + 1) * P], xc[:, 0:512],
                              start=True, stop=True)
                    ins = pe.matmul(sp_[:, b1, c1:c1 + 16], gw[b][:, gate * P:(gate + 1) * P], xc[:, 512:T],
                                    start=True, stop=True)
                ins.then_inc(gates_done, 1)

            def v_out(n):
                wait_count(pe, ysb_done, n)
                for i in range(4):
                    pe.transpose(sp_[:, 3, P * i:P * (i + 1)], vs[:, P * i:P * (i + 1)], ident)
                for e, (bk, c0) in enumerate(V_LAST):
                    ins = pe.matmul(sp_[0:SZ[4], bk, c0:c0 + HEAD], vs[:, 512:T], ident[:, HEAD * e:HEAD * (e + 1)],
                                    start=True, stop=True)
                ins.then_inc(tvs_done, 1)

            def l1_small(i, b, unit, half):
                n = 2 * i + b
                before = not (isinstance(n, int) and n == 0)
                if (unit, half) == (0, 0) and before:
                    values(n - 1, 1)
                if (unit, half) == (0, 1):
                    if before:
                        heads_out(n - 1)
                    gates(n, b, i)
                if (unit, half) == (1, 0):
                    pe.wait_ge(tri_done, n + 1)
                    v_out(n)
                    scores(n, b, 0)
                if (unit, half) == (2, 1):
                    suffix(n, 0)
                if (unit, half) == (3, 0):
                    values(n, 0)
                    scores(n, b, 1)
                if (unit, half) == (4, 1):
                    suffix(n, 1)

            def l1_block(i, b, products=True):
                for c in range(5):
                    def after(k):
                        if k % 4 == 3:
                            l1_small(i, b, c, k // 4)
                    if products:
                        hgemm(At(10, i, W_L1 + 5 * (b + 1) + c), At(10, i, T_L1 + 5 * (b + 1) + c), after=after)
                    else:
                        l1_small(i, b, c, 0)
                        l1_small(i, b, c, 1)

            for c in range(5):
                hgemm(At(10, 0, W_L1 + c), At(10, 0, T_L1 + c), ready=(nlo_done, 2 * KD) if c == 0 else None,
                      after=norm_behind(2) if c == 0 else None)
            for b in range(2):
                l1_block(0, b)
            with pe.Fori(1, 3) as i:
                for b in range(2):
                    l1_block(i, b)
            l1_block(3, 0)
            l1_block(3, 1, products=False)
            values(7, 1)
            heads_out(7)

            project(W_OUT1, T_OUT1, y_hi, y_lo, KD, (ylo_done, 16))
            ffn_in(W_FI1, T_FI1, 3)
            project(W_FO1, T_FO1, hid_hi, hid_lo, KH, (hlo_done, KF))
            sum_squares(4)

        @block.scalar
        def _(act):
            ch = Chain(act, a_seq)

            def split_hi(w, kt=KD):
                act.wait_ge(raw_in[w.par], 16 * (w.half + 1))
                wait_count(act, unit_done, w.v - 1)
                act.activation(whi[w.par][:, 0:kt * P], raw[w.par][:, 0:kt * P], ACT.Copy).then_inc(hi_done, 1)
                act.wait_ge(hi_done, w.v + 1)

            def gained(n, m):
                act.activation(hn_hi[:, m, :], hT[:, m, :], ACT.Copy, scale=pcol(NORMS[n], m)).then_inc(nhi_done, 1)

            def square(n, m, s):
                wait_count(act, acc_done, KD * n + m - 1)
                act.activation(sq[s][:], hT[:, m, :], ACT.Square).then_inc(sq_done, 1)

            def root(n):
                act.wait_ge(ssq_done, n + 1)
                act.activation(halves(rstd[:]), sp_[:, 0:2, 0:H2], ACT.Sqrt, scale=1.0 / D_MODEL,
                               bias=eps_col[:, 0:1]).then_inc(root_done, 1)

            act.dma_start(cst[:], cst_h[:, 0:5 * P]).then_inc(const_in, 16)
            act.wait_ge(vec_in, 16)
            for m in range(KD):
                if m % 2 == 0:
                    act.wait_ge(h_in[m // 2], 16)
                gained(0, m)
                if m == 0:
                    split_hi(At(0, 0, 0))
                square(0, m, m % 2)
            split_hi(At(0, 0, 1))
            act.wait_ge(prep_done, 1)
            root(0)

            act.activation(aexp[:], pcol("ssd_alog", rows=16), ACT.Exp).then_inc(aexp_done, 1)
            act.wait_ge(dtx_done, 1)
            ch.link(act.activation(dtl[:], dtx[:], ACT.Abs))
            ch.link(act.activation(dtl[:], dtl[:], ACT.Exp, scale=-1.0))
            act.activation(dtl[:], dtl[:], ACT.Ln, bias=1.0).then_inc(dtl_done, 1)

            def load_bc(g):
                src = cs_d[bass.ds(HPG * g, HPG), :].unsqueeze(0).to_broadcast([P, HPG, T])
                act.dma_start(cs_bc[:], src).then_inc(bc_in, 16)

            def ssd_silu(g):
                act.wait_ge(conv_done, 4 * (g + 1))
                act.activation(xcv[:], xcv[:], ACT.Silu)
                act.wait_ge(pair_free[(T_SSD + 5) % 2], (T_SSD + 5) // 2 + 1 + 3 * g)
                act.activation(zc[:], zc[:], ACT.Silu).then_inc(silu_done, 1)

            def ssd_small(g, step):
                if step == 0:
                    ssd_silu(g)
                if step == 1:
                    act.wait_ge(txs_done, g + 1)
                    wait_count(act, ytok_done, HPG * g)
                    act.activation(xs_tok[:, 0:4, :].rearrange("p (b i) c -> p b (i c)", b=2), sp_[:, 0:2, :], ACT.Copy)
                    act.activation(xs_tok[0:SZ[4], 4, :], sp_[0:SZ[4], 2, 0:256], ACT.Copy).then_inc(xstok_done, 1)
                    for h in range(2):
                        decay(g, h)
                if step == 2:
                    act.wait_ge(tz_done, g + 1)
                    wait_count(act, yz_done, g)
                    act.activation(z_tok[:, 0:4, :].rearrange("p (b i) c -> p b (i c)", b=2), sp_[:, 0:2, :], ACT.Copy)
                    act.activation(z_tok[0:SZ[4], 4, :], sp_[0:SZ[4], 2, 0:256], ACT.Copy).then_inc(ztok_done, 1)
                if step == 3:
                    act.wait_ge(cb_done, g + 1)
                    for b, n, at in BANKS:
                        act.activation(cbs[:, at:at + n], sp_[:, b, 0:n], ACT.Copy)
                    act.activation(cbs[0:SZ[4], FULL:CAUSAL], sp_[0:SZ[4], 2, 416:432], ACT.Copy).then_inc(cbs_done, 1)
                if step == 4:
                    for h in range(2, 4):
                        decay(g, h)
                if step == 5:
                    act.wait_ge(yz_done, g + 1)
                    wait_count(act, yrs_done, g)
                    for i in range(NT):
                        ins = act.activation(x_dt[0:SZ[i], i, :], y_tok[0:SZ[i], i, :], ACT.Square,
                                             accum_out=ssq_tok[0:SZ[i], i:i + 1])
                    ins.then_inc(ysq_done, 1)
                if step == 6:
                    act.wait_ge(tout_done, g + 1)
                    for c in range(2):
                        act.activation(yT[:, 2 * g + c, 0:512], sp_[:, 2 * c, :], ACT.Copy, scale=pcol("ssd_norm", 2 * g + c))
                        ins = act.activation(yT[:, 2 * g + c, 512:T], sp_[:, 2 * c + 1, 0:16], ACT.Copy,
                                             scale=pcol("ssd_norm", 2 * g + c))
                    ins.then_inc(yout_done, 1)

            def decay(g, h):
                act.wait_ge(arg_done, HPG * g + h + 1)
                e = dec[h % 2]
                act.activation(e[:, 0:FULL], e[:, 0:FULL], ACT.Exp)
                act.activation(e[0:SZ[4], FULL:CAUSAL], e[0:SZ[4], FULL:CAUSAL], ACT.Exp).then_inc(e_done, 1)

            split_hi(At(6, 0, W_SSD + 1))
            for c in range(5):
                split_hi(At(6, 0, W_SSD + c + 2))
                if c == 0:
                    act.wait_ge(cs_done, 1)
                    act.dma_start(cs_d, csr[:]).then_inc(cs_out, 16)
                    act.wait_ge(cs_out, 16)
                    load_bc(0)

            def ssd_stage(g):
                for c in range(6):
                    split_hi(At(6, g, W_SSD + c + 1))
                    ssd_small(g - 1, c)
                    if c == 4:
                        act.wait_ge(arg_done, HPG * g)
                        load_bc(g)
                ssd_small(g - 1, 6)

            ssd_stage(1)
            with act.Fori(2, SSD_GROUPS) as g:
                ssd_stage(g)
            for c in range(7):
                ssd_small(SSD_GROUPS - 1, c)

            def ret_gate(r, c):
                t = At(8, r, T_RET + 6 + c)
                act.wait_ge(pair_free[t.par], t.half + 1)
                act.activation(gr[:, c, :], gr[:, c, :], ACT.Silu).then_inc(gs_done, 1)

            def ret_small(r, step):
                if step == 1:
                    act.wait_ge(tv_done, r + 1)
                    wait_count(act, o_done, r)
                    act.activation(v_tok[:, 0:4, :].rearrange("p (b i) c -> p b (i c)", b=2), sp_[:, 0:2, :], ACT.Copy)
                    act.activation(v_tok[0:SZ[4], 4, :], sp_[0:SZ[4], 2, 0:256], ACT.Copy).then_inc(vtok_done, 1)

            for c in range(8):
                split_hi(At(8, 0, W_RET + c + 1))
            ret_gate(0, 0)

            def ret_stage(r):
                for c in range(8):
                    split_hi(At(8, r, W_RET + c + 1))
                    if c == 0:
                        ret_gate(r - 1, 1)
                    if c == 7:
                        ret_gate(r, 0)
                    ret_small(r - 1, c)

            ret_stage(1)
            with act.Fori(2, RET_HEADS) as r:
                ret_stage(r)
            ret_gate(RET_HEADS - 1, 1)
            ret_small(RET_HEADS - 1, 1)

            def project(wb, tb, kt, n, src=False, following=True):
                if src:
                    for k in range(16):
                        act.activation(y_hi[:, k, :], yT[:, k, :], ACT.Copy).then_inc(yhi_done, 1)
                        if k == 7:
                            split_hi(At(0, 0, wb + 1), kt)
                else:
                    split_hi(At(0, 0, wb + 1), kt)

                def tile(i, s, m, last=False):
                    if following or not last:
                        split_hi(At(4, i, wb + 2 * s + 2), KD if last else kt)
                    if not last:
                        split_hi(At(4, i, wb + 2 * s + 3), kt)
                    t = At(2, i, tb + s)
                    act.wait_ge(pair_free[t.par], t.half + 1)
                    square(n, m, s)
                    if following:
                        gained(n, m)

                for s in range(2):
                    tile(0, s, s)
                with act.Fori(1, KD // 2 - 1) as i:
                    for s in range(2):
                        tile(i, s, 2 * i + s)
                tile(KD // 2 - 1, 0, KD - 2)
                tile(KD // 2 - 1, 1, KD - 1, last=True)

            def ffn_in(wb, tb, L):
                def gate(i):
                    act.wait_ge(cg_done, KF * L + i)
                    act.activation(cg[:], cg[:], ACT.Silu).then_inc(sg_done, 1)

                def hid(i):
                    act.wait_ge(hidf_done, KF * L + i)
                    act.activation(hid_hi[:, i - 1, :], hidf[:], ACT.Copy).then_inc(hhi_done, 1)

                split_hi(At(2, 0, wb + 1))
                split_hi(At(2, 0, wb + 2))

                def pair(i, kt=KD):
                    split_hi(At(2, i, wb + 1))
                    gate(i)
                    split_hi(At(2, i, wb + 2), kt)
                    hid(i)

                pair(1)
                with act.Fori(2, KF - 1) as i:
                    pair(i)
                pair(KF - 1, KH)
                gate(KF)
                hid(KF)

            act.wait_ge(yret_done, RET_HEADS)
            project(W_OUT0, T_OUT0, KD, 1, src=True)
            root(1)
            ffn_in(W_FI0, T_FI0, 0)
            project(W_FO0, T_FO0, KH, 2)
            root(2)

            act.wait_ge(spl_done, 1)
            ch.link(act.activation(nspt[:], pcol("lru_lam", 0, 8), ACT.Abs))
            ch.link(act.activation(nspt[:], nspt[:], ACT.Exp, scale=-1.0))
            act.activation(nspt[:], nspt[:], ACT.Ln, bias=1.0).then_inc(spl_ln, 1)
            act.wait_ge(spl_done, 2)

            def soft(n, e):
                act.wait_ge(z_done, 2 * n + e + 1)
                for b, w, at in BANKS:
                    act.activation(lbuf[:, at:at + w], sp_[:, b, 0:w], ACT.Abs)
                ch.link(act.activation(lbuf[0:SZ[4], FULL:CAUSAL], sp_[0:SZ[4], 2, 416:432], ACT.Abs))
                act.activation(lbuf[:, 0:FULL], lbuf[:, 0:FULL], ACT.Exp, scale=-1.0)
                ch.link(act.activation(lbuf[0:SZ[4], FULL:CAUSAL], lbuf[0:SZ[4], FULL:CAUSAL], ACT.Exp, scale=-1.0))
                for b, w, at in BANKS:
                    if b == 2:
                        act.activation(lbuf[0:SZ[4], FULL:CAUSAL], lbuf[0:SZ[4], FULL:CAUSAL], ACT.Ln, bias=1.0)
                    act.activation(lbuf[:, at:at + w], lbuf[:, at:at + w], ACT.Ln, bias=1.0).then_inc(l_done, 1)

            def load_exp():
                act.activation(idle_a[:, 0:1], eps_col[:], ACT.Exp)

            def weigh(n, e):
                act.wait_ge(suf_done, 2 * n + e + 1)
                wait_count(act, pv_done, 2 * n + e - 1)
                for b, w, at in BANKS:
                    act.activation(wts[e][:, at:at + w], sp_[:, b, 0:w], ACT.Exp)
                act.activation(wts[e][0:SZ[4], FULL:CAUSAL], sp_[0:SZ[4], 2, 416:432], ACT.Exp).then_inc(w_done, 1)

            def l1_gates(n):
                act.wait_ge(gates_done, n + 1)
                wait_count(act, ylru_done, n)
                for dst, gate, (b0, b1, c1) in ((tr, 0, (0, 1, 0)), (ti, 1, (2, 1, 16))):
                    act.activation(dst[:, 0:512], sp_[:, b0, 0:512], ACT.Tanh, scale=0.5, bias=hb_col(gate, n))
                    ins = act.activation(dst[:, 512:T], sp_[:, b1, c1:c1 + 16], ACT.Tanh, scale=0.5,
                                         bias=hb_col(gate, n))
                ins.then_inc(tri_done, 1)
                act.wait_ge(tri_done, n + 1)
                act.activation(lt[:], tr[:], ACT.Tanh, scale=nsp_col(n), bias=nsp_col(n))
                act.activation(la[:], tr[:], ACT.Exp, scale=nsp_col(n), bias=nsp_col(n)).then_inc(la_done, 1)
                act.wait_ge(gu_done, n + 1)
                act.activation(ge[:], ge[:], ACT.Tanh, scale=GELU_C).then_inc(gth_done, 1)

            def l1_v(n):
                act.wait_ge(tvs_done, n + 1)
                wait_count(act, pv_done, 2 * n)
                act.activation(sv_tok[:, 0:4, :], sp_[:, 3, :].rearrange("p (i c) -> p i c", c=P), ACT.Copy)
                act.wait_ge(z_done, 2 * n + 1)
                for e, (bk, c0) in enumerate(V_LAST):
                    ins = act.activation(sv_tok[0:SZ[4], 4, HEAD * e:HEAD * (e + 1)], sp_[0:SZ[4], bk, c0:c0 + HEAD],
                                         ACT.Copy)
                ins.then_inc(svtok_done, 1)

            def l1_heads_out(n, following=True):
                act.wait_ge(tso_done, n + 1)
                act.activation(yT[:, n, 0:512], sp_[:, 3, :], ACT.Copy)
                if following:
                    act.wait_ge(gates_done, n + 2)
                act.activation(yT[:, n, 512:T], sp_[:, 1, 32:48], ACT.Copy).then_inc(ysb_done, 1)

            def hb_col(gate, n):
                return hb[:, gate, bass.ds(n, 1)]

            def nsp_col(n):
                return nsp[:, bass.ds(n, 1)]

            for c in range(5):
                split_hi(At(10, 0, W_L1 + c + 1))

            def l1_block(i, b, products=True):
                n = 2 * i + b

                def split(c):
                    if products:
                        split_hi(At(10, i, W_L1 + 5 * (b + 1) + c))

                before = not (isinstance(n, int) and n == 0)
                if before:
                    weigh(n - 1, 1)
                split(1)
                if before:
                    l1_heads_out(n - 1)
                l1_gates(n)
                split(2)
                l1_v(n)
                soft(n, 0)
                split(3)
                split(4)
                load_exp()
                weigh(n, 0)
                soft(n, 1)
                split(5)
                act.wait_ge(lb_done, n + 1)
                act.activation(lb[:], lb[:], ACT.Sqrt, scale=0.25).then_inc(root1_done, 1)
                load_exp()

            for b in range(2):
                l1_block(0, b)
            with act.Fori(1, 3) as i:
                ch.enter(i, 1, 8)
                for b in range(2):
                    l1_block(i, b)
            ch.leave(1, 3)
            l1_block(3, 0)
            l1_block(3, 1, products=False)
            weigh(7, 1)
            l1_heads_out(7, following=False)
            act.wait_ge(ysb_done, 8)
            act.wait_ge(ylru_done, 8)
            project(W_OUT1, T_OUT1, KD, 3, src=True)
            root(3)
            ffn_in(W_FI1, T_FI1, 1)
            project(W_FO1, T_FO1, KH, 4, following=False)
            root(4)

        @block.vector
        def _(ve):
            ch = Chain(ve, v_seq)

            def split_lo(w, kt=KD):
                ve.wait_ge(hi_done, w.v + 1)
                n = slice(0, kt * P)
                ve.tensor_tensor(wlo[w.par][:, n], raw[w.par][:, n], whi[w.par][:, n].bitcast(f32),
                                 ALU.subtract).then_inc(lo_done, 1)
                ve.wait_ge(lo_done, w.v + 1)

            def gained(n, m):
                ve.wait_ge(nhi_done, KD * n + m + 1)
                ve.scalar_tensor_tensor(hn_lo[:, m, :], hT[:, m, :], pcol(NORMS[n], m), hn_hi[:, m, :].bitcast(f32),
                                        ALU.mult, ALU.subtract).then_inc(nlo_done, 1)

            def add_squares(n, m, s, first=False):
                ve.wait_ge(sq_done, KD * n + m + 1)
                if first:
                    wait_count(ve, ssq_done, n)
                    ve.tensor_copy(acc[:], sq[s][:]).then_inc(acc_done, 1)
                else:
                    ve.wait_ge(acc_done, KD * n + m)
                    ve.tensor_tensor(acc[:], acc[:], sq[s][:], ALU.add).then_inc(acc_done, 1)

            def invert(n):
                ve.wait_ge(root_done, n + 1)
                ve.reciprocal(rstd[:], rstd[:]).then_inc(rstd_done, 1)
                ve.wait_ge(rstd_done, n + 1)

            def evacuate(w, t, dst, scale=None):
                ve.wait_ge(unit_done, w.v + 1)
                if scale is None:
                    ins = ve.tensor_tensor(dst, gout(t.par), halves(rstd[:]), ALU.mult)
                else:
                    ins = ve.scalar_tensor_tensor(dst, gout(t.par), scale, halves(rstd[:]), ALU.mult, ALU.mult)
                ins.then_inc(pair_free[t.par], 1)

            def conv(dst, src, taps, w0, b0, link, done):
                link(ve.tensor_scalar(dst, src[:, taps - 1:taps - 1 + T], w0(taps - 1), b0, ALU.mult, ALU.add))
                for k in range(taps - 2, -1, -1):
                    ins = ve.scalar_tensor_tensor(dst, src[:, k:k + T], w0(k), dst, ALU.mult, ALU.add)
                    if k:
                        link(ins)
                ins.then_inc(done, 1)

            for s in range(2):
                ve.memset(ub[s][:, 0:3], 0.0)
            ve.memset(neg_half[:], -0.5)
            ve.memset(one_row[:], 1.0)
            ve.memset(eps_col[:], EPS).then_inc(prep_done, 1)
            ve.wait_ge(vec_in, 16)
            for m in range(KD):
                if m % 2 == 0:
                    ve.wait_ge(h_in[m // 2], 16)
                gained(0, m)
                if m == 0:
                    split_lo(At(0, 0, 0))
                add_squares(0, m, m % 2, first=m == 0)
            ve.wait_ge(const_in, 16)
            ve.tensor_copy(ident_b[:], ident)
            ve.tensor_copy(never[:], cst[:, 4 * P:5 * P])
            ve.tensor_copy(neg_r[:], cst[:, 2 * P:4 * P].rearrange("p (a c) -> p a c", a=2))
            split_lo(At(0, 0, 1))
            invert(0)

            ve.wait_ge(unit_done, 1)
            ve.tensor_tensor(halves(dtx[:]), gp[0][0:16, :, 0:H2], halves(rstd[0:16, :]),
                             ALU.mult).then_inc(pair_free[0], 1)
            ve.wait_ge(pair_free[0], 1)
            ve.tensor_scalar(dtx[:], dtx[:], pcol("ssd_dtb", rows=16), None, ALU.add).then_inc(dtx_done, 1)
            ve.wait_ge(dtl_done, 1)
            ch.link(ve.scalar_tensor_tensor(dtx[:], dtx[:], 0.0, dtl[:], ALU.max, ALU.add))
            ve.wait_ge(aexp_done, 1)
            ch.link(ve.tensor_scalar(dtl[:], dtx[:], aexp[:, 0:1], -1.0, ALU.mult, ALU.mult))
            ve.tensor_tensor_scan(csr[:], one_row[:], dtl[:], 0.0, ALU.mult, ALU.add).then_inc(cs_done, 1)

            def ssd_tile(g, c):
                w, t = At(6, g, W_SSD + c), At(6, g, T_SSD + c)
                if c >= 4:
                    wait_count(ve, tz_done, g)
                    evacuate(w, t, halves(zc[:, c - 4, :]))
                    return
                wait_count(ve, conv_done, 4 * g + c - 1)
                evacuate(w, t, halves(ub[c % 2][:, 3:3 + T]))
                ve.wait_ge(pair_free[t.par], t.half + 1)
                ct = 2 * g + c if c < 2 else (8 + g if c == 2 else 12 + g)
                wait_count(ve, txs_done if c < 2 else cb_done, g)
                conv(xcv[:, c, :], ub[c % 2], 4, lambda k: pcol("ssd_cw", 4 * ct + k), pcol("ssd_cb", ct),
                     ch.link, conv_done)

            def bc4(ap, n):
                return ap.unsqueeze(3).to_broadcast([n, ap.shape[1], HPG, HEAD])

            def heads(ap):
                return ap.rearrange("p i (h d) -> p i h d", h=HPG)

            def ssd_small(g, step):
                if step == 1:
                    for h in range(2):
                        args(g, h)
                    ve.wait_ge(xstok_done, g + 1)
                    wait_count(ve, y_done, HPG * g)
                    dts = dt_tok[:, :, bass.ds(HPG * g, HPG)]
                    ve.tensor_tensor(heads(x_dt[:, 0:4, :]), heads(xs_tok[:, 0:4, :]), bc4(dts[:, 0:4, :], P), ALU.mult)
                    ch.link(ve.tensor_tensor(heads(x_dt[0:SZ[4], 4:5, :]), heads(xs_tok[0:SZ[4], 4:5, :]),
                                             bc4(dts[0:SZ[4], 4:5, :], SZ[4]), ALU.mult))
                    skip = pcol("ssd_d", HPG * g, HPG).unsqueeze(1).to_broadcast([P, 4, HPG])
                    ve.tensor_tensor(heads(xs_tok[:, 0:4, :]), heads(xs_tok[:, 0:4, :]), bc4(skip, P), ALU.mult)
                    ch.link(ve.tensor_tensor(heads(xs_tok[0:SZ[4], 4:5, :]), heads(xs_tok[0:SZ[4], 4:5, :]),
                                             bc4(skip[0:SZ[4], 0:1, :], SZ[4]), ALU.mult))
                if step in (3, 4):
                    if step == 4:
                        for h in range(2):
                            take(g, h)
                            args(g, h + 2)
                    for h in ((0, 1) if step == 3 else (2, 3)):
                        ve.wait_ge(es_done, HPG * g + h + 1)
                        ve.wait_ge(cbs_done, g + 1)
                        e = dec[h % 2]
                        ve.tensor_tensor(e[:, 0:FULL], e[:, 0:FULL], cbs[:, 0:FULL], ALU.mult)
                        ve.tensor_tensor(e[0:SZ[4], FULL:CAUSAL], e[0:SZ[4], FULL:CAUSAL], cbs[0:SZ[4], FULL:CAUSAL],
                                         ALU.mult).then_inc(m_done, 1)
                if step == 5:
                    take(g, 2)
                    take(g, 3)
                    ve.wait_ge(ytok_done, HPG * (g + 1))
                    ve.wait_ge(ztok_done, g + 1)
                    ve.tensor_tensor(y_tok[:, 0:4, :], y_tok[:, 0:4, :], z_tok[:, 0:4, :], ALU.mult)
                    ve.tensor_tensor(y_tok[0:SZ[4], 4, :], y_tok[0:SZ[4], 4, :], z_tok[0:SZ[4], 4, :],
                                     ALU.mult).then_inc(yz_done, 1)
                    ve.wait_ge(yrs_done, g + 1)
                    for i in range(NT):
                        ins = ve.tensor_scalar(y_tok[0:SZ[i], i, :], y_tok[0:SZ[i], i, :], rs_tok[0:SZ[i], i:i + 1],
                                               None, ALU.mult)
                    ins.then_inc(yn_done, 1)

            def args(g, h):
                if h == 0:
                    ve.wait_ge(bc_in, 16 * (g + 1))
                wait_count(ve, y_done, HPG * g + h - 1)
                for j in range(NT):
                    ins = ve.tensor_scalar(dec[h % 2][0:SZ[j], OFF[j]:OFF[j] + WJ[j]], cs_bc[0:SZ[j], h, P * j:T],
                                           ncs_tok[0:SZ[j], j, bass.ds(HPG * g + h, 1)], 0.0, ALU.add, ALU.min)
                ins.then_inc(arg_done, 1)

            def take(g, h):
                ve.wait_ge(y_done, HPG * g + h + 1)
                if h == 0:
                    wait_count(ve, tout_done, g)
                c = slice(HEAD * h, HEAD * (h + 1))
                ve.tensor_tensor(y_tok[:, 0:4, c], sp_[:, h, 0:256].rearrange("p (i d) -> p i d", d=HEAD),
                                 xs_tok[:, 0:4, c], ALU.add)
                ve.tensor_tensor(y_tok[0:SZ[4], 4, c], sp_[0:SZ[4], h, 256:320], xs_tok[0:SZ[4], 4, c],
                                 ALU.add).then_inc(ytok_done, 1)

            split_lo(At(6, 0, W_SSD + 1))
            ve.wait_ge(dtT_done, 1)
            for n, (dst, sign) in enumerate(((dt_tok, 1.0), (ncs_tok, -1.0))):
                ve.tensor_scalar(dst[:, 0:4, :], sp_[:, 2, 80 * n:80 * n + 64].rearrange("p (i h) -> p i h", h=16),
                                 sign, None, ALU.mult)
                ins = ve.tensor_scalar(dst[0:SZ[4], 4, :], sp_[0:SZ[4], 2, 80 * n + 64:80 * n + 80], sign, None,
                                       ALU.mult)
            ins.then_inc(dtok_done, 1)
            for c in range(5):
                split_lo(At(6, 0, W_SSD + c + 2))
                ssd_tile(0, c)

            def ssd_stage(g):
                for c in range(6):
                    split_lo(At(6, g, W_SSD + c + 1))
                    if c == 0:
                        ssd_tile(g - 1, 5)
                    else:
                        ssd_tile(g, c - 1)
                    ssd_small(g - 1, c)

            ve.wait_ge(dtok_done, 1)
            ssd_stage(1)
            with ve.Fori(2, SSD_GROUPS) as g:
                ch.enter(g, 2, 14)
                ssd_stage(g)
            ch.leave(2, SSD_GROUPS)
            ssd_tile(SSD_GROUPS - 1, 5)
            for c in range(6):
                ssd_small(SSD_GROUPS - 1, c)

            ve.wait_ge(yout_done, SSD_GROUPS)
            ve.memset(ret_nh[:], -0.5).then_inc(prep_done, 1)

            def ret_tile(r, c):
                if c < 2:
                    wait_count(ve, rot_done, 2 * r - 1)
                elif c < 4:
                    wait_count(ve, rot_done, 2 * r)
                elif c < 6:
                    wait_count(ve, tv_done, r)
                else:
                    wait_count(ve, yret_done, r)
                evacuate(At(8, r, W_RET + c), At(8, r, T_RET + c), halves((qr, kr, vr, gr)[c // 2][:, c % 2, :]))

            def rotate(r, dst, src, last_tile, link):
                t = At(8, r, T_RET + last_tile)
                ve.wait_ge(pair_free[t.par], t.half + 1)
                wait_count(ve, sc_done, r)
                cos, sin = rope[:, 0, :], rope[:, 1, :]
                ve.tensor_tensor(rt[:], src[:, 1, :], sin, ALU.mult)
                link(ve.tensor_tensor(dst[:, 0, :], src[:, 0, :], cos, ALU.mult))
                link(ve.tensor_tensor(dst[:, 0, :], dst[:, 0, :], rt[:], ALU.subtract))
                ve.tensor_tensor(rt[:], src[:, 1, :], cos, ALU.mult)
                link(ve.tensor_tensor(dst[:, 1, :], src[:, 0, :], sin, ALU.mult))
                ve.tensor_tensor(dst[:, 1, :], dst[:, 1, :], rt[:], ALU.add).then_inc(rot_done, 1)

            def ret_small(r, step):
                if step == 2:
                    ve.wait_ge(sc_done, r + 1)
                    wait_count(ve, o_done, r)
                    for j, q0, n, b, c0, at in PIECES:
                        d0 = q0 - P * j
                        ins = ve.tensor_tensor(sdec[0:SZ[j], at:at + n], sp_[0:SZ[j], b, c0:c0 + n],
                                               rdec[0:SZ[j], r, d0:d0 + n], ALU.mult)
                    ins.then_inc(sdec_done, 1)
                if step == 4:
                    ve.wait_ge(o_done, r + 1)
                    wait_count(ve, tro_done, r)
                    for i in range(NT):
                        ins = ve.bn_stats(stats[0:SZ[i], i, :], sp_[0:SZ[i], i // 2, (i % 2) * 256:(i % 2) * 256 + 256])
                    ch.link(ins)
                    ve.tensor_copy(idle_v[:, 0:1], eps_col[:])
                    for i in range(NT):
                        ins = ve.bn_aggr(mv[0:SZ[i], i, :], stats[0:SZ[i], i, :])
                    ins.then_inc(mv_done, 1)
                    ve.wait_ge(rrs_done, r + 1)
                    for i in range(NT):
                        ins = ve.tensor_scalar(o_tok[0:SZ[i], i, :], sp_[0:SZ[i], i // 2, (i % 2) * 256:(i % 2) * 256 + 256],
                                               mv[0:SZ[i], i, 0:1], ret_rs[0:SZ[i], i:i + 1], ALU.subtract, ALU.mult)
                    ins.then_inc(on_done, 1)
                if step == 6:
                    ve.wait_ge(gs_done, 2 * (r + 1))
                    ve.wait_ge(tro_done, r + 1)
                    for c in range(2):
                        gain = pcol("ret_norm", 2 * r + c)
                        ve.scalar_tensor_tensor(yT[:, 8 + 2 * r + c, 0:512], sp_[:, 2 * c, :], gain, gr[:, c, 0:512],
                                                ALU.mult, ALU.mult)
                        ins = ve.scalar_tensor_tensor(yT[:, 8 + 2 * r + c, 512:T], sp_[:, 2 * c + 1, 0:16], gain,
                                                      gr[:, c, 512:T], ALU.mult, ALU.mult)
                    ins.then_inc(yret_done, 1)

            def ret_stage(r):
                for c in range(8):
                    split_lo(At(8, r, W_RET + c + 1))
                    if c == 0:
                        ret_tile(r - 1, 7)
                    else:
                        ret_tile(r, c - 1)
                    if c == 2:
                        rotate(r, rq, qr, 1, ch.link)
                    if c == 4:
                        rotate(r, rk, kr, 3, ch.link)
                    ret_small(r - 1, c)

            ve.wait_ge(tab_in, 32)
            for c in range(8):
                split_lo(At(8, 0, W_RET + c + 1))
                if c > 0:
                    ret_tile(0, c - 1)
                if c == 2:
                    rotate(0, rq, qr, 1, ch.link)
                if c == 4:
                    rotate(0, rk, kr, 3, ch.link)
            ret_stage(1)
            with ve.Fori(2, RET_HEADS) as r:
                ch.enter(r, 2, 7)
                ret_stage(r)
            ch.leave(2, RET_HEADS)
            ret_tile(RET_HEADS - 1, 7)
            for c in (2, 4, 6):
                ret_small(RET_HEADS - 1, c)

            def project(wb, tb, kt, n, yb=None, following=True):
                if yb is not None:
                    for k in range(16):
                        ve.wait_ge(yhi_done, yb + k + 1)
                        ve.tensor_tensor(y_lo[:, k, :], yT[:, k, :], y_hi[:, k, :].bitcast(f32),
                                         ALU.subtract).then_inc(ylo_done, 1)
                        if k == 7:
                            split_lo(At(0, 0, wb + 1), kt)
                else:
                    split_lo(At(0, 0, wb + 1), kt)

                def tile(i, s, m, last=False):
                    if following or not last:
                        split_lo(At(4, i, wb + 2 * s + 2), KD if last else kt)
                    if not last:
                        split_lo(At(4, i, wb + 2 * s + 3), kt)
                    ve.wait_ge(unit_done, At(4, i, wb + 2 * s + 2).v)
                    t = At(2, i, tb + s)
                    ve.tensor_tensor(halves(hT[:, m, :]), gout(t.par), halves(hT[:, m, :]), ALU.add)\
                      .then_inc(pair_free[t.par], 1)
                    add_squares(n, m, s, first=isinstance(m, int) and m == 0)
                    if following:
                        gained(n, m)

                for s in range(2):
                    tile(0, s, s)
                with ve.Fori(1, KD // 2 - 1) as i:
                    for s in range(2):
                        tile(i, s, 2 * i + s)
                tile(KD // 2 - 1, 0, KD - 2)
                tile(KD // 2 - 1, 1, KD - 1, last=True)

            def ffn_in(wb, tb, L):
                def f_conv(i, half, dst, done):
                    t = At(2, i, tb + half)
                    wait_count(ve, (cg_done, cu_done)[half], KF * L + i)
                    evacuate(At(2, i, wb + half), t, halves(ubf[half][:, 2:2 + T]))
                    ve.wait_ge(pair_free[t.par], t.half + 1)
                    ct = i + KF * half
                    conv(dst[:], ubf[half], 3, lambda k: pcol(f"f{L}_cw", 3 * ct + k), pcol(f"f{L}_cb", ct),
                         ch.link, done)

                def slot_a(i):
                    f_conv(i - 1, 1, cu, cu_done)
                    ve.wait_ge(cu_done, KF * L + i)
                    ve.wait_ge(sg_done, KF * L + i)
                    ve.tensor_tensor(hidf[:], cg[:], cu[:], ALU.mult).then_inc(hidf_done, 1)

                def lo(i):
                    ve.wait_ge(hhi_done, KF * L + i)
                    ve.tensor_tensor(hid_lo[:, i - 1, :], hidf[:], hid_hi[:, i - 1, :].bitcast(f32),
                                     ALU.subtract).then_inc(hlo_done, 1)

                ve.wait_ge(unit_done, wb)
                for s in range(2):
                    ins = ve.memset(ubf[s][:, 0:2], 0.0)
                ch.link(ins)
                split_lo(At(2, 0, wb + 1))
                split_lo(At(2, 0, wb + 2))
                f_conv(0, 0, cg, cg_done)

                def pair(i, kt=KD):
                    split_lo(At(2, i, wb + 1))
                    slot_a(i)
                    split_lo(At(2, i, wb + 2), kt)
                    f_conv(i, 0, cg, cg_done)
                    lo(i)

                pair(1)
                with ve.Fori(2, KF - 1) as i:
                    ch.enter(i, 2, 4)
                    pair(i)
                ch.leave(2, KF - 1)
                pair(KF - 1, KH)
                slot_a(KF)
                lo(KF)

            project(W_OUT0, T_OUT0, KD, 1, yb=0)
            invert(1)
            ffn_in(W_FI0, T_FI0, 0)
            project(W_FO0, T_FO0, KH, 2)
            invert(2)

            ch.link(ve.memset(ubx[:, 0:3], 0.0))
            ve.tensor_scalar(hb[:, 0, :], pcol("lru_ba", 0, 8), 0.5, None, ALU.mult)
            ve.tensor_scalar(hb[:, 1, :], pcol("lru_bx", 0, 8), 0.5, None, ALU.mult)
            ve.tensor_scalar(nsp[:], pcol("lru_lam", 0, 8), -1.0, 0.0, ALU.mult, ALU.max).then_inc(spl_done, 1)
            ve.wait_ge(spl_ln, 1)
            ve.wait_ge(spl_done, 1)
            ch.link(ve.tensor_tensor(nsp[:], nsp[:], nspt[:], ALU.add))
            ve.tensor_scalar(nsp[:], nsp[:], -0.5 * LRU_C, None, ALU.mult).then_inc(spl_done, 1)

            def soft(n, e):
                for b, w, at in BANKS:
                    ve.wait_ge(l_done, 3 * (2 * n + e) + b + 1)
                    ve.scalar_tensor_tensor(spb[:, at:at + w], sp_[:, b, 0:w], 0.0, lbuf[:, at:at + w], ALU.max, ALU.add)
                ch.link(ve.scalar_tensor_tensor(spb[0:SZ[4], FULL:CAUSAL], sp_[0:SZ[4], 2, 416:432], 0.0,
                                                lbuf[0:SZ[4], FULL:CAUSAL], ALU.max, ALU.add))
                wait_count(ve, suf_done, 2 * n + e)
                ve.tensor_copy(sp_hi[:, 0:FULL], spb[:, 0:FULL])
                ch.link(ve.tensor_copy(sp_hi[0:SZ[4], FULL:CAUSAL], spb[0:SZ[4], FULL:CAUSAL]))
                ve.tensor_tensor(sp_lo[:, 0:FULL], spb[:, 0:FULL], sp_hi[:, 0:FULL].bitcast(f32), ALU.subtract)
                ve.tensor_tensor(sp_lo[0:SZ[4], FULL:CAUSAL], spb[0:SZ[4], FULL:CAUSAL],
                                 sp_hi[0:SZ[4], FULL:CAUSAL].bitcast(f32), ALU.subtract).then_inc(spf_done, 1)

            def take_head(n, e):
                ve.wait_ge(pv_done, 2 * n + e + 1)
                if e == 0:
                    wait_count(ve, tso_done, n)
                c = slice(HEAD * e, HEAD * (e + 1))
                ve.tensor_copy(so_tok[:, 0:4, c], sp_[:, 3, 0:256].rearrange("p (i d) -> p i d", d=HEAD))
                ve.tensor_copy(so_tok[0:SZ[4], 4, c], sp_[0:SZ[4], 3, 256:320]).then_inc(so_done, 1)

            def l1_tile(i, b, c):
                n = 2 * i + b
                w, t = At(10, i, W_L1 + 5 * b + c), At(10, i, T_L1 + 5 * b + c)
                if c < 2:
                    wait_count(ve, z_done, 2 * n - 2)
                if c == 2:
                    wait_count(ve, tvs_done, n)
                if c == 4:
                    wait_count(ve, xc_done, n)
                dst = (qs[b % 2][:], ks[b % 2][:], vs[:], gt[:], ubx[:, 3:3 + T])[c]
                evacuate(w, t, halves(dst), SB_SCALE if c == 0 else None)

            def lru_in(i, b):
                n = 2 * i + b
                t = At(10, i, T_L1 + 5 * b + 4)
                ve.wait_ge(pair_free[t.par], t.half + 1)
                wait_count(ve, gates_done, n)
                conv(xc[:], ubx, 4, lambda k: pcol("lru_cw", 4 * n + k), pcol("lru_cb", n), ch.link, xc_done)

            def gelu_in(n):
                wait_count(ve, ylru_done, n)
                ch.link(ve.tensor_tensor(ge[:], gt[:], gt[:], ALU.mult))
                ch.link(ve.tensor_scalar(ge[:], ge[:], 0.044715, 1.0, ALU.mult, ALU.add))
                ve.tensor_tensor(ge[:], ge[:], gt[:], ALU.mult).then_inc(gu_done, 1)

            def lru_var(n):
                ve.wait_ge(la_done, n + 1)
                ve.scalar_tensor_tensor(ti[:], ti[:], 1.0, xc[:], ALU.add, ALU.mult)
                ch.link(ve.tensor_scalar(lb[:], lt[:], -1.0, 1.0, ALU.mult, ALU.add))
                ch.link(ve.reciprocal(lb[:], lb[:]))
                ch.link(ve.scalar_tensor_tensor(lb[:], lt[:], -2.0, lb[:], ALU.mult, ALU.mult))
                ve.tensor_scalar(lb[:], lb[:], 0.0, None, ALU.max).then_inc(lb_done, 1)

            def gelu_out(n):
                ve.wait_ge(gth_done, n + 1)
                ch.link(ve.scalar_tensor_tensor(ge[:], ge[:], 1.0, gt[:], ALU.add, ALU.mult))

            def lru_out(n):
                ve.wait_ge(root1_done, n + 1)
                ch.link(ve.tensor_tensor(lb[:], lb[:], ti[:], ALU.mult))
                ch.link(ve.tensor_tensor_scan(tr[:], la[:], lb[:], 0.0, ALU.mult, ALU.add))
                ve.scalar_tensor_tensor(yT[:, 8 + n, :], ge[:], 0.5, tr[:], ALU.mult, ALU.mult).then_inc(ylru_done, 1)

            for c in range(4):
                split_lo(At(10, 0, W_L1 + c + 1))
                l1_tile(0, 0, c)
            split_lo(At(10, 0, W_L1 + 5))

            def l1_block(i, b, products=True):
                n = 2 * i + b

                def split(c):
                    if products:
                        split_lo(At(10, i, W_L1 + 5 * (b + 1) + c))

                def tile(c):
                    if products:
                        l1_tile(i, b + 1, c)

                l1_tile(i, b, 4)
                lru_in(i, b)
                split(1)
                if not (isinstance(n, int) and n == 0):
                    take_head(n - 1, 1)
                    lru_out(n - 1)
                gelu_in(n)
                split(2)
                tile(0)
                soft(n, 0)
                split(3)
                tile(1)
                lru_var(n)
                split(4)
                tile(2)
                gelu_out(n)
                take_head(n, 0)
                tile(3)
                soft(n, 1)
                split(5)

            for b in range(2):
                l1_block(0, b)
            with ve.Fori(1, 3) as i:
                ch.enter(i, 1, 30)
                for b in range(2):
                    l1_block(i, b)
            ch.leave(1, 3)
            l1_block(3, 0)
            l1_block(3, 1, products=False)
            take_head(7, 1)
            lru_out(7)
            project(W_OUT1, T_OUT1, KD, 3, yb=16)
            invert(3)
            ffn_in(W_FI1, T_FI1, 1)
            project(W_FO1, T_FO1, KH, 4, following=False)
            invert(4)
            for m in range(KD):
                ve.scalar_tensor_tensor(yT[:, m, :], hT[:, m, :], pcol("final", m), rstd[:], ALU.mult,
                                        ALU.mult).then_inc(final_done, 1)

        @block.gpsimd
        def _(po):
            ch = Chain(po, g_seq)

            def await_count(sem_, n, k=0):
                po.wait_ge(sem_, n)
                po.tensor_tensor(idle_g[:, k:k + 1], eps_col[:], eps_col[:], ALU.mult)

            def mask(buf, done):
                for j in range(NT):
                    blk = buf[0:SZ[j], OFF[j]:OFF[j] + SZ[j]]
                    ins = po.affine_select(out=blk, in_=blk, compare_op=ALU.is_ge, fill=0.0, base=0,
                                           pattern=[[1, SZ[j]]], channel_multiplier=-1)
                ins.then_inc(done, 1)

            po.wait_ge(prep_done, 1)
            with po.Fori(0, SSD_GROUPS) as g:
                ch.enter(g, 0, 1)
                for h in range(HPG):
                    await_count(e_done, HPG * g + h + 1, h)
                    mask(dec[h % 2], es_done)
                await_count(ysq_done, g + 1, 4)
                po.tensor_scalar(rs_tok[:, 0:4], ssq_tok[:, 0:4], 1.0 / 256, EPS, ALU.mult, ALU.add)
                ch.link(po.tensor_scalar(rs_tok[0:SZ[4], 4:5], ssq_tok[0:SZ[4], 4:5], 1.0 / 256, EPS, ALU.mult, ALU.add))
                po.tensor_tensor(rs_tok[:, 0:4], rs_tok[:, 0:4], neg_half[:, 0:4], ALU.pow)
                po.tensor_tensor(rs_tok[0:SZ[4], 4:5], rs_tok[0:SZ[4], 4:5], neg_half[0:SZ[4], 4:5],
                                 ALU.pow).then_inc(yrs_done, 1)
            ch.leave(0, SSD_GROUPS)
            po.wait_ge(prep_done, 2)
            with po.Fori(0, RET_HEADS) as r:
                ch.enter(r, 0, 1)
                await_count(mv_done, r + 1, 5)
                po.tensor_scalar(ret_rs[:, 0:4], mv[:, 0:4, 1], 1.0, EPS, ALU.mult, ALU.add)
                ch.link(po.tensor_scalar(ret_rs[0:SZ[4], 4:5], mv[0:SZ[4], 4:5, 1], 1.0, EPS, ALU.mult, ALU.add))
                po.tensor_tensor(ret_rs[:, 0:4], ret_rs[:, 0:4], ret_nh[:, 0:4], ALU.pow)
                po.tensor_tensor(ret_rs[0:SZ[4], 4:5], ret_rs[0:SZ[4], 4:5], ret_nh[0:SZ[4], 4:5],
                                 ALU.pow).then_inc(rrs_done, 1)
            ch.leave(0, RET_HEADS)


def kernel(**inputs):
    import numpy as np
    import concourse.bacc as bacc
    from concourse.bass_utils import run_bass_kernel_spmd as run

    a = {k: np.asarray(v) for k, v in inputs.items()}

    def units(w, cols, kts):
        res = []
        for c in cols:
            k0 = 0
            for kt in kts:
                blk = w[k0 * P:(k0 + kt) * P, c:c + P]
                res.append(blk.reshape(kt, P, P).transpose(1, 0, 2).reshape(P, kt * P))
                k0 += kt
        return np.ascontiguousarray(np.stack(res))

    def per_channel(v):
        v = v.reshape(-1, v.shape[-1])
        return v.reshape(v.shape[0], -1, P).transpose(2, 1, 0).reshape(P, -1)

    def rows(v):
        res = np.zeros((P, 1), np.float32)
        res[:v.size, 0] = v
        return res

    h = np.concatenate([a["meta_tokens"], a["x"][0]], 0)
    x_h = np.ascontiguousarray(h.reshape(T, KD, P).transpose(2, 1, 0))
    parts = {"mix0": per_channel(a["l0_mix_norm"]), "ffn0": per_channel(a["l0_ffn_norm"]),
             "mix1": per_channel(a["l1_mix_norm"]), "ffn1": per_channel(a["l1_ffn_norm"]),
             "final": per_channel(a["final_norm"]), "ssd_cw": per_channel(a["l0_ssd_conv_w"]),
             "ssd_cb": per_channel(a["l0_ssd_conv_b"]), "ssd_norm": per_channel(a["l0_ssd_norm"]),
             "ret_norm": per_channel(a["l0_ret_norm"]),
             "f0_cw": per_channel(a["l0_ffn_conv_w"]), "f0_cb": per_channel(a["l0_ffn_conv_b"]),
             "f1_cw": per_channel(a["l1_ffn_conv_w"]), "f1_cb": per_channel(a["l1_ffn_conv_b"]),
             "lru_cw": per_channel(a["l1_lru_conv_w"]), "lru_cb": per_channel(a["l1_lru_conv_b"]),
             "lru_ba": per_channel(a["l1_lru_ba"]), "lru_bx": per_channel(a["l1_lru_bx"]),
             "lru_lam": per_channel(a["l1_lru_lambda"]), "ssd_d": np.tile(a["l0_ssd_d"][None], (P, 1)),
             "ssd_dtb": rows(a["l0_ssd_dt_bias"]), "ssd_alog": rows(a["l0_ssd_a_log"])}
    vec_h = np.ascontiguousarray(np.concatenate([parts[n] for n in COLS], 1))

    f = np.float32
    half = P
    inv = (1.0 / (f(10000.0) ** (np.arange(half, dtype=f) / f(half - 1)))).astype(f)
    ang = (np.arange(T, dtype=f)[None, :] * inv[:, None]).astype(f)
    tri = (np.arange(P)[:, None] >= np.arange(P)[None, :]).astype(f)
    cst_h = np.concatenate([np.eye(P, dtype=f), np.ones((P, P), f), -tri, -np.ones((P, P), f), -1e30 * tri, np.cos(ang),
                            np.sin(ang)],
                           1).astype(f)
    log_gamma = np.log1p(-np.exp2(-5.0 - np.arange(RET_HEADS)))
    diff = np.arange(T)[None, :] - np.arange(P)[:, None]
    dec_h = np.where(diff[:, None, :] >= 0, np.exp(log_gamma[None, :, None] * np.maximum(diff, 0)[:, None, :]), 0.0)
    dec_h = (dec_h / 16.0).astype(f)

    w = a["l0_w_in"]
    z0, x0, b0, c0 = 0, 1024, 2048, 2560
    dt0, q0 = 3072, 3088
    ssd_cols = [c for g in range(SSD_GROUPS) for c in (x0 + 256 * g, x0 + 256 * g + P, b0 + P * g, c0 + P * g,
                                                       z0 + 256 * g, z0 + 256 * g + P)]
    ret_cols = [q0 + 1024 * n + 256 * r + P * d for r in range(RET_HEADS) for n in range(4) for d in range(2)]
    l1_cols = [1024 * n + P * i for i in range(8) for n in range(5)]
    fi_cols = [FFN * n + P * i for i in range(KF) for n in range(2)]
    oc = [P * m for m in range(KD)]
    gate = np.ascontiguousarray(np.concatenate([a["l1_lru_wa"], a["l1_lru_wx"]], 2))
    arrays = [x_h, vec_h, cst_h, dec_h, units(w, [dt0], [KD]), units(w, ssd_cols, [KD]), units(w, ret_cols, [KD]),
              units(a["l0_w_out"], oc, [KD, KD]), units(a["l0_ffn_w_in"], fi_cols, [KD]),
              units(a["l0_ffn_w_out"], oc, [KH, KH]), units(a["l1_w_in"], l1_cols, [KD]),
              units(a["l1_w_out"], oc, [KD, KD]), units(a["l1_ffn_w_in"], fi_cols, [KD]),
              units(a["l1_ffn_w_out"], oc, [KH, KH]), gate]
    nc = bacc.Bacc("TRN2", target_bir_lowering=False, num_devices=1)
    named = {f"in_{n}": v for n, v in enumerate(arrays)}
    aps = [nc.dram_tensor(k, v.shape, mybir.dt.from_np(v.dtype), kind="ExternalInput").ap() for k, v in named.items()]
    out = nc.dram_tensor("out", (P, KD, SEQ), mybir.dt.float32, kind="ExternalOutput").ap()
    build(nc, *aps, out)
    r = run(nc, [named], core_ids=[0])
    got = r.results[0]["out"]
    return np.ascontiguousarray(got.transpose(2, 1, 0).reshape(1, SEQ, D_MODEL))
```

```python
import concourse.bass as bass
from concourse import mybir
from contextlib import ExitStack

P = 128
D_MODEL, SEQ, N_META = 1024, 512, 16
T = SEQ + N_META
H2 = T // 2
KD = D_MODEL // P
EPS = 1e-6
SSD_HEADS, SSD_GROUPS, HEAD = 16, 4, 64
HPG = SSD_HEADS // SSD_GROUPS
RET_HEADS = 4
SB_SCALE = HEAD ** -0.5
LRU_C = 8.0
GELU_C = (2.0 / 3.141592653589793) ** 0.5
FFN = 2816
KF = FFN // P
KH = KF // 2
NT = 5
SZ = [P, P, P, P, T - 4 * P]
WJ = [T - P * j for j in range(NT)]
OFF = [sum(WJ[:j]) for j in range(NT)]
CAUSAL = sum(WJ)
FULL = OFF[4]
PIECES = [(0, 0, 512, 0, 0, 0), (0, 512, 16, 1, 0, 512), (1, 128, 400, 1, 16, 528),
          (2, 256, 272, 2, 0, 928), (3, 384, 144, 2, 272, 1200), (4, 512, 16, 2, 416, 1344)]
BANKS = [(0, 512, 0), (1, 416, 512), (2, 416, 928)]

V_LAST = ((1, 416), (2, 432))

COLS = {}
_n = 0
for _name, _k in [("mix0", KD), ("ffn0", KD), ("mix1", KD), ("ffn1", KD), ("final", KD),
                  ("ssd_cw", 64), ("ssd_cb", 16), ("ssd_norm", 8), ("ret_norm", 8),
                  ("f0_cw", 3 * 2 * KF), ("f0_cb", 2 * KF), ("f1_cw", 3 * 2 * KF), ("f1_cb", 2 * KF),
                  ("lru_cw", 32), ("lru_cb", 8), ("lru_ba", 8), ("lru_bx", 8), ("lru_lam", 8),
                  ("ssd_d", 16), ("ssd_dtb", 1), ("ssd_alog", 1)]:
    COLS[_name] = _n
    _n += _k
NCOL = _n
NORMS = ("mix0", "ffn0", "mix1", "ffn1", "final")

W_DT, W_SSD, W_RET, W_OUT0, W_FI0, W_FO0 = 0, 1, 25, 57, 73, 117
W_L1, W_OUT1, W_FI1, W_FO1, W_END = 133, 173, 189, 233, 249
T_DT, T_SSD, T_RET, T_OUT0, T_FI0, T_FO0 = 0, 1, 25, 57, 73, 117
T_L1, T_OUT1, T_FI1, T_FO1 = 125, 165, 181, 225

EARLY = (tuple(range(8)), (0, 1, 2, 3, 8, 9, 10, 11))
LATE = tuple(tuple(k for k in range(16) if k not in e) for e in EARLY)


class At:

    def __init__(self, a, i, c):
        self.a, self.i, self.c = a, i, c
        self.v = a * i + c
        self.par = c % 2
        self.half = (a // 2) * i + c // 2


def wait_count(eng, sem, n):
    if isinstance(n, int) and n <= 0:
        return
    eng.wait_ge(sem, n)


class Chain:

    def __init__(self, eng, sem):
        self.eng, self.sem, self.base, self.n = eng, sem, 0, 0

    def link(self, ins):
        ins.then_inc(self.sem, 1)
        self.n += 1
        self.eng.wait_ge(self.sem, self.base + self.n)

    def enter(self, i, lo, per):
        self.saved, self.per = self.base + self.n, per
        self.base, self.n = self.saved + per * (i - lo), 0

    def leave(self, lo, hi):
        assert self.n == self.per, f"{self.n} links in the loop's body, not {self.per}"
        self.base, self.n = self.saved + self.per * (hi - lo), 0


def build(nc, x_h, vec_h, cst_h, dec_h, w_dt, w_ssd, w_ret, w_out0, w_fi0, w_fo0, w_l1, w_out1, w_fi1, w_fo1,
          w_gate, out):
    f32, f32r = mybir.dt.float32, mybir.dt.float32r
    ALU, ACT = mybir.AluOpType, mybir.ActivationFunctionType
    ctx = ExitStack()
    with ctx:
        def sb(name, shape, dt=f32, where=ctx):
            return where.enter_context(nc.sbuf_tensor(name, shape, dt))

        def sem(name):
            return ctx.enter_context(nc.semaphore(name))

        hT = sb("hT", [P, KD, T])
        hn_hi = sb("hn_hi", [P, KD, T], f32r)
        hn_lo = sb("hn_lo", [P, KD, T], f32r)
        raw = [sb(f"raw{s}", [P, KH * P]) for s in range(2)]
        whi = [sb(f"whi{s}", [P, KH * P], f32r) for s in range(2)]
        wlo = [sb(f"wlo{s}", [P, KH * P], f32r) for s in range(2)]
        vec = sb("vec", [P, NCOL])
        cst = sb("cst", [P, 5 * P])
        ident_b = sb("ident_b", [P, P], mybir.dt.bfloat16)
        never = sb("never", [P, P], mybir.dt.bfloat16)
        neg_r = sb("neg_r", [P, 2, P], f32r)
        ident, ones = cst[:, 0:P], cst[:, P:2 * P]
        sq = sb("sq", [P, 2, T])
        acc = sb("acc", [P, T])
        rstd = sb("rstd", [P, T])
        eps_col = sb("eps_col", [P, 1])
        idle_g, idle_v, idle_a = (sb(n, [P, 6]) for n in ("idle_g", "idle_v", "idle_a"))

        def scope():
            return ExitStack()

        with scope() as mix:
            yT = sb("yT", [P, 16, T], f32, mix)
            ub = sb("ub", [P, 2, 3 + T], f32, mix)
            qr, kr = sq, ub[:, :, 3:3 + T]
            vr = sb("vr", [P, 2, T], f32, mix)
            gr = sb("gr", [P, 2, T], f32, mix)
            with scope() as s1:
                xcv = sb("xcv", [P, 4, T], f32, s1)
                zc = sb("zc", [P, 2, T], f32, s1)
                xs_tok = sb("xs_tok", [P, NT, 256], f32, s1)
                x_dt = sb("x_dt", [P, NT, 256], f32, s1)
                z_tok = sb("z_tok", [P, NT, 256], f32, s1)
                y_tok = sb("y_tok", [P, NT, 256], f32, s1)
                cbs = sb("cbs", [P, CAUSAL], f32, s1)
                dec = [sb(f"dec{s}", [P, CAUSAL], f32, s1) for s in range(2)]
                cs_bc = sb("cs_bc", [P, HPG, T], f32, s1)
                dt_tok = sb("dt_tok", [P, NT, SSD_HEADS], f32, s1)
                ncs_tok = sb("ncs_tok", [P, NT, SSD_HEADS], f32, s1)
                dtx, dtl = (vr[0:SSD_HEADS, n, :] for n in range(2))
                csr, one_row = (gr[0:SSD_HEADS, n, :] for n in range(2))
                aexp = sb("aexp", [SSD_HEADS, 1], f32, s1)
                ssq_tok = sb("ssq_tok", [P, NT], f32, s1)
                rs_tok = sb("rs_tok", [P, NT], f32, s1)
                neg_half = sb("neg_half", [P, NT], f32, s1)
            with scope() as s2:
                rope = sb("rope", [P, 2, T], f32, s2)
                rdec = sb("rdec", [P, RET_HEADS, T], f32, s2)
                rq = sb("rq", [P, 2, T], f32, s2)
                rk = sb("rk", [P, 2, T], f32, s2)
                rt = sb("rt", [P, T], f32, s2)
                v_tok = sb("v_tok", [P, NT, 256], f32, s2)
                sdec = sb("sdec", [P, CAUSAL], f32, s2)
                o_tok = sb("o_tok", [P, NT, 256], f32, s2)
                stats = sb("stats", [P, NT, 6], f32, s2)
                mv = sb("mv", [P, NT, 2], f32, s2)
                ret_rs = sb("ret_rs", [P, NT], f32, s2)
                ret_nh = sb("ret_nh", [P, NT], f32, s2)
            with scope() as s3:
                qs = [sb(f"qs{s}", [P, T], f32, s3) for s in range(2)]
                ks = [sb(f"ks{s}", [P, T], f32, s3) for s in range(2)]
                vs, gt, xc, tr = vr[:, 0, :], vr[:, 1, :], gr[:, 0, :], gr[:, 1, :]
                ubx = ub[:, 0, :]
                gw = [sb(f"gw{s}", [P, 2 * P], f32, s3) for s in range(2)]
                sv_tok = sb("sv_tok", [P, NT, P], f32, s3)
                so_tok = sb("so_tok", [P, NT, P], f32, s3)
                lbuf = sb("lbuf", [P, CAUSAL], f32, s3)
                spb = sb("spb", [P, CAUSAL], f32, s3)
                sp_hi = sb("sp_hi", [P, CAUSAL], f32r, s3)
                sp_lo = sb("sp_lo", [P, CAUSAL], f32r, s3)
                wts = [sb(f"wts{s}", [P, CAUSAL], f32, s3) for s in range(2)]
                ti, la, lt, lb, ge = (sb(n, [P, T], f32, s3) for n in ("ti", "la", "lt", "lb", "ge"))
                hb = sb("hb", [P, 2, 8], f32, s3)
                nsp = sb("nsp", [P, 8], f32, s3)
                nspt = sb("nspt", [P, 8], f32, s3)
            with scope() as s4:
                y_hi = sb("y_hi", [P, KD, T], f32r, s4)
                y_lo = sb("y_lo", [P, KD, T], f32r, s4)
        with scope() as ffn:
            hid_hi = sb("hid_hi", [P, KF, T], f32r, ffn)
            hid_lo = sb("hid_lo", [P, KF, T], f32r, ffn)
            ubf = [sb(f"ubf{s}", [P, 2 + T], f32, ffn) for s in range(2)]
            cg = sb("cg", [P, T], f32, ffn)
            cu = sb("cu", [P, T], f32, ffn)
            hidf = sb("hidf", [P, T], f32, ffn)

        gp = [ctx.enter_context(nc.psum_tensor(f"gp{s}", [P, 2, 512], f32)) for s in range(2)]
        sp_ = ctx.enter_context(nc.psum_tensor("small", [P, 4, 512], f32))

        def halves(ap):
            return ap.rearrange("p (h t) -> p h t", h=2)

        def gout(s):
            return gp[s][:, :, 0:H2]

        def pcol(name, c=0, n=1, rows=P):
            return vec[0:rows, bass.ds(COLS[name] + c, n)]

        cs_d = nc.dram_tensor("cs_scratch", [SSD_HEADS, T], f32, kind="Internal").ap()

        raw_in = [sem(f"raw_in{s}") for s in range(2)]
        hi_done, lo_done, unit_done = sem("hi_done"), sem("lo_done"), sem("unit_done")
        pair_free = [sem(f"pair_free{s}") for s in range(2)]
        vec_in, const_in = sem("vec_in"), sem("const_in")
        h_in = [sem(f"h_in{c}") for c in range(KD // 2)]
        sq_done, acc_done, ssq_done, root_done = (sem(n) for n in ("sq_done", "acc_done", "ssq_done", "root_done"))
        rstd_done, nhi_done, nlo_done = sem("rstd_done"), sem("nhi_done"), sem("nlo_done")
        v_seq, a_seq, g_seq = sem("v_seq"), sem("a_seq"), sem("g_seq")
        yhi_done, ylo_done = sem("yhi_done"), sem("ylo_done")
        cg_done, cu_done, sg_done = sem("cg_done"), sem("cu_done"), sem("sg_done")
        hidf_done, hhi_done, hlo_done = sem("hidf_done"), sem("hhi_done"), sem("hlo_done")
        final_done, out_done = sem("final_done"), sem("out_done")
        dtl_done, aexp_done, cs_done, cs_out = (sem(n) for n in ("dtl_done", "aexp_done", "cs_done", "cs_out"))
        dtx_done, dtT_done, dtok_done, bc_in = sem("dtx_done"), sem("dtT_done"), sem("dtok_done"), sem("bc_in")
        conv_done, silu_done, txs_done, xstok_done = (
            sem(n) for n in ("conv_done", "silu_done", "txs_done", "xstok_done"))
        tz_done, ztok_done, cb_done, cbs_done = (sem(n) for n in ("tz_done", "ztok_done", "cb_done", "cbs_done"))
        arg_done, e_done, es_done, m_done, y_done, ytok_done = (
            sem(n) for n in ("arg_done", "e_done", "es_done", "m_done", "y_done", "ytok_done"))
        yz_done, ysq_done, yrs_done, yn_done, tout_done, yout_done = (
            sem(n) for n in ("yz_done", "ysq_done", "yrs_done", "yn_done", "tout_done", "yout_done"))
        tab_in, rot_done, tv_done, vtok_done, sc_done, sdec_done = (
            sem(n) for n in ("tab_in", "rot_done", "tv_done", "vtok_done", "sc_done", "sdec_done"))
        o_done, mv_done, rrs_done, on_done, tro_done, yret_done, gs_done = (
            sem(n) for n in ("o_done", "mv_done", "rrs_done", "on_done", "tro_done", "yret_done", "gs_done"))
        gw_in = [sem(f"gw_in{s}") for s in range(2)]
        xc_done, gates_done, tri_done, la_done, lb_done, root1_done = (
            sem(n) for n in ("xc_done", "gates_done", "tri_done", "la_done", "lb_done", "root1_done"))
        z_done, l_done, spf_done, suf_done, w_done, pv_done, so_done = (
            sem(n) for n in ("z_done", "l_done", "spf_done", "suf_done", "w_done", "pv_done", "so_done"))
        tvs_done, svtok_done, tso_done, ysb_done, gu_done, gth_done, ylru_done = (
            sem(n) for n in ("tvs_done", "svtok_done", "tso_done", "ysb_done", "gu_done", "gth_done", "ylru_done"))
        sum_done, sphi_done = sem("sum_done"), sem("sphi_done")
        prep_done, spl_done, spl_ln = sem("prep_done"), sem("spl_done"), sem("spl_ln")

        block = ctx.enter_context(nc.Block())

        @block.sync
        def _(sp):
            def unit(w, src, kt=KD):
                wait_count(sp, lo_done, w.v - 1)
                sp.dma_start(raw[w.par][:, 0:kt * P], src).then_inc(raw_in[w.par], 16)

            for c in range(KD // 2):
                sp.dma_start(hT[:, 2 * c:2 * c + 2, :], x_h[:, 2 * c:2 * c + 2, :]).then_inc(h_in[c], 16)
                if c == 0:
                    unit(At(0, 0, 0), w_dt[0])
            unit(At(0, 0, 1), w_ssd[0])
            for c in range(1, 6):
                unit(At(6, 0, W_SSD + c), w_ssd[c])
            with sp.Fori(1, SSD_GROUPS) as g:
                for c in range(6):
                    unit(At(6, g, W_SSD + c), w_ssd[6 * g + c])
            for c in range(8):
                unit(At(8, 0, W_RET + c), w_ret[c])
            with sp.Fori(1, RET_HEADS) as r:
                for c in range(8):
                    unit(At(8, r, W_RET + c), w_ret[8 * r + c])

            def stream(base, n, src, kt=KD):
                with sp.Fori(0, n // 2) as i:
                    for s in range(2):
                        unit(At(2, i, base + s), src[2 * i + s], kt)

            stream(W_OUT0, 16, w_out0)
            stream(W_FI0, 2 * KF, w_fi0)
            stream(W_FO0, 16, w_fo0, KH)

            def l1_pair(i):
                for b in range(2):
                    for c in range(5):
                        if c == 4:
                            if isinstance(i, int):
                                sp.wait_ge(unit_done, W_L1)
                            else:
                                sp.wait_ge(gates_done, 2 * i + b - 1)
                            sp.dma_start(gw[b][:], w_gate[2 * i + b]).then_inc(gw_in[b], 16)
                        unit(At(10, i, W_L1 + 5 * b + c), w_l1[10 * i + 5 * b + c])

            l1_pair(0)
            with sp.Fori(1, 4) as i:
                l1_pair(i)
            stream(W_OUT1, 16, w_out1)
            stream(W_FI1, 2 * KF, w_fi1)
            stream(W_FO1, 16, w_fo1, KH)
            for c in range(KD // 2):
                sp.wait_ge(final_done, 2 * c + 2)
                sp.dma_start(out[:, 2 * c:2 * c + 2, :], yT[:, 2 * c:2 * c + 2, N_META:T]).then_inc(out_done, 16)
            sp.wait_ge(out_done, 16 * (KD // 2))

        @block.tensor
        def _(pe):
            def gemm(w, t, rhs_hi, rhs_lo, k0=0, kt=KD, first=True, last=True, ready=None, after=None):
                pe.wait_ge(lo_done, w.v + 1)
                if first:
                    wait_count(pe, pair_free[t.par], t.half)
                for k in range(kt):
                    if ready is not None:
                        pe.wait_ge(ready[0], ready[1] + k0 + k + 1)
                    cols = slice(k * P, (k + 1) * P)
                    for n, (wp, rp) in enumerate(((whi, rhs_hi), (whi, rhs_lo), (wlo, rhs_hi))):
                        for h in range(2):
                            ins = pe.matmul(gp[t.par][:, h, 0:H2], wp[w.par][:, cols],
                                            rp[:, k0 + k, h * H2:(h + 1) * H2],
                                            start=first and k == 0 and n == 0,
                                            stop=last and k == kt - 1 and n == 2)
                    if k == kt - 1:
                        ins.then_inc(unit_done, 1)
                    if after is not None:
                        after(k)

            def hgemm(w, t, ready=None, after=None):
                gemm(w, t, hn_hi, hn_lo, ready=ready, after=after)

            def sum_squares(n):
                pe.wait_ge(acc_done, KD * (n + 1))
                for h in range(2):
                    ins = pe.matmul(sp_[:, h, 0:H2], ones, acc[:, h * H2:(h + 1) * H2], start=True, stop=True)
                ins.then_inc(ssq_done, 1)

            def norm_behind(n):
                return lambda k: sum_squares(n) if k == 1 else None

            def to_tokens(src, bank0, done):
                for i in range(NT):
                    for c in range(2):
                        ins = pe.transpose(sp_[0:SZ[i], bank0 + i // 2, (i % 2) * 256 + c * P:(i % 2) * 256 + (c + 1) * P],
                                           src[:, c, P * i:P * i + SZ[i]], ident)
                ins.then_inc(done, 1)

            def to_channels(src, done):
                for i in range(NT):
                    for c in range(2):
                        dst = sp_[:, 2 * c, P * i:P * i + P] if i < 4 else sp_[:, 2 * c + 1, 0:SZ[4]]
                        ins = pe.transpose(dst, src[0:SZ[i], i, c * P:(c + 1) * P], ident[0:SZ[i], 0:SZ[i]])
                ins.then_inc(done, 1)

            def causal(keys, queries, done, once=False):
                for j, q0, n, b, c0, _ in PIECES:
                    for d, (kk, qq) in enumerate(zip(keys, queries)):
                        ins = pe.matmul(sp_[0:SZ[j], b, c0:c0 + n], kk[:, P * j:P * j + SZ[j]], qq[:, q0:q0 + n],
                                        start=(d == 0) if not once else c0 == 0, stop=d == len(keys) - 1,
                                        skip_group_check=once)
                if done is not None:
                    ins.then_inc(done, 1)

            def mix_values(wt, val, dst, done):
                for i in range(NT):
                    for j in range(i + 1):
                        at = OFF[j] + P * (i - j)
                        ins = pe.matmul(dst(i), wt[0:SZ[j], at:at + SZ[i]], val(j), start=j == 0, stop=j == i)
                ins.then_inc(done, 1)

            hgemm(At(0, 0, W_DT), At(0, 0, T_DT), ready=(nlo_done, 0))
            pe.wait_ge(const_in, 16)
            sum_squares(0)
            for c in range(6):
                hgemm(At(6, 0, W_SSD + c), At(6, 0, T_SSD + c))
                if c == 2:
                    pe.wait_ge(cs_done, 1)
                    for n, src in enumerate((dtx, csr)):
                        for i in range(NT):
                            ins = pe.transpose(sp_[0:SZ[i], 2, 80 * n + 16 * i:80 * n + 16 * i + 16],
                                               src[:, P * i:P * i + SZ[i]], ident[0:16, 0:16])
                    ins.then_inc(dtT_done, 1)
            pe.wait_ge(dtok_done, 1)

            def ssd_small(g, step):
                if step == 0:
                    pe.wait_ge(silu_done, g + 1)
                    wait_count(pe, yout_done, g)
                    to_tokens(xcv[:, 0:2, :], 0, txs_done)
                if step == 1:
                    pe.wait_ge(xstok_done, g + 1)
                    to_tokens(zc, 0, tz_done)
                if step == 2:
                    pe.wait_ge(ztok_done, g + 1)
                    causal([xcv[:, 2, :]], [xcv[:, 3, :]], cb_done)
                if step in (3, 4):
                    for h in ((0, 1) if step == 3 else (2, 3)):
                        pe.wait_ge(m_done, HPG * g + h + 1)
                        if h == 0:
                            pe.wait_ge(cbs_done, g + 1)
                        mix_values(dec[h % 2], lambda j: x_dt[0:SZ[j], j, HEAD * h:HEAD * (h + 1)],
                                   lambda i: sp_[0:SZ[i], h, HEAD * i:HEAD * (i + 1)], y_done)

            def ssd_back(g):
                def after(k):
                    if k == 3:
                        pe.wait_ge(yn_done, g + 1)
                        to_channels(y_tok, tout_done)
                return after

            def ssd_stage(g):
                for c in range(6):
                    later = c == 0 and not (isinstance(g, int) and g < 2)
                    hgemm(At(6, g, W_SSD + c), At(6, g, T_SSD + c), after=ssd_back(g - 2) if later else None)
                    ssd_small(g - 1, c)

            ssd_stage(1)
            with pe.Fori(2, SSD_GROUPS) as g:
                ssd_stage(g)

            def ret_small(r, step):
                if step == 0:
                    wait_count(pe, yret_done, r)
                    pe.wait_ge(pair_free[(T_RET + 5) % 2], (T_RET + 5) // 2 + 1 + 4 * r)
                    to_tokens(vr, 0, tv_done)
                if step == 1:
                    pe.wait_ge(vtok_done, r + 1)
                    pe.wait_ge(rot_done, 2 * (r + 1))
                    causal([rk[:, 0, :], rk[:, 1, :]], [rq[:, 0, :], rq[:, 1, :]], sc_done)
                if step == 3:
                    pe.wait_ge(sdec_done, r + 1)
                    mix_values(sdec, lambda j: v_tok[0:SZ[j], j, :],
                               lambda i: sp_[0:SZ[i], i // 2, (i % 2) * 256:(i % 2) * 256 + 256], o_done)
                if step == 5:
                    pe.wait_ge(on_done, r + 1)
                    to_channels(o_tok, tro_done)

            for c in range(8):
                hgemm(At(8, 0, W_RET + c), At(8, 0, T_RET + c),
                      after=ssd_back({0: SSD_GROUPS - 2, 6: SSD_GROUPS - 1}[c]) if c in (0, 6) else None)
                if c < 5:
                    ssd_small(SSD_GROUPS - 1, c)

            def ret_stage(r):
                for c in range(8):
                    hgemm(At(8, r, W_RET + c), At(8, r, T_RET + c))
                    ret_small(r - 1, c)

            ret_stage(1)
            with pe.Fori(2, RET_HEADS) as r:
                ret_stage(r)
            for c in range(8):
                hgemm(At(0, 0, W_OUT0 + c), At(0, 0, T_OUT0 + c), ready=(ylo_done, 0) if c == 0 else None)
                ret_small(RET_HEADS - 1, c)

            def project(wb, tb, rhs_hi, rhs_lo, kt, ready, per=2):
                def tile(i, s, first_pair):
                    for kh in range(per):
                        gemm(At(2 * per, i, wb + per * s + kh), At(2, i, tb + s), rhs_hi, rhs_lo, k0=kh * kt, kt=kt,
                             first=kh == 0, last=kh == per - 1, ready=ready if first_pair and s == 0 else None)

                for s in range(2):
                    tile(0, s, True)
                with pe.Fori(1, KD // 2) as i:
                    for s in range(2):
                        tile(i, s, False)

            def ffn_in(wb, tb, n):
                for s in range(2):
                    hgemm(At(2, 0, wb + s), At(2, 0, tb + s), ready=(nlo_done, KD * n) if s == 0 else None,
                          after=norm_behind(n) if s == 0 else None)
                with pe.Fori(1, KF) as i:
                    for s in range(2):
                        hgemm(At(2, i, wb + s), At(2, i, tb + s))

            project(W_OUT0 + KD, T_OUT0 + KD, y_hi, y_lo, KD, (ylo_done, KD), per=1)
            ffn_in(W_FI0, T_FI0, 1)
            project(W_FO0, T_FO0, hid_hi, hid_lo, KH, (hlo_done, 0))

            def scores(n, b, e):
                rows = slice(HEAD * e, HEAD * (e + 1))
                causal([ks[b][rows, :]], [qs[b][rows, :]], None, once=True)
                for j, _, _, bk, c0, _ in (PIECES[0], *PIECES[2:]):
                    ins = pe.matmul(sp_[0:SZ[j], bk, c0:c0 + SZ[j]], ident_b[0:SZ[j], 0:SZ[j]],
                                    never[0:SZ[j], 0:SZ[j]], start=False, stop=True, skip_group_check=True)
                ins.then_inc(z_done, 1)

            def suffix(n, e):
                pe.wait_ge(spf_done, 2 * n + e + 1)
                if e == 0:
                    pe.wait_ge(svtok_done, n + 1)
                for j, q0, w, bk, c0, _ in PIECES:
                    for jj in range(j, NT):
                        lo = max(q0, P * jj)
                        if lo >= q0 + w:
                            continue
                        lhs = neg_r[0:SZ[j], 0, 0:SZ[j]] if jj == j else neg_r[0:SZ[jj], 1, 0:SZ[j]]
                        at = OFF[jj] + lo - P * jj
                        for part in (sp_hi, sp_lo):
                            ins = pe.matmul(sp_[0:SZ[j], bk, c0 + lo - q0:c0 + w], lhs,
                                            part[0:SZ[jj], at:at + q0 + w - lo], start=False, stop=True,
                                            skip_group_check=True)
                ins.then_inc(suf_done, 1)

            def values(n, e):
                pe.wait_ge(w_done, 2 * n + e + 1)
                wait_count(pe, so_done, 2 * n + e)
                mix_values(wts[e], lambda j: sv_tok[0:SZ[j], j, HEAD * e:HEAD * (e + 1)],
                           lambda i: sp_[0:SZ[i], 3, HEAD * i:HEAD * (i + 1)], pv_done)

            def heads_out(n):
                pe.wait_ge(so_done, 2 * n + 2)
                for i in range(NT):
                    dst = sp_[:, 3, P * i:P * (i + 1)] if i < 4 else sp_[:, 1, 32:32 + SZ[4]]
                    ins = pe.transpose(dst, so_tok[0:SZ[i], i, :], ident[0:SZ[i], 0:SZ[i]])
                ins.then_inc(tso_done, 1)

            def gates(n, b, half_n):
                pe.wait_ge(xc_done, n + 1)
                pe.wait_ge(gw_in[b], 16 * (half_n + 1))
                for gate, (b0, b1, c1) in enumerate(((0, 1, 0), (2, 1, 16))):
                    pe.matmul(sp_[:, b0, 0:512], gw[b][:, gate * P:(gate + 1) * P], xc[:, 0:512],
                              start=True, stop=True)
                    ins = pe.matmul(sp_[:, b1, c1:c1 + 16], gw[b][:, gate * P:(gate + 1) * P], xc[:, 512:T],
                                    start=True, stop=True)
                ins.then_inc(gates_done, 1)

            def v_out(n):
                wait_count(pe, ysb_done, n)
                for i in range(4):
                    pe.transpose(sp_[:, 3, P * i:P * (i + 1)], vs[:, P * i:P * (i + 1)], ident)
                for e, (bk, c0) in enumerate(V_LAST):
                    ins = pe.matmul(sp_[0:SZ[4], bk, c0:c0 + HEAD], vs[:, 512:T], ident[:, HEAD * e:HEAD * (e + 1)],
                                    start=True, stop=True)
                ins.then_inc(tvs_done, 1)

            def l1_small(i, b, unit, half):
                n = 2 * i + b
                before = not (isinstance(n, int) and n == 0)
                if (unit, half) == (0, 0) and before:
                    values(n - 1, 1)
                if (unit, half) == (0, 1):
                    if before:
                        heads_out(n - 1)
                    gates(n, b, i)
                if (unit, half) == (1, 0):
                    pe.wait_ge(tri_done, n + 1)
                    v_out(n)
                    scores(n, b, 0)
                if (unit, half) == (2, 1):
                    suffix(n, 0)
                if (unit, half) == (3, 0):
                    values(n, 0)
                    scores(n, b, 1)
                if (unit, half) == (4, 1):
                    suffix(n, 1)

            def l1_block(i, b, ready=None):
                for c in range(5):
                    def after(k):
                        if k % 4 == 3:
                            l1_small(i, b, c, k // 4)
                    hgemm(At(10, i, W_L1 + 5 * (b + 1) + c), At(10, i, T_L1 + 5 * (b + 1) + c),
                          ready=ready if c == 0 else None, after=after)

            for c in range(5):
                hgemm(At(10, 0, W_L1 + c), At(10, 0, T_L1 + c), ready=(nlo_done, 2 * KD) if c == 0 else None,
                      after=norm_behind(2) if c == 0 else None)
            for b in range(2):
                l1_block(0, b)
            with pe.Fori(1, 3) as i:
                for b in range(2):
                    l1_block(i, b)
            l1_block(3, 0)
            l1_block(3, 1, ready=(ylo_done, 2 * KD))
            for c in range(5, 8):
                def after(k):
                    if c == 5 and k == 3:
                        values(7, 1)
                    if c == 5 and k == 7:
                        heads_out(7)
                hgemm(At(0, 0, W_OUT1 + c), At(0, 0, T_OUT1 + c), after=after)

            project(W_OUT1 + KD, T_OUT1 + KD, y_hi, y_lo, KD, (ylo_done, 3 * KD), per=1)
            ffn_in(W_FI1, T_FI1, 3)
            project(W_FO1, T_FO1, hid_hi, hid_lo, KH, (hlo_done, KF))
            sum_squares(4)

        @block.scalar
        def _(act):
            ch = Chain(act, a_seq)

            def split_hi(w, kt=KD):
                act.wait_ge(raw_in[w.par], 16 * (w.half + 1))
                wait_count(act, unit_done, w.v - 1)
                act.activation(whi[w.par][:, 0:kt * P], raw[w.par][:, 0:kt * P], ACT.Copy).then_inc(hi_done, 1)
                act.wait_ge(hi_done, w.v + 1)

            def gained(n, m):
                act.activation(hn_hi[:, m, :], hT[:, m, :], ACT.Copy, scale=pcol(NORMS[n], m)).then_inc(nhi_done, 1)

            def square(n, m, s):
                wait_count(act, acc_done, KD * n + m - 1)
                act.activation(sq[:, s, :], hT[:, m, :], ACT.Square).then_inc(sq_done, 1)

            def root(n):
                act.wait_ge(ssq_done, n + 1)
                act.activation(halves(rstd[:]), sp_[:, 0:2, 0:H2], ACT.Sqrt, scale=1.0 / D_MODEL,
                               bias=eps_col[:, 0:1]).then_inc(root_done, 1)

            act.dma_start(vec[:], vec_h).then_inc(vec_in, 16)
            act.dma_start(cst[:], cst_h[:, 0:5 * P]).then_inc(const_in, 16)
            act.wait_ge(vec_in, 16)
            for m in range(KD):
                if m % 2 == 0:
                    act.wait_ge(h_in[m // 2], 16)
                gained(0, m)
                if m == 0:
                    split_hi(At(0, 0, 0))
                square(0, m, m % 2)
            split_hi(At(0, 0, 1))
            split_hi(At(6, 0, W_SSD + 1))
            act.wait_ge(prep_done, 1)
            root(0)

            act.activation(aexp[:], pcol("ssd_alog", rows=16), ACT.Exp).then_inc(aexp_done, 1)
            split_hi(At(6, 0, W_SSD + 2))
            act.wait_ge(dtx_done, 1)
            ch.link(act.activation(dtl, dtx, ACT.Abs))
            ch.link(act.activation(dtl, dtl, ACT.Exp, scale=-1.0))
            act.activation(dtl, dtl, ACT.Ln, bias=1.0).then_inc(dtl_done, 1)

            def load_bc(g):
                src = cs_d[bass.ds(HPG * g, HPG), :].unsqueeze(0).to_broadcast([P, HPG, T])
                act.dma_start(cs_bc[:], src).then_inc(bc_in, 16)

            def ssd_silu(g):
                act.wait_ge(conv_done, 4 * (g + 1))
                act.activation(xcv[:], xcv[:], ACT.Silu)
                act.wait_ge(pair_free[(T_SSD + 4) % 2], (T_SSD + 4) // 2 + 1 + 3 * g)
                act.activation(zc[:, 0, :], zc[:, 0, :], ACT.Silu)

            def ssd_small(g, step):
                if step == 0:
                    act.wait_ge(pair_free[(T_SSD + 5) % 2], (T_SSD + 5) // 2 + 1 + 3 * g)
                    act.activation(zc[:, 1, :], zc[:, 1, :], ACT.Silu).then_inc(silu_done, 1)
                if step == 1:
                    act.wait_ge(txs_done, g + 1)
                    wait_count(act, ytok_done, HPG * g)
                    act.activation(xs_tok[:, 0:4, :].rearrange("p (b i) c -> p b (i c)", b=2), sp_[:, 0:2, :], ACT.Copy)
                    act.activation(xs_tok[0:SZ[4], 4, :], sp_[0:SZ[4], 2, 0:256], ACT.Copy).then_inc(xstok_done, 1)
                    for h in range(2):
                        decay(g, h)
                if step == 2:
                    act.wait_ge(tz_done, g + 1)
                    wait_count(act, yz_done, g)
                    act.activation(z_tok[:, 0:4, :].rearrange("p (b i) c -> p b (i c)", b=2), sp_[:, 0:2, :], ACT.Copy)
                    act.activation(z_tok[0:SZ[4], 4, :], sp_[0:SZ[4], 2, 0:256], ACT.Copy).then_inc(ztok_done, 1)
                if step == 3:
                    act.wait_ge(cb_done, g + 1)
                    for b, n, at in BANKS:
                        act.activation(cbs[:, at:at + n], sp_[:, b, 0:n], ACT.Copy)
                    act.activation(cbs[0:SZ[4], FULL:CAUSAL], sp_[0:SZ[4], 2, 416:432], ACT.Copy).then_inc(cbs_done, 1)
                if step == 4:
                    for h in range(2, 4):
                        decay(g, h)
                if step == 5:
                    act.wait_ge(yz_done, g + 1)
                    wait_count(act, yrs_done, g)
                    for i in range(NT):
                        ins = act.activation(x_dt[0:SZ[i], i, :], y_tok[0:SZ[i], i, :], ACT.Square,
                                             accum_out=ssq_tok[0:SZ[i], i:i + 1])
                    ins.then_inc(ysq_done, 1)
                if step == 6:
                    act.wait_ge(tout_done, g + 1)
                    for c in range(2):
                        act.activation(yT[:, 2 * g + c, 0:512], sp_[:, 2 * c, :], ACT.Copy, scale=pcol("ssd_norm", 2 * g + c))
                        ins = act.activation(yT[:, 2 * g + c, 512:T], sp_[:, 2 * c + 1, 0:16], ACT.Copy,
                                             scale=pcol("ssd_norm", 2 * g + c))
                    ins.then_inc(yout_done, 1)

            def decay(g, h):
                act.wait_ge(arg_done, HPG * g + h + 1)
                e = dec[h % 2]
                act.activation(e[:, 0:FULL], e[:, 0:FULL], ACT.Exp)
                act.activation(e[0:SZ[4], FULL:CAUSAL], e[0:SZ[4], FULL:CAUSAL], ACT.Exp).then_inc(e_done, 1)

            for c in range(1, 5):
                split_hi(At(6, 0, W_SSD + c + 2))
                if c == 2:
                    act.wait_ge(cs_done, 1)
                    act.dma_start(cs_d, csr).then_inc(cs_out, 16)
                if c == 3:
                    act.wait_ge(cs_out, 16)
                    load_bc(0)
            ssd_silu(0)

            def ssd_stage(g):
                for c in range(6):
                    if c == 0:
                        ssd_small(g - 1, 0)
                    split_hi(At(6, g, W_SSD + c + 1))
                    if c > 0:
                        ssd_small(g - 1, c)
                    if c == 0 and not (isinstance(g, int) and g < 2):
                        ssd_small(g - 2, 6)
                    if c == 4:
                        act.wait_ge(arg_done, HPG * g)
                        load_bc(g)
                ssd_silu(g)

            ssd_stage(1)
            with act.Fori(2, SSD_GROUPS) as g:
                ssd_stage(g)

            def ret_gate(r, c):
                t = At(8, r, T_RET + 6 + c)
                act.wait_ge(pair_free[t.par], t.half + 1)
                act.activation(gr[:, c, :], gr[:, c, :], ACT.Silu).then_inc(gs_done, 1)

            def ret_small(r, step):
                if step == 1:
                    act.wait_ge(tv_done, r + 1)
                    wait_count(act, o_done, r)
                    act.activation(v_tok[:, 0:4, :].rearrange("p (b i) c -> p b (i c)", b=2), sp_[:, 0:2, :], ACT.Copy)
                    act.activation(v_tok[0:SZ[4], 4, :], sp_[0:SZ[4], 2, 0:256], ACT.Copy).then_inc(vtok_done, 1)

            for c in range(8):
                if c == 0:
                    ssd_small(SSD_GROUPS - 1, 0)
                split_hi(At(8, 0, W_RET + c + 1))
                if 0 < c < 6:
                    ssd_small(SSD_GROUPS - 1, c)
                if c in (0, 6):
                    ssd_small({0: SSD_GROUPS - 2, 6: SSD_GROUPS - 1}[c], 6)
                if c == 6:
                    act.wait_ge(yout_done, SSD_GROUPS)
                    act.dma_start(rope[:], cst_h[:, 5 * P:5 * P + 2 * T].rearrange("p (a t) -> p a t", a=2))\
                       .then_inc(tab_in, 16)
                    act.dma_start(rdec[:], dec_h).then_inc(tab_in, 16)
            ret_gate(0, 0)

            def ret_stage(r):
                for c in range(8):
                    split_hi(At(8, r, W_RET + c + 1))
                    if c == 0:
                        ret_gate(r - 1, 1)
                    if c == 7:
                        ret_gate(r, 0)
                    ret_small(r - 1, c)

            ret_stage(1)
            with act.Fori(2, RET_HEADS) as r:
                ret_stage(r)

            def y_part(dst, tiles, wb):
                for k, y in enumerate(tiles):
                    act.activation(dst[:, k, :], yT[:, y, :], ACT.Copy).then_inc(yhi_done, 1)
                    if k == 3:
                        split_hi(At(0, 0, wb + 1))

            act.wait_ge(unit_done, W_OUT0)
            y_part(hn_hi, EARLY[0], W_OUT0)
            ret_gate(RET_HEADS - 1, 1)
            ret_small(RET_HEADS - 1, 1)
            for c in range(1, 8):
                split_hi(At(0, 0, W_OUT0 + c + 1))

            def project(wb, tb, kt, n, per=2, following=True):
                def tile(i, s, m, last=False):
                    if per == 1 and not last:
                        split_hi(At(2, i, wb + s + 2))
                    if per == 2 and (following or not last):
                        split_hi(At(4, i, wb + 2 * s + 2), KD if last else kt)
                    if per == 2 and not last:
                        split_hi(At(4, i, wb + 2 * s + 3), kt)
                    t = At(2, i, tb + s)
                    act.wait_ge(pair_free[t.par], t.half + 1)
                    square(n, m, s)
                    if following:
                        gained(n, m)

                for s in range(2):
                    tile(0, s, s)
                with act.Fori(1, KD // 2 - 1) as i:
                    for s in range(2):
                        tile(i, s, 2 * i + s)
                tile(KD // 2 - 1, 0, KD - 2)
                tile(KD // 2 - 1, 1, KD - 1, last=True)

            def ffn_in(wb, tb, L):
                def gate(i):
                    act.wait_ge(cg_done, KF * L + i)
                    act.activation(cg[:], cg[:], ACT.Silu).then_inc(sg_done, 1)

                def hid(i):
                    act.wait_ge(hidf_done, KF * L + i)
                    act.activation(hid_hi[:, i - 1, :], hidf[:], ACT.Copy).then_inc(hhi_done, 1)

                split_hi(At(2, 0, wb + 2))

                def pair(i, kt=KD):
                    split_hi(At(2, i, wb + 1))
                    gate(i)
                    split_hi(At(2, i, wb + 2), kt)
                    hid(i)

                pair(1)
                with act.Fori(2, KF - 1) as i:
                    pair(i)
                pair(KF - 1, KH)
                split_hi(At(2, KF, wb + 1), KH)
                gate(KF)
                hid(KF)

            act.wait_ge(yret_done, RET_HEADS)
            y_part(y_hi, LATE[0], W_OUT0 + KD)
            project(W_OUT0 + KD, T_OUT0 + KD, KD, 1, per=1)
            split_hi(At(2, 0, W_FI0 + 1))
            root(1)
            ffn_in(W_FI0, T_FI0, 0)
            project(W_FO0, T_FO0, KH, 2)
            split_hi(At(10, 0, W_L1 + 1))
            root(2)

            act.wait_ge(spl_done, 1)
            ch.link(act.activation(nspt[:], pcol("lru_lam", 0, 8), ACT.Abs))
            ch.link(act.activation(nspt[:], nspt[:], ACT.Exp, scale=-1.0))
            act.activation(nspt[:], nspt[:], ACT.Ln, bias=1.0).then_inc(spl_ln, 1)
            act.wait_ge(spl_done, 2)

            def soft(n, e):
                act.wait_ge(z_done, 2 * n + e + 1)
                for b, w, at in BANKS:
                    act.activation(lbuf[:, at:at + w], sp_[:, b, 0:w], ACT.Abs)
                ch.link(act.activation(lbuf[0:SZ[4], FULL:CAUSAL], sp_[0:SZ[4], 2, 416:432], ACT.Abs))
                act.activation(lbuf[:, 0:FULL], lbuf[:, 0:FULL], ACT.Exp, scale=-1.0)
                ch.link(act.activation(lbuf[0:SZ[4], FULL:CAUSAL], lbuf[0:SZ[4], FULL:CAUSAL], ACT.Exp, scale=-1.0))
                for b, w, at in BANKS:
                    if b == 2:
                        act.activation(lbuf[0:SZ[4], FULL:CAUSAL], lbuf[0:SZ[4], FULL:CAUSAL], ACT.Ln, bias=1.0)
                    act.activation(lbuf[:, at:at + w], lbuf[:, at:at + w], ACT.Ln, bias=1.0).then_inc(l_done, 1)
                for b, w, at in BANKS:
                    act.wait_ge(sum_done, 3 * (2 * n + e) + b + 1)
                    if b == 2:
                        act.activation(sp_hi[0:SZ[4], FULL:CAUSAL], spb[0:SZ[4], FULL:CAUSAL], ACT.Copy)
                    act.activation(sp_hi[:, at:at + w], spb[:, at:at + w], ACT.Copy).then_inc(sphi_done, 1)

            def load_exp():
                act.activation(idle_a[:, 0:1], eps_col[:], ACT.Exp)

            def weigh(n, e):
                act.wait_ge(suf_done, 2 * n + e + 1)
                wait_count(act, pv_done, 2 * n + e - 1)
                for b, w, at in BANKS:
                    act.activation(wts[e][:, at:at + w], sp_[:, b, 0:w], ACT.Exp)
                act.activation(wts[e][0:SZ[4], FULL:CAUSAL], sp_[0:SZ[4], 2, 416:432], ACT.Exp).then_inc(w_done, 1)

            def l1_gates(n):
                act.wait_ge(gates_done, n + 1)
                wait_count(act, ylru_done, n)
                for dst, gate, (b0, b1, c1) in ((tr, 0, (0, 1, 0)), (ti, 1, (2, 1, 16))):
                    act.activation(dst[:, 0:512], sp_[:, b0, 0:512], ACT.Tanh, scale=0.5, bias=hb_col(gate, n))
                    ins = act.activation(dst[:, 512:T], sp_[:, b1, c1:c1 + 16], ACT.Tanh, scale=0.5,
                                         bias=hb_col(gate, n))
                ins.then_inc(tri_done, 1)
                act.wait_ge(tri_done, n + 1)
                act.activation(lt[:], tr, ACT.Tanh, scale=nsp_col(n), bias=nsp_col(n))
                act.activation(la[:], tr, ACT.Exp, scale=nsp_col(n), bias=nsp_col(n)).then_inc(la_done, 1)
                act.wait_ge(gu_done, n + 1)
                act.activation(ge[:], ge[:], ACT.Tanh, scale=GELU_C).then_inc(gth_done, 1)

            def l1_v(n):
                act.wait_ge(tvs_done, n + 1)
                wait_count(act, pv_done, 2 * n)
                act.activation(sv_tok[:, 0:4, :], sp_[:, 3, :].rearrange("p (i c) -> p i c", c=P), ACT.Copy)
                act.wait_ge(z_done, 2 * n + 1)
                for e, (bk, c0) in enumerate(V_LAST):
                    ins = act.activation(sv_tok[0:SZ[4], 4, HEAD * e:HEAD * (e + 1)], sp_[0:SZ[4], bk, c0:c0 + HEAD],
                                         ACT.Copy)
                ins.then_inc(svtok_done, 1)

            def l1_heads_out(n, following=True):
                act.wait_ge(tso_done, n + 1)
                act.activation(yT[:, n, 0:512], sp_[:, 3, :], ACT.Copy)
                if following:
                    act.wait_ge(gates_done, n + 2)
                act.activation(yT[:, n, 512:T], sp_[:, 1, 32:48], ACT.Copy).then_inc(ysb_done, 1)

            def hb_col(gate, n):
                return hb[:, gate, bass.ds(n, 1)]

            def nsp_col(n):
                return nsp[:, bass.ds(n, 1)]

            for c in range(1, 5):
                split_hi(At(10, 0, W_L1 + c + 1))

            def l1_block(i, b, early=False):
                n = 2 * i + b

                def split(c):
                    split_hi(At(10, i, W_L1 + 5 * (b + 1) + c))

                before = not (isinstance(n, int) and n == 0)
                if before:
                    weigh(n - 1, 1)
                if early:
                    act.wait_ge(unit_done, W_OUT1)
                    y_part(hn_hi, EARLY[1], W_OUT1)
                else:
                    split(1)
                if before:
                    l1_heads_out(n - 1)
                l1_gates(n)
                split(2)
                l1_v(n)
                soft(n, 0)
                split(3)
                split(4)
                load_exp()
                weigh(n, 0)
                soft(n, 1)
                split(5)
                act.wait_ge(lb_done, n + 1)
                act.activation(lb[:], lb[:], ACT.Sqrt, scale=0.25).then_inc(root1_done, 1)
                load_exp()

            for b in range(2):
                l1_block(0, b)
            with act.Fori(1, 3) as i:
                ch.enter(i, 1, 8)
                for b in range(2):
                    l1_block(i, b)
            ch.leave(1, 3)
            l1_block(3, 0)
            l1_block(3, 1, early=True)
            weigh(7, 1)
            split_hi(At(0, 0, W_OUT1 + 6))
            l1_heads_out(7, following=False)
            split_hi(At(0, 0, W_OUT1 + 7))
            split_hi(At(0, 0, W_OUT1 + 8))
            act.wait_ge(ysb_done, 8)
            act.wait_ge(ylru_done, 8)
            y_part(y_hi, LATE[1], W_OUT1 + KD)
            project(W_OUT1 + KD, T_OUT1 + KD, KD, 3, per=1)
            split_hi(At(2, 0, W_FI1 + 1))
            root(3)
            ffn_in(W_FI1, T_FI1, 1)
            project(W_FO1, T_FO1, KH, 4, following=False)
            root(4)

        @block.vector
        def _(ve):
            ch = Chain(ve, v_seq)

            def split_lo(w, kt=KD):
                ve.wait_ge(hi_done, w.v + 1)
                n = slice(0, kt * P)
                ve.tensor_tensor(wlo[w.par][:, n], raw[w.par][:, n], whi[w.par][:, n].bitcast(f32),
                                 ALU.subtract).then_inc(lo_done, 1)
                ve.wait_ge(lo_done, w.v + 1)

            def gained(n, m):
                ve.wait_ge(nhi_done, KD * n + m + 1)
                ve.scalar_tensor_tensor(hn_lo[:, m, :], hT[:, m, :], pcol(NORMS[n], m), hn_hi[:, m, :].bitcast(f32),
                                        ALU.mult, ALU.subtract).then_inc(nlo_done, 1)

            def add_squares(n, m, s, first=False):
                ve.wait_ge(sq_done, KD * n + m + 1)
                if first:
                    wait_count(ve, ssq_done, n)
                    ve.tensor_copy(acc[:], sq[:, s, :]).then_inc(acc_done, 1)
                else:
                    ve.wait_ge(acc_done, KD * n + m)
                    ve.tensor_tensor(acc[:], acc[:], sq[:, s, :], ALU.add).then_inc(acc_done, 1)

            def invert(n):
                ve.wait_ge(root_done, n + 1)
                ve.reciprocal(rstd[:], rstd[:]).then_inc(rstd_done, 1)
                ve.wait_ge(rstd_done, n + 1)

            def evacuate(w, t, dst, scale=None):
                ve.wait_ge(unit_done, w.v + 1)
                if scale is None:
                    ins = ve.tensor_tensor(dst, gout(t.par), halves(rstd[:]), ALU.mult)
                else:
                    ins = ve.scalar_tensor_tensor(dst, gout(t.par), scale, halves(rstd[:]), ALU.mult, ALU.mult)
                ins.then_inc(pair_free[t.par], 1)

            def conv(dst, src, taps, w0, b0, link, done):
                link(ve.tensor_scalar(dst, src[:, taps - 1:taps - 1 + T], w0(taps - 1), b0, ALU.mult, ALU.add))
                for k in range(taps - 2, -1, -1):
                    ins = ve.scalar_tensor_tensor(dst, src[:, k:k + T], w0(k), dst, ALU.mult, ALU.add)
                    if k:
                        link(ins)
                ins.then_inc(done, 1)

            for s in range(2):
                ve.memset(ub[:, s, 0:3], 0.0)
            ve.memset(neg_half[:], -0.5)
            ve.memset(one_row, 1.0)
            ve.memset(eps_col[:], EPS).then_inc(prep_done, 1)
            ve.wait_ge(vec_in, 16)
            for m in range(KD):
                if m % 2 == 0:
                    ve.wait_ge(h_in[m // 2], 16)
                gained(0, m)
                if m == 0:
                    split_lo(At(0, 0, 0))
                add_squares(0, m, m % 2, first=m == 0)
            split_lo(At(0, 0, 1))
            ve.wait_ge(const_in, 16)
            ve.tensor_copy(ident_b[:], ident)
            ve.tensor_copy(never[:], cst[:, 4 * P:5 * P])
            ve.tensor_copy(neg_r[:], cst[:, 2 * P:4 * P].rearrange("p (a c) -> p a c", a=2))
            split_lo(At(6, 0, W_SSD + 1))
            invert(0)

            ve.wait_ge(unit_done, 1)
            ve.tensor_tensor(halves(dtx), gp[0][0:16, :, 0:H2], halves(rstd[0:16, :]),
                             ALU.mult).then_inc(pair_free[0], 1)
            ve.wait_ge(pair_free[0], 1)
            ve.tensor_scalar(dtx, dtx, pcol("ssd_dtb", rows=16), None, ALU.add).then_inc(dtx_done, 1)
            def ssd_tile(g, c):
                w, t = At(6, g, W_SSD + c), At(6, g, T_SSD + c)
                if c >= 4:
                    wait_count(ve, tz_done, g)
                    evacuate(w, t, halves(zc[:, c - 4, :]))
                    return
                wait_count(ve, conv_done, 4 * g + c - 1)
                evacuate(w, t, halves(ub[:, c % 2, 3:3 + T]))

            def ssd_conv(g, c):
                t = At(6, g, T_SSD + c)
                ve.wait_ge(pair_free[t.par], t.half + 1)
                ct = 2 * g + c if c < 2 else (8 + g if c == 2 else 12 + g)
                wait_count(ve, txs_done if c < 2 else cb_done, g)
                conv(xcv[:, c, :], ub[:, c % 2, :], 4, lambda k: pcol("ssd_cw", 4 * ct + k), pcol("ssd_cb", ct),
                     ch.link, conv_done)

            def bc4(ap, n):
                return ap.unsqueeze(3).to_broadcast([n, ap.shape[1], HPG, HEAD])

            def heads(ap):
                return ap.rearrange("p i (h d) -> p i h d", h=HPG)

            def ssd_small(g, step):
                if step == 1:
                    for h in range(2):
                        args(g, h)
                    ve.wait_ge(xstok_done, g + 1)
                    wait_count(ve, y_done, HPG * g)
                    dts = dt_tok[:, :, bass.ds(HPG * g, HPG)]
                    ve.tensor_tensor(heads(x_dt[:, 0:4, :]), heads(xs_tok[:, 0:4, :]), bc4(dts[:, 0:4, :], P), ALU.mult)
                    ch.link(ve.tensor_tensor(heads(x_dt[0:SZ[4], 4:5, :]), heads(xs_tok[0:SZ[4], 4:5, :]),
                                             bc4(dts[0:SZ[4], 4:5, :], SZ[4]), ALU.mult))
                    skip = pcol("ssd_d", HPG * g, HPG).unsqueeze(1).to_broadcast([P, 4, HPG])
                    ve.tensor_tensor(heads(xs_tok[:, 0:4, :]), heads(xs_tok[:, 0:4, :]), bc4(skip, P), ALU.mult)
                    ch.link(ve.tensor_tensor(heads(xs_tok[0:SZ[4], 4:5, :]), heads(xs_tok[0:SZ[4], 4:5, :]),
                                             bc4(skip[0:SZ[4], 0:1, :], SZ[4]), ALU.mult))
                if step in (3, 4):
                    for h in ((0, 1) if step == 3 else (2, 3)):
                        ve.wait_ge(es_done, HPG * g + h + 1)
                        ve.wait_ge(cbs_done, g + 1)
                        e = dec[h % 2]
                        ve.tensor_tensor(e[:, 0:FULL], e[:, 0:FULL], cbs[:, 0:FULL], ALU.mult)
                        ve.tensor_tensor(e[0:SZ[4], FULL:CAUSAL], e[0:SZ[4], FULL:CAUSAL], cbs[0:SZ[4], FULL:CAUSAL],
                                         ALU.mult).then_inc(m_done, 1)
                if step == 5:
                    take(g, 2)
                    take(g, 3)
                    ve.wait_ge(ytok_done, HPG * (g + 1))
                    ve.wait_ge(ztok_done, g + 1)
                    ve.tensor_tensor(y_tok[:, 0:4, :], y_tok[:, 0:4, :], z_tok[:, 0:4, :], ALU.mult)
                    ve.tensor_tensor(y_tok[0:SZ[4], 4, :], y_tok[0:SZ[4], 4, :], z_tok[0:SZ[4], 4, :],
                                     ALU.mult).then_inc(yz_done, 1)
                if step == 6:
                    ve.wait_ge(yrs_done, g + 1)
                    for i in range(NT):
                        ins = ve.tensor_scalar(y_tok[0:SZ[i], i, :], y_tok[0:SZ[i], i, :], rs_tok[0:SZ[i], i:i + 1],
                                               None, ALU.mult)
                    ins.then_inc(yn_done, 1)

            def ssd_heads(g):
                for h in range(2):
                    take(g, h)
                    args(g, h + 2)

            def args(g, h):
                if h == 0:
                    ve.wait_ge(bc_in, 16 * (g + 1))
                wait_count(ve, y_done, HPG * g + h - 1)
                for j in range(NT):
                    ins = ve.tensor_scalar(dec[h % 2][0:SZ[j], OFF[j]:OFF[j] + WJ[j]], cs_bc[0:SZ[j], h, P * j:T],
                                           ncs_tok[0:SZ[j], j, bass.ds(HPG * g + h, 1)], 0.0, ALU.add, ALU.min)
                ins.then_inc(arg_done, 1)

            def take(g, h):
                ve.wait_ge(y_done, HPG * g + h + 1)
                if h == 0:
                    wait_count(ve, tout_done, g)
                c = slice(HEAD * h, HEAD * (h + 1))
                ve.tensor_tensor(y_tok[:, 0:4, c], sp_[:, h, 0:256].rearrange("p (i d) -> p i d", d=HEAD),
                                 xs_tok[:, 0:4, c], ALU.add)
                ve.tensor_tensor(y_tok[0:SZ[4], 4, c], sp_[0:SZ[4], h, 256:320], xs_tok[0:SZ[4], 4, c],
                                 ALU.add).then_inc(ytok_done, 1)

            for c in range(5):
                split_lo(At(6, 0, W_SSD + c + 2))
                ssd_tile(0, c)
                if c == 3:
                    ve.wait_ge(dtT_done, 1)
                    for n, (dst, sign) in enumerate(((dt_tok, 1.0), (ncs_tok, -1.0))):
                        ve.tensor_scalar(dst[:, 0:4, :], sp_[:, 2, 80 * n:80 * n + 64].rearrange("p (i h) -> p i h", h=16),
                                         sign, None, ALU.mult)
                        ins = ve.tensor_scalar(dst[0:SZ[4], 4, :], sp_[0:SZ[4], 2, 80 * n + 64:80 * n + 80], sign, None,
                                               ALU.mult)
                    ins.then_inc(dtok_done, 1)
                if c < 4:
                    ssd_conv(0, c)
                if c == 0:
                    ve.wait_ge(dtl_done, 1)
                    ch.link(ve.scalar_tensor_tensor(dtx, dtx, 0.0, dtl, ALU.max, ALU.add))
                    ve.wait_ge(aexp_done, 1)
                    ch.link(ve.tensor_scalar(dtl, dtx, aexp[:, 0:1], -1.0, ALU.mult, ALU.mult))
                    ve.tensor_tensor_scan(csr, one_row, dtl, 0.0, ALU.mult, ALU.add).then_inc(cs_done, 1)

            def ssd_slot(g, c, w, tile, conv_):
                if c == 3:
                    ssd_small(g, 3)
                    split_lo(w)
                    tile(2)
                    ssd_heads(g)
                elif c == 4:
                    split_lo(w)
                    ssd_small(g, 4)
                    tile(3)
                    conv_(2)
                elif c == 5:
                    ssd_small(g, 5)
                    split_lo(w)
                    tile(4)
                    conv_(3)
                else:
                    if c == 0:
                        tile(-1)
                    split_lo(w)
                    if c > 0:
                        tile(c - 1)
                    if c in (1, 2):
                        conv_(c - 1)
                    if c < 3:
                        ssd_small(g, c)

            def ssd_stage(g):
                for c in range(6):
                    if c == 0 and not (isinstance(g, int) and g < 2):
                        ssd_small(g - 2, 6)
                    ssd_slot(g - 1, c, At(6, g, W_SSD + c + 1),
                             lambda t: ssd_tile(g - 1, 5) if t < 0 else ssd_tile(g, t), lambda t: ssd_conv(g, t))

            ve.wait_ge(dtok_done, 1)
            ssd_stage(1)
            with ve.Fori(2, SSD_GROUPS) as g:
                ch.enter(g, 2, 14)
                ssd_stage(g)
            ch.leave(2, SSD_GROUPS)


            def ret_tile(r, c):
                if c < 2:
                    wait_count(ve, rot_done, 2 * r - 1)
                elif c < 4:
                    wait_count(ve, rot_done, 2 * r)
                elif c < 6:
                    wait_count(ve, tv_done, r)
                else:
                    wait_count(ve, yret_done, r)
                evacuate(At(8, r, W_RET + c), At(8, r, T_RET + c), halves((qr, kr, vr, gr)[c // 2][:, c % 2, :]))

            def rotate(r, dst, src, last_tile, link):
                t = At(8, r, T_RET + last_tile)
                ve.wait_ge(pair_free[t.par], t.half + 1)
                wait_count(ve, sc_done, r)
                cos, sin = rope[:, 0, :], rope[:, 1, :]
                ve.tensor_tensor(rt[:], src[:, 1, :], sin, ALU.mult)
                link(ve.tensor_tensor(dst[:, 0, :], src[:, 0, :], cos, ALU.mult))
                link(ve.tensor_tensor(dst[:, 0, :], dst[:, 0, :], rt[:], ALU.subtract))
                ve.tensor_tensor(rt[:], src[:, 1, :], cos, ALU.mult)
                link(ve.tensor_tensor(dst[:, 1, :], src[:, 0, :], sin, ALU.mult))
                ve.tensor_tensor(dst[:, 1, :], dst[:, 1, :], rt[:], ALU.add).then_inc(rot_done, 1)

            def ret_small(r, step):
                if step == 2:
                    ve.wait_ge(sc_done, r + 1)
                    wait_count(ve, o_done, r)
                    for j, q0, n, b, c0, at in PIECES:
                        d0 = q0 - P * j
                        ins = ve.tensor_tensor(sdec[0:SZ[j], at:at + n], sp_[0:SZ[j], b, c0:c0 + n],
                                               rdec[0:SZ[j], r, d0:d0 + n], ALU.mult)
                    ins.then_inc(sdec_done, 1)
                if step == 4:
                    ve.wait_ge(o_done, r + 1)
                    wait_count(ve, tro_done, r)
                    for i in range(NT):
                        ins = ve.bn_stats(stats[0:SZ[i], i, :], sp_[0:SZ[i], i // 2, (i % 2) * 256:(i % 2) * 256 + 256])
                    ch.link(ins)
                    ve.tensor_copy(idle_v[:, 0:1], eps_col[:])
                    for i in range(NT):
                        ins = ve.bn_aggr(mv[0:SZ[i], i, :], stats[0:SZ[i], i, :])
                    ins.then_inc(mv_done, 1)
                    ve.wait_ge(rrs_done, r + 1)
                    for i in range(NT):
                        ins = ve.tensor_scalar(o_tok[0:SZ[i], i, :], sp_[0:SZ[i], i // 2, (i % 2) * 256:(i % 2) * 256 + 256],
                                               mv[0:SZ[i], i, 0:1], ret_rs[0:SZ[i], i:i + 1], ALU.subtract, ALU.mult)
                    ins.then_inc(on_done, 1)
                if step == 6:
                    ve.wait_ge(gs_done, 2 * (r + 1))
                    ve.wait_ge(tro_done, r + 1)
                    for c in range(2):
                        gain = pcol("ret_norm", 2 * r + c)
                        ve.scalar_tensor_tensor(yT[:, 8 + 2 * r + c, 0:512], sp_[:, 2 * c, :], gain, gr[:, c, 0:512],
                                                ALU.mult, ALU.mult)
                        ins = ve.scalar_tensor_tensor(yT[:, 8 + 2 * r + c, 512:T], sp_[:, 2 * c + 1, 0:16], gain,
                                                      gr[:, c, 512:T], ALU.mult, ALU.mult)
                    ins.then_inc(yret_done, 1)

            def ret_stage(r):
                for c in range(8):
                    split_lo(At(8, r, W_RET + c + 1))
                    if c == 0:
                        ret_tile(r - 1, 7)
                        if isinstance(r, int) and r == 1:
                            ve.wait_ge(rot_done, 1)
                            rotate(0, rk, kr, 3, ch.link)
                    else:
                        ret_tile(r, c - 1)
                    if c == 2:
                        rotate(r, rq, qr, 1, ch.link)
                    if c == 4:
                        rotate(r, rk, kr, 3, ch.link)
                    ret_small(r - 1, c)

            for c in range(8):
                if c in (0, 6):
                    ssd_small({0: SSD_GROUPS - 2, 6: SSD_GROUPS - 1}[c], 6)
                ssd_slot(SSD_GROUPS - 1, c, At(8, 0, W_RET + c + 1),
                         lambda t: ssd_tile(SSD_GROUPS - 1, 5) if t < 0 else ret_tile(0, t), lambda t: None)
            ve.wait_ge(yout_done, SSD_GROUPS)
            ve.memset(ret_nh[:], -0.5).then_inc(prep_done, 1)
            ve.wait_ge(tab_in, 32)
            rotate(0, rq, qr, 1, ch.link)
            ret_stage(1)
            with ve.Fori(2, RET_HEADS) as r:
                ch.enter(r, 2, 7)
                ret_stage(r)
            ch.leave(2, RET_HEADS)

            def y_part(dst_hi, dst_lo, tiles, wb, count):
                for k, y in enumerate(tiles):
                    ve.wait_ge(yhi_done, count + k + 1)
                    ve.tensor_tensor(dst_lo[:, k, :], yT[:, y, :], dst_hi[:, k, :].bitcast(f32),
                                     ALU.subtract).then_inc(ylo_done, 1)
                    if k == 3:
                        split_lo(At(0, 0, wb + 1))

            def add_tile(w, t, m):
                ve.wait_ge(unit_done, w.v + 1)
                ve.tensor_tensor(halves(hT[:, m, :]), gout(t.par), halves(hT[:, m, :]), ALU.add)\
                  .then_inc(pair_free[t.par], 1)

            ret_tile(RET_HEADS - 1, 7)
            y_part(hn_hi, hn_lo, EARLY[0], W_OUT0, 0)
            for c in range(1, 8):
                split_lo(At(0, 0, W_OUT0 + c + 1))
                add_tile(At(0, 0, W_OUT0 + c - 1), At(0, 0, T_OUT0 + c - 1), c - 1)
                if c in (2, 4, 6):
                    ret_small(RET_HEADS - 1, c)
            add_tile(At(0, 0, W_OUT0 + 7), At(0, 0, T_OUT0 + 7), 7)

            def project(wb, tb, kt, n, per=2, following=True):
                def tile(i, s, m, last=False):
                    if per == 1 and not last:
                        split_lo(At(2, i, wb + s + 2))
                    if per == 2 and (following or not last):
                        split_lo(At(4, i, wb + 2 * s + 2), KD if last else kt)
                    if per == 2 and not last:
                        split_lo(At(4, i, wb + 2 * s + 3), kt)
                    add_tile(At(2 * per, i, wb + per * s + per - 1), At(2, i, tb + s), m)
                    add_squares(n, m, s, first=isinstance(m, int) and m == 0)
                    if following:
                        gained(n, m)

                for s in range(2):
                    tile(0, s, s)
                with ve.Fori(1, KD // 2 - 1) as i:
                    for s in range(2):
                        tile(i, s, 2 * i + s)
                tile(KD // 2 - 1, 0, KD - 2)
                tile(KD // 2 - 1, 1, KD - 1, last=True)

            def ffn_in(wb, tb, L):
                def f_conv(i, half, dst, done):
                    t = At(2, i, tb + half)
                    wait_count(ve, (cg_done, cu_done)[half], KF * L + i)
                    evacuate(At(2, i, wb + half), t, halves(ubf[half][:, 2:2 + T]))
                    ve.wait_ge(pair_free[t.par], t.half + 1)
                    ct = i + KF * half
                    conv(dst[:], ubf[half], 3, lambda k: pcol(f"f{L}_cw", 3 * ct + k), pcol(f"f{L}_cb", ct),
                         ch.link, done)

                def slot_a(i):
                    f_conv(i - 1, 1, cu, cu_done)
                    ve.wait_ge(cu_done, KF * L + i)
                    ve.wait_ge(sg_done, KF * L + i)
                    ve.tensor_tensor(hidf[:], cg[:], cu[:], ALU.mult).then_inc(hidf_done, 1)

                def lo(i):
                    ve.wait_ge(hhi_done, KF * L + i)
                    ve.tensor_tensor(hid_lo[:, i - 1, :], hidf[:], hid_hi[:, i - 1, :].bitcast(f32),
                                     ALU.subtract).then_inc(hlo_done, 1)

                ve.wait_ge(unit_done, wb)
                for s in range(2):
                    ins = ve.memset(ubf[s][:, 0:2], 0.0)
                ch.link(ins)
                split_lo(At(2, 0, wb + 2))
                f_conv(0, 0, cg, cg_done)

                def pair(i, kt=KD):
                    split_lo(At(2, i, wb + 1))
                    slot_a(i)
                    split_lo(At(2, i, wb + 2), kt)
                    f_conv(i, 0, cg, cg_done)
                    lo(i)

                pair(1)
                with ve.Fori(2, KF - 1) as i:
                    ch.enter(i, 2, 4)
                    pair(i)
                ch.leave(2, KF - 1)
                pair(KF - 1, KH)
                split_lo(At(2, KF, wb + 1), KH)
                slot_a(KF)
                lo(KF)

            y_part(y_hi, y_lo, LATE[0], W_OUT0 + KD, KD)
            project(W_OUT0 + KD, T_OUT0 + KD, KD, 1, per=1)
            split_lo(At(2, 0, W_FI0 + 1))
            invert(1)
            ffn_in(W_FI0, T_FI0, 0)
            project(W_FO0, T_FO0, KH, 2)
            split_lo(At(10, 0, W_L1 + 1))
            invert(2)

            ch.link(ve.memset(ubx[:, 0:3], 0.0))
            ve.tensor_scalar(hb[:, 0, :], pcol("lru_ba", 0, 8), 0.5, None, ALU.mult)
            ve.tensor_scalar(hb[:, 1, :], pcol("lru_bx", 0, 8), 0.5, None, ALU.mult)
            ve.tensor_scalar(nsp[:], pcol("lru_lam", 0, 8), -1.0, 0.0, ALU.mult, ALU.max).then_inc(spl_done, 1)
            ve.wait_ge(spl_ln, 1)
            ve.wait_ge(spl_done, 1)
            ch.link(ve.tensor_tensor(nsp[:], nsp[:], nspt[:], ALU.add))
            ve.tensor_scalar(nsp[:], nsp[:], -0.5 * LRU_C, None, ALU.mult).then_inc(spl_done, 1)

            def soft(n, e):
                for b, w, at in BANKS:
                    ve.wait_ge(l_done, 3 * (2 * n + e) + b + 1)
                    if b == 2:
                        ve.scalar_tensor_tensor(spb[0:SZ[4], FULL:CAUSAL], sp_[0:SZ[4], 2, 416:432], 0.0,
                                                lbuf[0:SZ[4], FULL:CAUSAL], ALU.max, ALU.add)
                    ve.scalar_tensor_tensor(spb[:, at:at + w], sp_[:, b, 0:w], 0.0, lbuf[:, at:at + w], ALU.max,
                                            ALU.add).then_inc(sum_done, 1)
                for b, w, at in BANKS:
                    ve.wait_ge(sphi_done, 3 * (2 * n + e) + b + 1)
                    if b == 2:
                        ve.tensor_tensor(sp_lo[0:SZ[4], FULL:CAUSAL], spb[0:SZ[4], FULL:CAUSAL],
                                         sp_hi[0:SZ[4], FULL:CAUSAL].bitcast(f32), ALU.subtract)
                    ins = ve.tensor_tensor(sp_lo[:, at:at + w], spb[:, at:at + w], sp_hi[:, at:at + w].bitcast(f32),
                                           ALU.subtract)
                ins.then_inc(spf_done, 1)

            def take_head(n, e):
                ve.wait_ge(pv_done, 2 * n + e + 1)
                if e == 0:
                    wait_count(ve, tso_done, n)
                c = slice(HEAD * e, HEAD * (e + 1))
                ve.tensor_copy(so_tok[:, 0:4, c], sp_[:, 3, 0:256].rearrange("p (i d) -> p i d", d=HEAD))
                ve.tensor_copy(so_tok[0:SZ[4], 4, c], sp_[0:SZ[4], 3, 256:320]).then_inc(so_done, 1)

            def l1_tile(i, b, c):
                n = 2 * i + b
                w, t = At(10, i, W_L1 + 5 * b + c), At(10, i, T_L1 + 5 * b + c)
                if c < 2:
                    wait_count(ve, z_done, 2 * n - 2)
                if c == 2:
                    wait_count(ve, tvs_done, n)
                if c == 4:
                    wait_count(ve, xc_done, n)
                dst = (qs[b % 2][:], ks[b % 2][:], vs, gt, ubx[:, 3:3 + T])[c]
                evacuate(w, t, halves(dst), SB_SCALE if c == 0 else None)

            def lru_in(i, b):
                n = 2 * i + b
                t = At(10, i, T_L1 + 5 * b + 4)
                ve.wait_ge(pair_free[t.par], t.half + 1)
                wait_count(ve, gates_done, n)
                conv(xc, ubx, 4, lambda k: pcol("lru_cw", 4 * n + k), pcol("lru_cb", n), ch.link, xc_done)

            def gelu_in(n):
                wait_count(ve, ylru_done, n)
                ch.link(ve.tensor_tensor(ge[:], gt, gt, ALU.mult))
                ch.link(ve.tensor_scalar(ge[:], ge[:], 0.044715, 1.0, ALU.mult, ALU.add))
                ve.tensor_tensor(ge[:], ge[:], gt, ALU.mult).then_inc(gu_done, 1)

            def lru_var(n):
                ve.wait_ge(la_done, n + 1)
                ve.scalar_tensor_tensor(ti[:], ti[:], 1.0, xc, ALU.add, ALU.mult)
                ch.link(ve.tensor_scalar(lb[:], lt[:], -1.0, 1.0, ALU.mult, ALU.add))
                ch.link(ve.reciprocal(lb[:], lb[:]))
                ch.link(ve.scalar_tensor_tensor(lb[:], lt[:], -2.0, lb[:], ALU.mult, ALU.mult))
                ve.tensor_scalar(lb[:], lb[:], 0.0, None, ALU.max).then_inc(lb_done, 1)

            def gelu_out(n):
                ve.wait_ge(gth_done, n + 1)
                ch.link(ve.scalar_tensor_tensor(ge[:], ge[:], 1.0, gt, ALU.add, ALU.mult))

            def lru_out(n):
                ve.wait_ge(root1_done, n + 1)
                ch.link(ve.tensor_tensor(lb[:], lb[:], ti[:], ALU.mult))
                ch.link(ve.tensor_tensor_scan(tr, la[:], lb[:], 0.0, ALU.mult, ALU.add))
                ve.scalar_tensor_tensor(yT[:, 8 + n, :], ge[:], 0.5, tr, ALU.mult, ALU.mult).then_inc(ylru_done, 1)

            for c in range(4):
                if c > 0:
                    split_lo(At(10, 0, W_L1 + c + 1))
                l1_tile(0, 0, c)
            split_lo(At(10, 0, W_L1 + 5))

            def l1_block(i, b, early=False):
                n = 2 * i + b

                def split(c):
                    split_lo(At(10, i, W_L1 + 5 * (b + 1) + c))

                def tile(c):
                    if early:
                        add_tile(At(0, 0, W_OUT1 + c), At(0, 0, T_OUT1 + c), c)
                    else:
                        l1_tile(i, b + 1, c)

                l1_tile(i, b, 4)
                if early:
                    y_part(hn_hi, hn_lo, EARLY[1], W_OUT1, 2 * KD)
                    lru_in(i, b)
                else:
                    lru_in(i, b)
                    split(1)
                if not (isinstance(n, int) and n == 0):
                    take_head(n - 1, 1)
                    lru_out(n - 1)
                gelu_in(n)
                split(2)
                tile(0)
                soft(n, 0)
                split(3)
                tile(1)
                lru_var(n)
                split(4)
                tile(2)
                gelu_out(n)
                take_head(n, 0)
                tile(3)
                soft(n, 1)
                split(5)

            for b in range(2):
                l1_block(0, b)
            with ve.Fori(1, 3) as i:
                ch.enter(i, 1, 22)
                for b in range(2):
                    l1_block(i, b)
            ch.leave(1, 3)
            l1_block(3, 0)
            l1_block(3, 1, early=True)
            add_tile(At(0, 0, W_OUT1 + 4), At(0, 0, T_OUT1 + 4), 4)
            take_head(7, 1)
            split_lo(At(0, 0, W_OUT1 + 6))
            lru_out(7)
            for c in (5, 6):
                add_tile(At(0, 0, W_OUT1 + c), At(0, 0, T_OUT1 + c), c)
                split_lo(At(0, 0, W_OUT1 + c + 2))
            add_tile(At(0, 0, W_OUT1 + 7), At(0, 0, T_OUT1 + 7), 7)
            y_part(y_hi, y_lo, LATE[1], W_OUT1 + KD, 3 * KD)
            project(W_OUT1 + KD, T_OUT1 + KD, KD, 3, per=1)
            split_lo(At(2, 0, W_FI1 + 1))
            invert(3)
            ffn_in(W_FI1, T_FI1, 1)
            project(W_FO1, T_FO1, KH, 4, following=False)
            invert(4)
            for m in range(KD):
                ve.scalar_tensor_tensor(yT[:, m, :], hT[:, m, :], pcol("final", m), rstd[:], ALU.mult,
                                        ALU.mult).then_inc(final_done, 1)

        @block.gpsimd
        def _(po):
            ch = Chain(po, g_seq)

            def await_count(sem_, n, k=0):
                po.wait_ge(sem_, n)
                po.tensor_tensor(idle_g[:, k:k + 1], eps_col[:], eps_col[:], ALU.mult)

            def mask(buf, done):
                for j in range(NT):
                    blk = buf[0:SZ[j], OFF[j]:OFF[j] + SZ[j]]
                    ins = po.affine_select(out=blk, in_=blk, compare_op=ALU.is_ge, fill=0.0, base=0,
                                           pattern=[[1, SZ[j]]], channel_multiplier=-1)
                ins.then_inc(done, 1)

            po.wait_ge(prep_done, 1)
            with po.Fori(0, SSD_GROUPS) as g:
                ch.enter(g, 0, 1)
                for h in range(HPG):
                    await_count(e_done, HPG * g + h + 1, h)
                    mask(dec[h % 2], es_done)
                await_count(ysq_done, g + 1, 4)
                po.tensor_scalar(rs_tok[:, 0:4], ssq_tok[:, 0:4], 1.0 / 256, EPS, ALU.mult, ALU.add)
                ch.link(po.tensor_scalar(rs_tok[0:SZ[4], 4:5], ssq_tok[0:SZ[4], 4:5], 1.0 / 256, EPS, ALU.mult, ALU.add))
                po.tensor_tensor(rs_tok[:, 0:4], rs_tok[:, 0:4], neg_half[:, 0:4], ALU.pow)
                po.tensor_tensor(rs_tok[0:SZ[4], 4:5], rs_tok[0:SZ[4], 4:5], neg_half[0:SZ[4], 4:5],
                                 ALU.pow).then_inc(yrs_done, 1)
            ch.leave(0, SSD_GROUPS)
            po.wait_ge(prep_done, 2)
            with po.Fori(0, RET_HEADS) as r:
                ch.enter(r, 0, 1)
                await_count(mv_done, r + 1, 5)
                po.tensor_scalar(ret_rs[:, 0:4], mv[:, 0:4, 1], 1.0, EPS, ALU.mult, ALU.add)
                ch.link(po.tensor_scalar(ret_rs[0:SZ[4], 4:5], mv[0:SZ[4], 4:5, 1], 1.0, EPS, ALU.mult, ALU.add))
                po.tensor_tensor(ret_rs[:, 0:4], ret_rs[:, 0:4], ret_nh[:, 0:4], ALU.pow)
                po.tensor_tensor(ret_rs[0:SZ[4], 4:5], ret_rs[0:SZ[4], 4:5], ret_nh[0:SZ[4], 4:5],
                                 ALU.pow).then_inc(rrs_done, 1)
            ch.leave(0, RET_HEADS)


def kernel(**inputs):
    import numpy as np
    import concourse.bacc as bacc
    from concourse.bass_utils import run_bass_kernel_spmd as run

    a = {k: np.asarray(v) for k, v in inputs.items()}

    def units(w, cols, kts):
        res = []
        for c in cols:
            k0 = 0
            for kt in kts:
                blk = w[k0 * P:(k0 + kt) * P, c:c + P]
                res.append(blk.reshape(kt, P, P).transpose(1, 0, 2).reshape(P, kt * P))
                k0 += kt
        return np.ascontiguousarray(np.stack(res))

    def per_channel(v):
        v = v.reshape(-1, v.shape[-1])
        return v.reshape(v.shape[0], -1, P).transpose(2, 1, 0).reshape(P, -1)

    def rows(v):
        res = np.zeros((P, 1), np.float32)
        res[:v.size, 0] = v
        return res

    h = np.concatenate([a["meta_tokens"], a["x"][0]], 0)
    x_h = np.ascontiguousarray(h.reshape(T, KD, P).transpose(2, 1, 0))
    parts = {"mix0": per_channel(a["l0_mix_norm"]), "ffn0": per_channel(a["l0_ffn_norm"]),
             "mix1": per_channel(a["l1_mix_norm"]), "ffn1": per_channel(a["l1_ffn_norm"]),
             "final": per_channel(a["final_norm"]), "ssd_cw": per_channel(a["l0_ssd_conv_w"]),
             "ssd_cb": per_channel(a["l0_ssd_conv_b"]), "ssd_norm": per_channel(a["l0_ssd_norm"]),
             "ret_norm": per_channel(a["l0_ret_norm"]),
             "f0_cw": per_channel(a["l0_ffn_conv_w"]), "f0_cb": per_channel(a["l0_ffn_conv_b"]),
             "f1_cw": per_channel(a["l1_ffn_conv_w"]), "f1_cb": per_channel(a["l1_ffn_conv_b"]),
             "lru_cw": per_channel(a["l1_lru_conv_w"]), "lru_cb": per_channel(a["l1_lru_conv_b"]),
             "lru_ba": per_channel(a["l1_lru_ba"]), "lru_bx": per_channel(a["l1_lru_bx"]),
             "lru_lam": per_channel(a["l1_lru_lambda"]), "ssd_d": np.tile(a["l0_ssd_d"][None], (P, 1)),
             "ssd_dtb": rows(a["l0_ssd_dt_bias"]), "ssd_alog": rows(a["l0_ssd_a_log"])}
    vec_h = np.ascontiguousarray(np.concatenate([parts[n] for n in COLS], 1))

    f = np.float32
    half = P
    inv = (1.0 / (f(10000.0) ** (np.arange(half, dtype=f) / f(half - 1)))).astype(f)
    ang = (np.arange(T, dtype=f)[None, :] * inv[:, None]).astype(f)
    tri = (np.arange(P)[:, None] >= np.arange(P)[None, :]).astype(f)
    cst_h = np.concatenate([np.eye(P, dtype=f), np.ones((P, P), f), -tri, -np.ones((P, P), f), -1e30 * tri, np.cos(ang),
                            np.sin(ang)],
                           1).astype(f)
    log_gamma = np.log1p(-np.exp2(-5.0 - np.arange(RET_HEADS)))
    diff = np.arange(T)[None, :] - np.arange(P)[:, None]
    dec_h = np.where(diff[:, None, :] >= 0, np.exp(log_gamma[None, :, None] * np.maximum(diff, 0)[:, None, :]), 0.0)
    dec_h = (dec_h / 16.0).astype(f)

    w = a["l0_w_in"]
    z0, x0, b0, c0 = 0, 1024, 2048, 2560
    dt0, q0 = 3072, 3088
    ssd_cols = [c for g in range(SSD_GROUPS) for c in (x0 + 256 * g, x0 + 256 * g + P, b0 + P * g, c0 + P * g,
                                                       z0 + 256 * g, z0 + 256 * g + P)]
    ret_cols = [q0 + 1024 * n + 256 * r + P * d for r in range(RET_HEADS) for n in range(4) for d in range(2)]
    l1_cols = [1024 * n + P * i for i in range(8) for n in range(5)]
    fi_cols = [FFN * n + P * i for i in range(KF) for n in range(2)]
    oc = [P * m for m in range(KD)]

    def out_units(w, layer):
        rows = w.reshape(16, P, D_MODEL)
        return np.concatenate([units(rows[list(half)].reshape(-1, D_MODEL), oc, [KD])
                               for half in (EARLY[layer], LATE[layer])])

    gate = np.ascontiguousarray(np.concatenate([a["l1_lru_wa"], a["l1_lru_wx"]], 2))
    arrays = [x_h, vec_h, cst_h, dec_h, units(w, [dt0], [KD]), units(w, ssd_cols, [KD]), units(w, ret_cols, [KD]),
              out_units(a["l0_w_out"], 0), units(a["l0_ffn_w_in"], fi_cols, [KD]),
              units(a["l0_ffn_w_out"], oc, [KH, KH]), units(a["l1_w_in"], l1_cols, [KD]),
              out_units(a["l1_w_out"], 1), units(a["l1_ffn_w_in"], fi_cols, [KD]),
              units(a["l1_ffn_w_out"], oc, [KH, KH]), gate]
    nc = bacc.Bacc("TRN2", target_bir_lowering=False, num_devices=1)
    named = {f"in_{n}": v for n, v in enumerate(arrays)}
    aps = [nc.dram_tensor(k, v.shape, mybir.dt.from_np(v.dtype), kind="ExternalInput").ap() for k, v in named.items()]
    out = nc.dram_tensor("out", (P, KD, SEQ), mybir.dt.float32, kind="ExternalOutput").ap()
    build(nc, *aps, out)
    r = run(nc, [named], core_ids=[0])
    got = r.results[0]["out"]
    return np.ascontiguousarray(got.transpose(2, 1, 0).reshape(1, SEQ, D_MODEL))
```
